# Optimizing a Trainium2 kernel written in Bass

```python
import math
import jax, jax.numpy as jnp
from jax import lax
import numpy as np
import jax
import jax.numpy as jnp

D_MODEL = 1024
BATCH = 1
SEQ = 512
DEPTH = 1

ATTN_WIDTH = D_MODEL // 2
ATTN_HEAD_DIM = 64
ATTN_QK_DIM = ATTN_HEAD_DIM // 2
ATTN_HEADS = ATTN_WIDTH // ATTN_HEAD_DIM
POOL_WIDTH = D_MODEL // 4
POOL_WINDOWS = (2, 4, 8, 16)
POOL_GROUPS = len(POOL_WINDOWS)
POOL_GROUP_DIM = POOL_WIDTH // POOL_GROUPS
CONV_WIDTH = D_MODEL // 4
CONV_GROUPS = 4
CONV_K = 3
MIX_WIDTH = ATTN_WIDTH + POOL_WIDTH + CONV_WIDTH
IN_WIDTH = 3 * ATTN_WIDTH + POOL_WIDTH + 3 * CONV_WIDTH
D_FF = ((8 * D_MODEL // 3 + 255) // 256) * 256
Q_BLOCK = 128
EPS = 1e-6


def rmsnorm(x, g):
    xf = x.astype(jnp.float32)
    y = xf * lax.rsqrt(jnp.mean(xf * xf, axis=-1, keepdims=True) + EPS)
    return (y * g.astype(jnp.float32)).astype(x.dtype)

def alibi_slopes(n_heads):
    return jnp.asarray(np.array([2.0 ** (-8.0 * (h + 1) / n_heads) for h in range(n_heads)], dtype=np.float32))

def diff_attention(q, k, v, lam, slopes):
    b_, s_ = q.shape[0], q.shape[1]
    nblk = s_ // Q_BLOCK
    scale = ATTN_QK_DIM ** -0.5
    qb = q.reshape(b_, nblk, Q_BLOCK, ATTN_HEADS, 2, ATTN_QK_DIM).transpose(1, 0, 2, 3, 4, 5)
    kpos = jnp.arange(s_)

    def one_block(args):
        qi, blk = args
        qpos = blk * Q_BLOCK + jnp.arange(Q_BLOCK)
        dist = jnp.abs(qpos[:, None] - kpos[None, :]).astype(jnp.float32)
        bias = -slopes[:, None, None] * dist[None]
        s = jnp.einsum('bqhpd,bkhpd->bphqk', qi, k).astype(jnp.float32) * scale + bias
        p = jax.nn.softmax(s, axis=-1)
        w = p[:, 0] - lam * p[:, 1]
        return jnp.einsum('bhqk,bkhd->bqhd', w.astype(v.dtype), v)

    out = lax.map(one_block, (qb, jnp.arange(nblk)))
    return out.transpose(1, 0, 2, 3, 4).reshape(b_, s_, ATTN_HEADS, ATTN_HEAD_DIM)

def multiscale_pool(u, w_pool, pool_scale):
    b_, s_, _ = u.shape
    uf = u.astype(jnp.float32)
    csum = jnp.concatenate([jnp.zeros((b_, 1, POOL_WIDTH), jnp.float32), jnp.cumsum(uf, axis=1)], axis=1)
    t = jnp.arange(s_)
    pooled = []
    for g, w in enumerate(POOL_WINDOWS):
        cg = csum[..., g * POOL_GROUP_DIM:(g + 1) * POOL_GROUP_DIM]
        lo = jnp.clip(t - w // 2, 0, s_)
        hi = jnp.clip(t + w - w // 2, 0, s_)
        total = jnp.take(cg, hi, axis=1) - jnp.take(cg, lo, axis=1)
        cnt = (hi - lo).astype(jnp.float32)
        pooled.append(total / cnt[None, :, None])
    pooled = jnp.stack(pooled, axis=2)
    diff = pooled - uf.reshape(b_, s_, POOL_GROUPS, POOL_GROUP_DIM)
    mixed = jnp.einsum('bsgc,gcd->bsgd', diff, w_pool.astype(jnp.float32))
    return (mixed.reshape(b_, s_, POOL_WIDTH) * pool_scale.astype(jnp.float32)).astype(u.dtype)

def short_gated_conv(b_gate, c_gate, xh, conv_w):
    u = c_gate * xh
    up = jnp.pad(u, ((0, 0), (1, 1), (0, 0)))
    y = conv_w[0] * up[:, :-2] + conv_w[1] * up[:, 1:-1] + conv_w[2] * up[:, 2:]
    return b_gate * y

def modulate(h, shift, scale):
    return h * (1.0 + scale[:, None, :]) + shift[:, None, :]

def first_inputs(seed: int = 0) -> dict:
    key = jax.random.key(seed)
    ks = jax.random.split(key, 20)
    f32 = jnp.float32
    n = lambda k, shape, s: jax.random.normal(k, shape, f32) * s
    return {
        "x": n(ks[0], (BATCH, SEQ, D_MODEL), 1.0),
        "c": n(ks[1], (BATCH, D_MODEL), 1.0),
        "w_ada": n(ks[2], (DEPTH, D_MODEL, 6 * D_MODEL), D_MODEL ** -0.5),
        "b_ada": n(ks[3], (DEPTH, 6 * D_MODEL), 0.02),
        "g_mix": 1.0 + n(ks[4], (DEPTH, D_MODEL), 0.1),
        "w_in": n(ks[5], (DEPTH, D_MODEL, IN_WIDTH), D_MODEL ** -0.5),
        "lambda_q1": n(ks[6], (DEPTH, ATTN_QK_DIM), 0.1),
        "lambda_k1": n(ks[7], (DEPTH, ATTN_QK_DIM), 0.1),
        "lambda_q2": n(ks[8], (DEPTH, ATTN_QK_DIM), 0.1),
        "lambda_k2": n(ks[9], (DEPTH, ATTN_QK_DIM), 0.1),
        "g_subln": 1.0 + n(ks[10], (DEPTH, ATTN_WIDTH), 0.1),
        "w_pool": n(ks[11], (DEPTH, POOL_GROUPS, POOL_GROUP_DIM, POOL_GROUP_DIM), POOL_GROUP_DIM ** -0.5),
        "pool_scale": 1.0 + n(ks[12], (DEPTH, POOL_WIDTH), 0.1),
        "conv_w": n(ks[13], (DEPTH, CONV_K, CONV_WIDTH), 0.5),
        "w_out": n(ks[14], (DEPTH, MIX_WIDTH, D_MODEL), MIX_WIDTH ** -0.5),
        "g_ffn": 1.0 + n(ks[15], (DEPTH, D_MODEL), 0.1),
        "w_gate_up": n(ks[16], (DEPTH, D_MODEL, 2 * D_FF), D_MODEL ** -0.5),
        "w_down": n(ks[17], (DEPTH, D_FF, D_MODEL), D_FF ** -0.5),
        "g_final": 1.0 + n(ks[18], (D_MODEL,), 0.1),
    }

def first_block(x, c, w_ada, b_ada, g_mix, w_in, lambda_q1, lambda_k1, lambda_q2, lambda_k2,
              g_subln, w_pool, pool_scale, conv_w, w_out, g_ffn, w_gate_up, w_down, g_final):
    b_, s_, _ = x.shape
    slopes = alibi_slopes(ATTN_HEADS)
    c_act = jax.nn.silu(c)
    o_q, o_k, o_v = ATTN_WIDTH, 2 * ATTN_WIDTH, 3 * ATTN_WIDTH
    o_p = o_v + POOL_WIDTH
    o_b, o_c = o_p + CONV_WIDTH, o_p + 2 * CONV_WIDTH
    for l in range(DEPTH):
        mod = c_act @ w_ada[l] + b_ada[l]
        sh1, sc1, gt1, sh2, sc2, gt2 = jnp.split(mod, 6, axis=-1)

        h = modulate(rmsnorm(x, g_mix[l]), sh1, sc1)
        proj = h @ w_in[l]
        q = proj[..., :o_q].reshape(b_, s_, ATTN_HEADS, 2, ATTN_QK_DIM)
        k = proj[..., o_q:o_k].reshape(b_, s_, ATTN_HEADS, 2, ATTN_QK_DIM)
        v = proj[..., o_k:o_v].reshape(b_, s_, ATTN_HEADS, ATTN_HEAD_DIM)
        u_pool = proj[..., o_v:o_p]
        b_gate, c_gate, x_conv = proj[..., o_p:o_b], proj[..., o_b:o_c], proj[..., o_c:]

        lambda_init = 0.8 - 0.6 * math.exp(-0.3 * l)
        lam = (jnp.exp(jnp.sum(lambda_q1[l].astype(jnp.float32) * lambda_k1[l].astype(jnp.float32)))
               - jnp.exp(jnp.sum(lambda_q2[l].astype(jnp.float32) * lambda_k2[l].astype(jnp.float32)))
               + lambda_init)
        attn = diff_attention(q, k, v, lam, slopes)
        attn = rmsnorm(attn, g_subln[l].reshape(ATTN_HEADS, ATTN_HEAD_DIM)) * (1.0 - lambda_init)
        y_a = attn.reshape(b_, s_, ATTN_WIDTH)
        y_b = multiscale_pool(u_pool, w_pool[l], pool_scale[l])
        y_c = short_gated_conv(b_gate, c_gate, x_conv, conv_w[l])

        mixed = jnp.concatenate([y_a, y_b, y_c], axis=-1) @ w_out[l]
        x = x + gt1[:, None, :] * mixed

        h = modulate(rmsnorm(x, g_ffn[l]), sh2, sc2)
        gate, up = jnp.split(h @ w_gate_up[l], 2, axis=-1)
        x = x + gt2[:, None, :] * ((jax.nn.silu(gate) * up) @ w_down[l])

    return rmsnorm(x, g_final)


N_MEM = 256
BLOCK = 128
FOX_HEADS = 8
FOX_HD = 64
SWA_HEADS = 8
SWA_KV_HEADS = 2
SWA_HD = 64
WINDOW = 128
MEM_HEADS = 4
MEM_HD = 128
N_BRANCH = 3
PEER_HEADS = 8
N_KEYS = 128
N_EXPERTS = N_KEYS * N_KEYS
PEER_QD = 256
PEER_TOPK = 16
PEER_CHUNK = 128
NEG_INF = -1e30

FOX_W = FOX_HEADS * FOX_HD
SWA_W = SWA_HEADS * SWA_HD
SWA_KV_W = SWA_KV_HEADS * SWA_HD
MEM_W = MEM_HEADS * MEM_HD
IN_WIDTHS = (FOX_W, FOX_W, FOX_W, FOX_HEADS, SWA_W, SWA_KV_W, SWA_KV_W, MEM_W, N_BRANCH * D_MODEL)
IN_COLS = 3 * FOX_W + FOX_HEADS + SWA_W + 2 * SWA_KV_W + MEM_W + N_BRANCH * D_MODEL


def rmsnorm_2(x, g):
    xf = x.astype(jnp.float32)
    y = xf * lax.rsqrt(jnp.mean(xf * xf, axis=-1, keepdims=True) + EPS)
    return (y * g.astype(jnp.float32)).astype(x.dtype)

def head_rmsnorm(x, g):
    xf = x.astype(jnp.float32)
    return xf * lax.rsqrt(jnp.mean(xf * xf, axis=-1, keepdims=True) + EPS) * g.astype(jnp.float32)

def alibi_slopes_2(n):
    return 2.0 ** (-8.0 * (jnp.arange(n, dtype=jnp.float32) + 1.0) / n)

def fox_attention(q, k, v, log_f):
    B, S, H, d = q.shape
    nb = S // BLOCK
    c = jnp.cumsum(log_f, axis=1).transpose(0, 2, 1)
    q_blocks = q.reshape(B, nb, BLOCK, H, d).transpose(1, 0, 2, 3, 4)
    c_blocks = c.reshape(B, H, nb, BLOCK).transpose(2, 0, 1, 3)
    vf = v.astype(jnp.float32)
    kpos = jnp.arange(S)
    scale = d ** -0.5

    def one_block(args):
        i, q_i, c_i = args
        s = jnp.einsum('bqhd,bkhd->bhqk', q_i, k) * scale
        s = s + (c_i[..., :, None] - c[..., None, :])
        qpos = i * BLOCK + jnp.arange(BLOCK)
        s = jnp.where(kpos[None, :] <= qpos[:, None], s, NEG_INF)
        p = jax.nn.softmax(s, axis=-1)
        return jnp.einsum('bhqk,bkhd->bqhd', p, vf)

    o = lax.map(one_block, (jnp.arange(nb), q_blocks, c_blocks))
    return o.transpose(1, 0, 2, 3, 4).reshape(B, S, H, d)

def swa_attention(q, k, v, sinks, slopes):
    B, S, Hq, d = q.shape
    G = k.shape[2]
    R = Hq // G
    nb = S // BLOCK
    qb = q.reshape(B, nb, BLOCK, G, R, d)

    def band(t):
        t = t.astype(jnp.float32)
        tp = jnp.concatenate([jnp.zeros((B, BLOCK, G, d), jnp.float32), t], axis=1)
        tp = tp.reshape(B, nb + 1, BLOCK, G, d)
        return jnp.concatenate([tp[:, :-1], tp[:, 1:]], axis=2)

    kb = band(k)
    vb = band(v)
    s = jnp.einsum('bnqgrd,bnkgd->bngrqk', qb, kb) * d ** -0.5
    qi = jnp.arange(BLOCK)[:, None]
    kj = jnp.arange(2 * BLOCK)[None, :]
    dist_i = qi + BLOCK - kj
    in_window = (dist_i >= 0) & (dist_i < WINDOW)
    blk_ok = (jnp.arange(nb)[:, None] > 0) | (jnp.arange(2 * BLOCK)[None, :] >= BLOCK)
    mask = in_window[None] & blk_ok[:, None, :]
    s = s - slopes.astype(jnp.float32).reshape(G, R)[:, :, None, None] * dist_i.astype(jnp.float32)
    s = jnp.where(mask[None, :, None, None], s, NEG_INF)
    sink = jnp.broadcast_to(sinks.astype(jnp.float32).reshape(1, 1, G, R, 1, 1), s.shape[:-1] + (1,))
    p = jax.nn.softmax(jnp.concatenate([s, sink], axis=-1), axis=-1)[..., :-1]
    o = jnp.einsum('bngrqk,bnkgd->bnqgrd', p, vb)
    return o.reshape(B, S, Hq, d)

def memory_attention(q, k, v):
    d = q.shape[-1]
    s = jnp.einsum('bshd,bmhd->bhsm', q, k) * d ** -0.5
    p = jax.nn.softmax(s, axis=-1)
    return jnp.einsum('bhsm,bmhd->bshd', p, v.astype(jnp.float32))

def peer_ffn(h, w_q, keys1, keys2, u, v):
    B, S, D = h.shape
    half = PEER_QD // 2
    q = (h @ w_q).astype(jnp.float32).reshape(B, S, PEER_HEADS, 2, half)
    s1 = jnp.einsum('bshd,hkd->bshk', q[..., 0, :], keys1.astype(jnp.float32))
    s2 = jnp.einsum('bshd,hkd->bshk', q[..., 1, :], keys2.astype(jnp.float32))
    v1, i1 = lax.top_k(s1, PEER_TOPK)
    v2, i2 = lax.top_k(s2, PEER_TOPK)
    cand = (v1[..., :, None] + v2[..., None, :]).reshape(B, S, PEER_HEADS, PEER_TOPK * PEER_TOPK)
    sv, si = lax.top_k(cand, PEER_TOPK)
    e1 = jnp.take_along_axis(i1, si // PEER_TOPK, axis=-1)
    e2 = jnp.take_along_axis(i2, si % PEER_TOPK, axis=-1)
    experts = e1 * N_KEYS + e2
    gates = jax.nn.softmax(sv, axis=-1)
    n_act = PEER_HEADS * PEER_TOPK
    n_chunks = (B * S) // PEER_CHUNK
    hc = h.reshape(n_chunks, PEER_CHUNK, D)
    ec = experts.reshape(n_chunks, PEER_CHUNK, n_act)
    gc = gates.reshape(n_chunks, PEER_CHUNK, n_act)

    def chunk(args):
        h_c, e_c, g_c = args
        a = jnp.einsum('cd,ced->ce', h_c.astype(jnp.float32), u[e_c].astype(jnp.float32))
        act = jax.nn.gelu(a, approximate=False) * g_c
        return jnp.einsum('ce,ced->cd', act, v[e_c].astype(jnp.float32))

    out = lax.map(chunk, (hc, ec, gc))
    return out.reshape(B, S, D).astype(h.dtype)

def second_inputs(seed: int = 0) -> dict:
    key = jax.random.key(seed)
    ks = jax.random.split(key, 25)
    L = DEPTH
    D = D_MODEL

    def nrm(k, shape, scale):
        return scale * jax.random.normal(k, shape, jnp.float32)

    return {
        'x': nrm(ks[0], (BATCH, SEQ, D), 1.0),
        'mem': nrm(ks[1], (BATCH, N_MEM, D), 1.0),
        'norm1_g': 1.0 + nrm(ks[2], (L, D), 0.02),
        'w_in': nrm(ks[3], (L, D, IN_COLS), D ** -0.5),
        'b_gate': nrm(ks[4], (L, N_BRANCH * D), 0.02),
        'b_forget': 2.0 + nrm(ks[5], (L, FOX_HEADS), 0.5),
        'fox_q_g': 1.0 + nrm(ks[6], (L, FOX_HD), 0.02),
        'fox_k_g': 1.0 + nrm(ks[7], (L, FOX_HD), 0.02),
        'swa_q_g': 1.0 + nrm(ks[8], (L, SWA_HD), 0.02),
        'swa_k_g': 1.0 + nrm(ks[9], (L, SWA_HD), 0.02),
        'swa_sinks': nrm(ks[10], (L, SWA_HEADS), 0.5),
        'mem_norm_g': 1.0 + nrm(ks[11], (L, D), 0.02),
        'w_mem_kv': nrm(ks[12], (L, D, 2 * MEM_W), D ** -0.5),
        'mem_q_g': 1.0 + nrm(ks[13], (L, MEM_HD), 0.02),
        'mem_k_g': 1.0 + nrm(ks[14], (L, MEM_HD), 0.02),
        'w_fox_o': nrm(ks[15], (L, FOX_W, D), FOX_W ** -0.5),
        'w_swa_o': nrm(ks[16], (L, SWA_W, D), SWA_W ** -0.5),
        'w_mem_o': nrm(ks[17], (L, MEM_W, D), MEM_W ** -0.5),
        'w_out': nrm(ks[18], (L, D, D), D ** -0.5),
        'norm2_g': 1.0 + nrm(ks[19], (L, D), 0.02),
        'w_peer_q': nrm(ks[20], (L, D, PEER_HEADS * PEER_QD), D ** -0.5),
        'peer_keys1': nrm(ks[21], (L, PEER_HEADS, N_KEYS, PEER_QD // 2), (PEER_QD // 2) ** -0.5),
        'peer_keys2': nrm(ks[22], (L, PEER_HEADS, N_KEYS, PEER_QD // 2), (PEER_QD // 2) ** -0.5),
        'peer_u': nrm(ks[23], (L, N_EXPERTS, D), D ** -0.5),
        'peer_v': nrm(ks[24], (L, N_EXPERTS, D), (PEER_HEADS * PEER_TOPK) ** -0.5),
    }

def second_block(x, mem, norm1_g, w_in, b_gate, b_forget, fox_q_g, fox_k_g, swa_q_g, swa_k_g,
              swa_sinks, mem_norm_g, w_mem_kv, mem_q_g, mem_k_g, w_fox_o, w_swa_o, w_mem_o,
              w_out, norm2_g, w_peer_q, peer_keys1, peer_keys2, peer_u, peer_v):
    B, S, D = x.shape
    M = mem.shape[1]
    splits = [int(c) for c in np.cumsum(IN_WIDTHS)[:-1]]
    slopes = alibi_slopes_2(SWA_HEADS)
    for l in range(DEPTH):
        h = rmsnorm_2(x, norm1_g[l])
        z = h @ w_in[l]
        fq, fk, fv, ff, sq, sk, sv, mq, gl = jnp.split(z, splits, axis=-1)

        fq = head_rmsnorm(fq.reshape(B, S, FOX_HEADS, FOX_HD), fox_q_g[l])
        fk = head_rmsnorm(fk.reshape(B, S, FOX_HEADS, FOX_HD), fox_k_g[l])
        log_f = jax.nn.log_sigmoid((ff + b_forget[l]).astype(jnp.float32))
        o_fox = fox_attention(fq, fk, fv.reshape(B, S, FOX_HEADS, FOX_HD), log_f)
        o_fox = o_fox.reshape(B, S, FOX_W).astype(x.dtype)

        sq = head_rmsnorm(sq.reshape(B, S, SWA_HEADS, SWA_HD), swa_q_g[l])
        sk = head_rmsnorm(sk.reshape(B, S, SWA_KV_HEADS, SWA_HD), swa_k_g[l])
        o_swa = swa_attention(sq, sk, sv.reshape(B, S, SWA_KV_HEADS, SWA_HD), swa_sinks[l], slopes)
        o_swa = o_swa.reshape(B, S, SWA_W).astype(x.dtype)

        mn = rmsnorm_2(mem, mem_norm_g[l])
        mk, mv = jnp.split(mn @ w_mem_kv[l], 2, axis=-1)
        mk = head_rmsnorm(mk.reshape(B, M, MEM_HEADS, MEM_HD), mem_k_g[l])
        mq = head_rmsnorm(mq.reshape(B, S, MEM_HEADS, MEM_HD), mem_q_g[l])
        o_mem = memory_attention(mq, mk, mv.reshape(B, M, MEM_HEADS, MEM_HD))
        o_mem = o_mem.reshape(B, S, MEM_W).astype(x.dtype)

        gates = jax.nn.sigmoid((gl + b_gate[l]).astype(jnp.float32)).astype(x.dtype)
        gates = gates.reshape(B, S, N_BRANCH, D)
        merged = (gates[:, :, 0] * (o_fox @ w_fox_o[l])
                  + gates[:, :, 1] * (o_swa @ w_swa_o[l])
                  + gates[:, :, 2] * (o_mem @ w_mem_o[l]))
        x = x + merged @ w_out[l]

        x = x + peer_ffn(rmsnorm_2(x, norm2_g[l]), w_peer_q[l], peer_keys1[l], peer_keys2[l],
                         peer_u[l], peer_v[l])
    return x


def setup_inputs(seed=0):
    out = dict(first_inputs(seed))
    for name, value in second_inputs(seed + 1).items():
        if name != "x":
            out[name + "_2"] = value
    return out


def reference(
    x, c, w_ada, b_ada, g_mix, w_in, lambda_q1, lambda_k1, lambda_q2, lambda_k2, g_subln,
    w_pool, pool_scale, conv_w, w_out, g_ffn, w_gate_up, w_down, g_final, mem_2, norm1_g_2,
    w_in_2, b_gate_2, b_forget_2, fox_q_g_2, fox_k_g_2, swa_q_g_2, swa_k_g_2, swa_sinks_2,
    mem_norm_g_2, w_mem_kv_2, mem_q_g_2, mem_k_g_2, w_fox_o_2, w_swa_o_2, w_mem_o_2, w_out_2,
    norm2_g_2, w_peer_q_2, peer_keys1_2, peer_keys2_2, peer_u_2, peer_v_2,
):
    x = first_block(
        x, c, w_ada, b_ada, g_mix, w_in, lambda_q1, lambda_k1, lambda_q2, lambda_k2, g_subln,
        w_pool, pool_scale, conv_w, w_out, g_ffn, w_gate_up, w_down, g_final,
    )
    return second_block(
        x, mem_2, norm1_g_2, w_in_2, b_gate_2, b_forget_2, fox_q_g_2, fox_k_g_2, swa_q_g_2,
        swa_k_g_2, swa_sinks_2, mem_norm_g_2, w_mem_kv_2, mem_q_g_2, mem_k_g_2, w_fox_o_2,
        w_swa_o_2, w_mem_o_2, w_out_2, norm2_g_2, w_peer_q_2, peer_keys1_2, peer_keys2_2,
        peer_u_2, peer_v_2,
    )


_drawn_inputs = setup_inputs


def setup_inputs(seed=0):
    import zlib

    import numpy as np

    out = dict(_drawn_inputs(seed))
    spreads = {}
    factors = {'lambda_q1': 8.0,
     'lambda_k1': 8.0,
     'lambda_q2': 5.238,
     'lambda_k2': 8.0,
     'norm1_g_2': 5.862,
     'b_gate_2': 8.0,
     'fox_q_g_2': 8.0,
     'fox_k_g_2': 8.0,
     'swa_q_g_2': 8.0,
     'swa_k_g_2': 8.0,
     'swa_sinks_2': 37.2,
     'mem_norm_g_2': 8.0,
     'mem_q_g_2': 8.0,
     'mem_k_g_2': 8.0,
     'norm2_g_2': 40.035}
    for name, (base, spread) in spreads.items():
        noise = np.random.default_rng([zlib.crc32(name.encode()), seed]).standard_normal(out[name].shape)
        drawn = base * np.exp(spread * noise) if base else spread * noise
        out[name] = jnp.asarray(drawn.astype(out[name].dtype))
    for name, factor in factors.items():
        out[name] = (out[name] * factor).astype(out[name].dtype)
    return out
```

```python
from contextlib import ExitStack

import concourse.bass as bass
from concourse import mybir

P = 128
T = 512
QT = T // P
D = 1024
KD = D // P
DFF = 2816
FT = DFF // P
FFN_GROUPS = (8, 8, 6)
HEADS = 8
HD = 64
MEM = 256
MEM_HEADS = 4
KEYS = 128
TOPK = 16
EPS = 1e-6
NEG_INF = -1e30
LAMBDA_INIT = 0.2

SLAB = 2048
N_ADA = 6 * D // 256
N_MID = 99
N_DENSE = KEYS + 1

F32 = mybir.dt.float32
F32R = mybir.dt.float32r
U32 = mybir.dt.uint32
I32 = mybir.dt.int32
ALU = mybir.AluOpType
ACT = mybir.ActivationFunctionType
AX = mybir.AxisListType.X

COLS = [("c", 8), ("b_ada", 48), ("g_mix", 8), ("g_subln", 4), ("pool_scale", 2), ("conv", 6), ("g_ffn", 8),
        ("g_final", 8), ("g_norm1", 8), ("b_gate", 24), ("g_fox_q", 1), ("g_fox_k", 1), ("g_swa_q", 1),
        ("g_swa_k", 1), ("g_mem", 8), ("g_mem_q", 1), ("g_mem_k", 1), ("g_norm2", 8), ("b_forget", 8),
        ("sinks", 8), ("lambda", 128), ("w_forget", 64), ("w_pool", 128)]
COL_AT = {}
N_COLS = 0
for _name, _width in COLS:
    COL_AT[_name] = (N_COLS, N_COLS + _width)
    N_COLS += _width

TABLES = [("ident", 128), ("mean_all", 128), ("mean_64", 128), ("mean_128", 128), ("distance", 896),
          ("pool_recip", 1024), ("causal", 128), ("upto", 512), ("swa_distance", 256), ("swa_mask", 256), ("iota", 128),
          ("iota16", 16)]
TABLE_AT = {}
N_TABLE = 0
for _name, _width in TABLES:
    TABLE_AT[_name] = (N_TABLE, N_TABLE + _width)
    N_TABLE += _width

LEVEL, DENSE = 3, True
ARENA = 19170


class Taken:

    def __init__(self, eng):
        self.eng = eng
        self.count = {}

    def take(self, sem, k=1):
        self.count[sem.name] = self.count.get(sem.name, 0) + k
        self.eng.wait_ge(sem, self.count[sem.name])


def build(nc, x_in, stream, cols_in, tables_in, mem_in, keys_in, out):
    g_dram = nc.dram_tensor("gates_dram", [QT, P, KEYS, P], F32, kind="Internal").ap()

    with ExitStack() as ctx:
        def sb(name, shape, dt=F32):
            return ctx.enter_context(nc.sbuf_tensor(name, shape, dt))

        def sem(name):
            return ctx.enter_context(nc.semaphore(name))

        X = sb("X", [P, KD, T])
        A_hi = sb("A_hi", [P, KD, T], F32R)
        A_lo = sb("A_lo", [P, KD, T], F32R)
        B_hi = sb("B_hi", [P, KD, T], F32R)
        B_lo = sb("B_lo", [P, KD, T], F32R)
        raw = sb("raw", [P, 2, SLAB])
        W_hi = sb("W_hi", [P, 2, SLAB], F32R)
        W_lo = sb("W_lo", [P, 2, SLAB], F32R)
        tab = sb("tab", [P, 512])
        col = sb("col", [P, N_COLS])
        wf_hi = sb("wf_hi", [P, KD, HEADS], F32R)
        wf_lo = sb("wf_lo", [P, KD, HEADS], F32R)
        mod = sb("mod", [P, 48])
        gs = sb("gs", [P, 2, KD])
        cact = sb("cact", [P, KD])
        small = sb("small", [P, 48])
        zero = sb("zero", [P, 1])
        arena = sb("arena", [P, ARENA])
        bank = [ctx.enter_context(nc.psum_tensor(f"bank{i}", [P, 512], F32)) for i in range(8)]

        def at(start, *shape):
            size = 1
            for n in shape:
                size *= n
            v = arena[:, start:start + size]
            if len(shape) == 2:
                v = v.rearrange("p (a b) -> p a b", b=shape[1])
            if len(shape) == 3:
                v = v.rearrange("p (a b c) -> p a b c", b=shape[1], c=shape[2])
            return v

        ident, mean_all, mean_64, mean_128 = (tab[:, i * P:(i + 1) * P] for i in range(4))

        def c_(name, i=0, n=1):
            a = COL_AT[name][0] + i
            return col[:, a:a + n]

        S = [at(512 * i, 512) for i in range(8)]
        Qt, Kt = at(4096, 4, T), at(6144, 4, T)
        V = at(8192, QT, 512)
        Ot = at(10240, 4, T)
        pool_in = at(12288, 2, 528)
        conv_in = at(13344, 2, 514)
        b_gate_t, c_gate_t = at(14372, 2, T), at(15396, 2, T)
        dist = at(16420, 896)
        pool_sum = at(17316, 2, 528)
        merged = at(12288, KD, T)
        upto = at(16384, 512)
        ck = at(16896, 2, 512)
        causal = at(17920, P)
        log_f, cq = at(18048, QT, HEADS), at(18080, QT, HEADS)
        swa_nd, swa_mask, swa_bias = at(16384, 256), at(16640, 256), at(16896, 2, 256)
        mem_t = at(8192, KD, MEM)
        mem_kt, mem_v = at(6144, MEM_HEADS, MEM), at(10240, 2, 512)
        mem_o = at(8192, MEM_HEADS, T)
        recip_cnt = [at(4096 * 0 + 512 * 6, 512), at(512 * 7, 512)]
        keys = at(0, 16, KEYS)
        peer_q = at(2048, 2, 2, T)
        top_v = at(4096, QT, HEADS, 2 * TOPK)
        top_i = at(5120, QT, HEADS, 2 * TOPK)
        sum_v = at(6144, QT, HEADS, TOPK)
        sum_i = at(6656, QT, HEADS, TOPK)
        rest_a = at(7168, 2, KEYS)
        cand = at(7424, 2, 256)
        cand_rest = at(7936, 256)
        iota16 = at(8192, TOPK)
        sel_hi, sel_lo = at(8208, P), at(8336, P)
        top_f = at(8464, HEADS, 2 * TOPK)
        eq = at(8720, 2048)
        picks = at(10768, QT, 3, P)
        iw = at(12304, 2, P)
        picks_t = at(16384, 3, T)
        iota = at(17920, KEYS)
        hot = at(18048, 4, 2, KEYS)
        g_stage = at(0, KEYS, P)
        act_t, act_g, g_in = at(0, 2, T), at(1024, 2, T), at(2048, 2, T)
        acc = at(3072, 2, T)

        slab_loaded = [sem("slab_loaded0"), sem("slab_loaded1")]
        ada_used = sem("ada_used")
        zero_ready = sem("zero_ready")
        slab_half = sem("slab_half")
        slab_split = sem("slab_split")
        slab_used = sem("slab_used")
        const_loaded, table_loaded = sem("const_loaded"), sem("table_loaded")
        lin_ready = [sem(f"lin_ready{i}") for i in range(4)]
        lin_free = [sem(f"lin_free{i}") for i in range(4)]
        work_ready = [sem(f"work_ready{i}") for i in range(2)]
        work_free = [sem(f"work_free{i}") for i in range(2)]
        turn_ready = [sem(f"turn_ready{i}") for i in range(2)]
        turn_free = [sem(f"turn_free{i}") for i in range(2)]
        act_stage, dve_stage = sem("act_stage"), sem("dve_stage")
        act_step, dve_step = sem("act_step"), sem("dve_step")
        cact_ready, mod_ready = sem("cact_ready"), sem("mod_ready")
        square_ready, square_used = sem("square_ready"), sem("square_used")
        normed = sem("normed")
        whole_ready = sem("whole_ready")
        hi_ready = sem("hi_ready")
        top_ready = sem("top_ready")
        exp_ready = sem("exp_ready")
        p_ready = sem("p_ready")
        values_used = sem("values_used")
        small_ready, small_done = sem("small_ready"), sem("small_done")
        hot_ready, hot_used = sem("hot_ready"), sem("hot_used")
        g_copied, g_stored = sem("g_copied"), sem("g_stored")
        g_loaded = [sem("g_loaded0"), sem("g_loaded1")]
        a_ready, gelu_ready, act_ready = sem("a_ready"), sem("gelu_ready"), sem("act_ready")
        act_hi_ready, act_lo_ready = sem("act_hi_ready"), sem("act_lo_ready")
        part_ready, part_added = sem("part_ready"), sem("part_added")
        x_done, stored = sem("x_done"), sem("stored")

        block = ctx.enter_context(nc.Block())
        NORMS = {
            "first": (X, T, lambda k: gs[:, 0, k:k + 1], lambda k: mod[:, k:k + 1], "A"),
            "ffn": (X, T, lambda k: gs[:, 1, k:k + 1], lambda k: mod[:, 24 + k:25 + k], "A"),
            "final": (X, T, lambda k: c_("g_final", k), None, None),
            "second": (X, T, lambda k: c_("g_norm1", k), None, "A"),
            "mem": (mem_t, MEM, lambda k: c_("g_mem", k), None, "B"),
            "peer": (X, T, lambda k: c_("g_norm2", k), None, "A"),
        }
        HEAD_NORMS = {
            "subln": ([Ot[:, i, :] for i in range(4)], T, mean_64, lambda i: small[:, 8 + i:9 + i]),
            "fox_q": ([Qt[:, i, :] for i in range(4)], T, mean_64, lambda i: small[:, 16:17]),
            "fox_k": ([Kt[:, i, :] for i in range(4)], T, mean_64, lambda i: c_("g_fox_k")),
            "swa_q": ([Qt[:, i, :] for i in range(4)], T, mean_64, lambda i: small[:, 17:18]),
            "swa_k": ([Kt[:, 0, :]], T, mean_64, lambda i: c_("g_swa_k")),
            "mem_q": ([Qt[:, i, :] for i in range(4)], T, mean_128, lambda i: small[:, 18:19]),
            "mem_k": ([mem_kt[:, i, :] for i in range(4)], MEM, mean_128, lambda i: c_("g_mem_k")),
        }

        def att(kind):
            if kind == "diff":
                return dict(heads=HEADS, parts=2, k0=lambda q: 0, k1=lambda q: QT,
                            q=lambda h, p: (Qt[64 * (h % 2) + 32 * p:64 * (h % 2) + 32 * p + 32, h // 2, :]),
                            k=lambda h, p: (Kt[64 * (h % 2) + 32 * p:64 * (h % 2) + 32 * p + 32, h // 2, :]),
                            v=lambda h, j: V[:, j, HD * h:HD * h + HD], m=HD,
                            o=lambda h: (64 * (h % 2), h // 2, Ot))
            if kind == "fox":
                return dict(heads=HEADS, parts=1, k0=lambda q: 0, k1=lambda q: q + 1,
                            q=lambda h, p: Qt[64 * (h % 2):64 * (h % 2) + 64, h // 2, :],
                            k=lambda h, p: Kt[64 * (h % 2):64 * (h % 2) + 64, h // 2, :],
                            v=lambda h, j: V[:, j, HD * h:HD * h + HD], m=HD,
                            o=lambda h: (64 * (h % 2), h // 2, Ot))
            if kind == "swa":
                return dict(heads=HEADS, parts=1, k0=lambda q: max(q - 1, 0), k1=lambda q: q + 1,
                            q=lambda h, p: Qt[64 * (h // 4):64 * (h // 4) + 64, h % 4, :],
                            k=lambda h, p: Kt[64 * (h // 4):64 * (h // 4) + 64, 0, :],
                            v=lambda h, j: V[:, j, HD * (h // 4):HD * (h // 4) + HD], m=HD,
                            o=lambda h: (64 * (h // 4), h % 4, Ot))
            return dict(heads=MEM_HEADS, parts=1, k0=lambda q: 0, k1=lambda q: MEM // P,
                        q=lambda h, p: Qt[:, h, :], k=lambda h, p: mem_kt[:, h, :],
                        v=lambda h, j: mem_v[:, j, P * h:P * h + P], m=P, o=lambda h: (0, h, mem_o))

        def units(a):
            return [(h, q) for h in range(a["heads"]) for q in range(QT)]

        BRANCHES = ("fox", "swa", "mem")

        P_SLOTS = {"diff": [S[2], S[3], at(14372, 512), at(14884, 512)]}
        for _kind in BRANCHES:
            P_SLOTS[_kind] = [S[2], S[3]]
        recip_cnt_both = at(512 * 6, 1024)

        tile_signal = []

        @block.sync
        def _(sp):
            base = N_ADA + N_MID

            for s in range(2):
                sp.dma_start(raw[:, s, :], stream[s, :, :]).then_inc(slab_loaded[s], 16)
            sp.dma_start(X[:, :, :], x_in.rearrange("(k p) t -> p k t", p=P)).then_inc(const_loaded, 16)
            with sp.Fori(2, N_ADA + 1, 2) as s:
                for j in range(2):
                    sp.wait_ge(ada_used, s + (j - 1))
                    sp.dma_start(raw[:, j, :], stream[s + j, :, :]).then_inc(slab_loaded[j], 16)
            tail = (base - N_ADA) % 2
            with sp.Fori(N_ADA + 2, base - tail - 1, 2) as s:
                for j in range(2):
                    sp.wait_ge(slab_split, s + (j - 1 - N_ADA))
                    sp.dma_start(raw[:, j, :], stream[s + j, :, :]).then_inc(slab_loaded[j], 16)
            for s in range(base - tail, base):
                sp.wait_ge(slab_split, s - 1 - N_ADA)
                sp.dma_start(raw[:, s % 2, :], stream[s, :, :]).then_inc(slab_loaded[s % 2], 16)

            def expert_slab(e, j):
                slot = (base + j) % 2
                sp.wait_ge(slab_split, e + (j + N_MID - 1))
                sp.dma_start(raw[:, slot, :], stream[e + (base + j), :, :]).then_inc(slab_loaded[slot], 16)
                if isinstance(e, int):
                    sp.wait_ge(g_stored, 16 * QT)
                else:
                    sp.wait_ge(act_ready, e + (j - 1))
                sp.dma_start(g_in[:, j, :].rearrange("p (q t) -> p q t", q=QT),
                             g_dram[:, :, e + j, :].rearrange("q p t -> p q t")).then_inc(g_loaded[j], 16)

            if DENSE:
                for j in range(2):
                    expert_slab(0, j)
                with sp.Fori(2, KEYS - 1, 2) as e:
                    for j in range(2):
                        expert_slab(e, j)
                sp.wait_ge(slab_split, N_MID + N_DENSE - 2)
                sp.dma_start(raw[:, base % 2, :], stream[base + KEYS, :, :]).then_inc(slab_loaded[base % 2], 16)
            sp.wait_ge(x_done, 1)
            sp.dma_start(out.rearrange("(k p) t -> p k t", p=P), X[:, :, :]).then_inc(stored, 16)
            sp.wait_ge(stored, 16)

        @block.gpsimd
        def _(pool):
            def split(s, j):
                pool.wait_ge(slab_loaded[j], s * 8 + 8 * (N_ADA + 2))
                if not isinstance(s, int) or s >= 2:
                    pool.wait_ge(slab_used, s + (j - 1))
                pool.tensor_tensor(W_hi[:, j, :], raw[:, j, :], zero[:, :].to_broadcast([P, SLAB]), ALU.add).then_inc(slab_half, 1)
                pool.wait_ge(slab_half, s + (j + 1))
                pool.tensor_tensor(W_lo[:, j, :], raw[:, j, :], W_hi[:, j, :].bitcast(F32),
                                   ALU.subtract).then_inc(slab_split, 1)

            pool.memset(zero[:, :], 0.0).then_inc(zero_ready, 1)
            pool.wait_ge(zero_ready, 1)
            n = N_MID + (N_DENSE if DENSE else 0)
            for j in range(2):
                split(0, j)
            with pool.Fori(2, n - n % 2 - 1, 2) as s:
                for j in range(2):
                    split(s, j)
            if n % 2:
                split(n - 1, 0)

        @block.tensor
        def _(pe):
            take = Taken(pe).take
            at_ = {"slab": 0, "lin": 0, "work": 0, "turn": 0, "values": 0}
            ready_in = [0, 0, 0, 0]
            mm = pe.matmul

            def stage():
                take(act_stage)
                take(dve_stage)

            def lin():
                n = at_["lin"]
                at_["lin"] += 1
                if n >= 4:
                    pe.wait_ge(lin_free[n % 4], n // 4)
                return n % 4

            def lin_done(last, b):
                ready_in[b] += 1
                tile_signal.append((lin_ready[b], ready_in[b]))
                last.then_inc(lin_ready[b], 1)

            def slab_done(last):
                tile_signal.append((slab_used, at_["slab"]))
                last.then_inc(slab_used, 1)

            def work():
                n = at_["work"]
                at_["work"] += 1
                if n >= 2:
                    pe.wait_ge(work_free[n % 2], n // 2)
                return n % 2

            def turn():
                n = at_["turn"]
                at_["turn"] += 1
                if n >= 2:
                    pe.wait_ge(turn_free[n % 2], n // 2)
                return n % 2

            def slab():
                s = at_["slab"]
                at_["slab"] += 1
                pe.wait_ge(slab_split, s + 1)
                return (N_ADA + s) % 2

            def product(to, pairs):
                n = len(pairs)
                for i, ((lh, ll), (rh, rl)) in enumerate(pairs):
                    mm(to, lh, rh, start=i == 0, stop=False)
                    mm(to, lh, rl, start=False, stop=False)
                    last = mm(to, ll, rh, start=False, stop=i == n - 1)
                return last

            def w_tile(slot, a, n=P):
                return W_hi[:, slot, a:a + n], W_lo[:, slot, a:a + n]

            def act_tile(which, k, a=0, n=T):
                hi, lo = (A_hi, A_lo) if which == "A" else (B_hi, B_lo)
                return hi[:, k, a:a + n], lo[:, k, a:a + n]

            def features_on_partitions(which, n_slabs, kts=KD, n=T):
                for _ in range(n_slabs):
                    slot = slab()
                    for m in range(2):
                        b = lin()
                        last = product(bank[b][:, 0:n], [(w_tile(slot, 256 * k + P * m), act_tile(which, k, 0, n))
                                                         for k in range(kts)])
                        if m == 0:
                            lin_done(last, b)
                    slab_done(last)

            def tokens_on_partitions(which, n_slabs, blocks, first=0, width=256):
                for _ in range(n_slabs):
                    if width == 256:
                        slot = slab()
                    else:
                        slot = (N_ADA + at_["slab"] - 1) % 2
                    for q in range(blocks):
                        b = lin()
                        last = product(bank[b][:, 0:width], [(act_tile(which, k, P * q, P),
                                                              w_tile(slot, 256 * k + first, width)) for k in range(KD)])
                        if q < blocks - 1:
                            lin_done(last, b)
                    slab_done(last)

            def norm(name):
                n = NORMS[name][1]
                b = work()
                for k in range(KD):
                    take(square_ready)
                    last = mm(bank[4 + b][:, 0:n], mean_all, S[k % 2][:, 0:n], start=k == 0, stop=k == KD - 1)
                    if k < KD - 2:
                        last.then_inc(square_used, 1)
                last.then_inc(work_ready[b], 1)

            def head_norm(name):
                tiles, n, mean, _ = HEAD_NORMS[name]
                for i in range(len(tiles)):
                    take(square_ready)
                    b = work()
                    mm(bank[4 + b][:, 0:n], mean, S[i % 2][:, 0:n], start=True, stop=True).then_inc(work_ready[b], 1)

            def attention(kind):
                a = att(kind)
                us = units(a)
                n0 = at_["turn"]
                o_bank = {}

                def scores(u):
                    h, q = us[u]
                    if kind == "fox" and q == 0:
                        b = work()
                        for j in range(QT):
                            last = mm(bank[4 + b][:, P * j:T], log_f[:, j, h:h + 1].to_broadcast([P, P]),
                                      upto[:, 0:T - P * j], start=j == 0, stop=j == QT - 1, skip_group_check=True)
                        last.then_inc(work_ready[b], 1)
                    for p in range(a["parts"]):
                        b = work()
                        w = P * (a["k1"](q) - a["k0"](q))
                        mm(bank[4 + b][:, 0:w], a["q"](h, p)[:, P * q:P * q + P],
                           a["k"](h, p)[:, P * a["k0"](q):P * a["k1"](q)], start=True, stop=True)\
                            .then_inc(work_ready[b], 1)

                def turns(u):
                    h, q = us[u]
                    take(p_ready)
                    b = turn()
                    for j in range(a["k1"](q) - a["k0"](q)):
                        last = pe.transpose(bank[6 + b][:, P * j:P * j + P], S[4 + u % 2][:, P * j:P * j + P], ident)
                    last.then_inc(turn_ready[b], 1)

                def values(u):
                    h, q = us[u]
                    pe.wait_ge(turn_free[(n0 + u) % 2], (n0 + u) // 2 + 1)
                    if q == 0:
                        o_bank[h] = lin()
                    row = a["o"](h)[0]
                    for j in range(a["k0"](q), a["k1"](q)):
                        jj = j - a["k0"](q)
                        last = mm(bank[o_bank[h]][row:row + a["m"], P * q:P * q + P], a["v"](h, j),
                                  S[6 + u % 2][:, P * jj:P * jj + P], start=jj == 0, stop=j == a["k1"](q) - 1)
                    last.then_inc(values_used, 1)
                    at_["values"] += 1
                    if q == QT - 1:
                        tile_signal.append((values_used, at_["values"]))

                for u in range(len(us) + 2):
                    if u < len(us):
                        scores(u)
                    if 1 <= u <= len(us):
                        turns(u - 1)
                    if u >= 2:
                        values(u - 2)

            take(const_loaded, 16 * 3)
            take(cact_ready)
            for s in range(N_ADA):
                pe.wait_ge(slab_loaded[s % 2], 16 * (s // 2 + 1))
                for m in range(2):
                    for k in range(KD):
                        last = mm(bank[7][:, 2 * s + m:2 * s + m + 1], raw[:, s % 2, 256 * k + P * m:256 * k + P * m + P],
                                  cact[:, k:k + 1], start=k == 0, stop=k == KD - 1)
                last.then_inc(ada_used, 1)

            norm("first")
            stage()
            features_on_partitions("A", 4)
            tokens_on_partitions("A", 2, QT)
            features_on_partitions("A", 4)
            stage()
            stage()
            for g in range(2):
                b = work()
                for r in range(2):
                    last = mm(bank[4 + b][64 * r:64 * r + 64, :], c_("w_pool", 64 * g, 64)[64 * r:64 * r + 64, :],
                              S[g][64 * r:64 * r + 64, :], start=True, stop=True, skip_group_check=True)
                last.then_inc(work_ready[b], 1)
            stage()
            attention("diff")
            stage()
            head_norm("subln")
            stage()
            features_on_partitions("B", 4)
            stage()
            norm("ffn")
            stage()
            for g in FFN_GROUPS:
                features_on_partitions("A", g)
                stage()
                features_on_partitions("B", 4, kts=g)
                stage()
            norm("final")
            stage()
            if LEVEL >= 2:
                norm("second")
                stage()
                for br in BRANCHES:
                    features_on_partitions("A", 2)
                    if br == "fox":
                        features_on_partitions("A", 2)
                        tokens_on_partitions("A", 2, QT)
                        for q in range(QT):
                            b = lin()
                            lin_done(product(bank[b][:, 0:HEADS], [(act_tile("A", k, P * q, P),
                                                                    (wf_hi[:, k, :], wf_lo[:, k, :]))
                                                                   for k in range(KD)]), b)
                        stage()
                        b = work()
                        for q in range(QT):
                            for j in range(q + 1):
                                last = mm(bank[4 + b][:, HEADS * q:HEADS * q + HEADS],
                                          upto[:, 0:P] if j == q else upto[:, P:2 * P], log_f[:, j, :],
                                          start=j == 0, stop=j == q)
                        last.then_inc(work_ready[b], 1)
                        head_norm("fox_q")
                        head_norm("fox_k")
                    elif br == "swa":
                        slot = slab()
                        b = lin()
                        lin_done(product(bank[b][:, :], [(w_tile(slot, 256 * k), act_tile("A", k))
                                                         for k in range(KD)]), b)
                        tokens_on_partitions("A", 1, QT, first=P, width=P)
                        stage()
                        head_norm("swa_q")
                        head_norm("swa_k")
                    else:
                        stage()
                        norm("mem")
                        stage()
                        features_on_partitions("B", 2, n=MEM)
                        tokens_on_partitions("B", 2, MEM // P)
                        stage()
                        head_norm("mem_q")
                        head_norm("mem_k")
                    stage()
                    attention(br)
                    stage()
                    stage()
                    for i in range(KD):
                        slot = slab()
                        b = lin()
                        lin_done(product(bank[b][:, :], [(w_tile(slot, P * k), act_tile("A", k))
                                                         for k in range(KD)]), b)
                        b = lin()
                        slab_done(product(bank[b][:, :], [(w_tile(slot, P * (KD + k)), act_tile("B", k))
                                                          for k in range(4)]))
                    stage()
                stage()
                features_on_partitions("B", 4)
                stage()
            if LEVEL >= 3:
                norm("peer")
                stage()
                take(act_stage)
                for h in range(HEADS):
                    n = at_["lin"]
                    features_on_partitions("A", 1)
                    for i in range(2):
                        pe.wait_ge(lin_free[(n + i) % 4], (n + i) // 4 + 1)
                    for q in range(QT):
                        b = work()
                        for half in range(2):
                            last = mm(bank[4 + b][:, KEYS * half:KEYS * half + KEYS],
                                      peer_q[:, h % 2, half, P * q:P * q + P], keys[:, 2 * h + half, :],
                                      start=True, stop=True)
                        last.then_inc(work_ready[b], 1)
                stage()
                for q in range(QT):
                    b = turn()
                    for i in range(3):
                        last = pe.transpose(bank[6 + b][:, P * i:P * i + P], picks[:, q, i, :], ident)
                    last.then_inc(turn_ready[b], 1)
                stage()
                pe.drain().then_inc(hot_used, 4)
                with pe.Fori(0, T - 7, 8) as t:
                    for j in range(8):
                        if j % 4 == 0:
                            pe.wait_ge(g_copied, t + j)
                        pe.wait_ge(hot_ready, t + (j + 1))
                        mm(bank[4 + j // 4][:, P * (j % 4):P * (j % 4) + P], hot[:, j % 4, 0, :], hot[:, j % 4, 1, :],
                           start=True, stop=True).then_inc(hot_used, 1)
                stage()
            if DENSE:
                def scores_of(e, j):
                    slot = (N_ADA + N_MID + j) % 2
                    pe.wait_ge(slab_split, e + (j + N_MID + 1))
                    if not isinstance(e, int) or e + j > 0:
                        pe.wait_ge(gelu_ready, e + j)
                    product(bank[0][:, :], [(w_tile(slot, P * k), act_tile("A", k)) for k in range(KD)])\
                        .then_inc(a_ready, 1)

                def outputs_of(e, j, first=False, final=False):
                    slot = (N_ADA + N_MID + j) % 2
                    pe.wait_ge(act_lo_ready, e + j)
                    for m in (6, 0, 1, 2, 7, 3, 4, 5):
                        part = m >= 6
                        if part and not (first and m == 6):
                            pe.wait_ge(part_added, e * 2 + (2 * j - 2 + m - 6))
                        lh, ll = w_tile(slot, D + P * m)
                        rh, rl = act_tile("B", (j + 1) % 2)
                        to = bank[1 if part else 2 + m]
                        mm(to[:, :], lh, rh, start=first or part, stop=False, skip_group_check=True)
                        mm(to[:, :], lh, rl, start=False, stop=False, skip_group_check=True)
                        last = mm(to[:, :], ll, rh, start=False, stop=final or part, skip_group_check=True)
                        if part:
                            last.then_inc(part_ready, 1)
                    last.then_inc(slab_used, 1)

                scores_of(0, 0)
                pe.drain().then_inc(slab_used, 1)
                scores_of(0, 1)
                outputs_of(0, 1, first=True)
                with pe.Fori(2, KEYS - 1, 2) as e:
                    for j in range(2):
                        scores_of(e, j)
                        outputs_of(e, j)
                pe.wait_ge(slab_split, N_MID + N_DENSE)
                outputs_of(KEYS, 0, final=True)

        @block.scalar
        def _(act):
            take = Taken(act).take
            at_ = {"tile": 0, "work": 0, "turn": 0, "values": 0}
            own = [0]

            def step(ins):
                own[0] += 1
                ins.then_inc(act_step, 1)
                act.wait_ge(act_step, own[0])

            def stage_end():
                act.drain().then_inc(act_stage, 1)
                take(dve_stage)

            def load(to, name):
                a, b = TABLE_AT[name]
                act.dma_start(to, tables_in[:, a:b]).then_inc(table_loaded, 16)
                loads[0] += 1

            loads = [0]

            def loaded():
                act.wait_ge(table_loaded, 16 * loads[0])

            def tile(read, skip=0):
                n = at_["tile"]
                at_["tile"] += 1
                act.wait_ge(*tile_signal[n])
                read(bank[n % 4]).then_inc(lin_free[n % 4], 1)

            def copy_to(to, width=T, scale=1.0):
                tile(lambda b: act.activation(to, b[:, 0:width], ACT.Copy, scale=scale))

            def skip(n):
                at_["tile"] += n

            def root(n, to):
                w = at_["work"]
                at_["work"] += 1
                act.wait_ge(work_ready[w % 2], w // 2 + 1)
                act.activation(to[:, 0:n], bank[4 + w % 2][:, 0:n], ACT.Sqrt, bias=small[:, 0:1])\
                    .then_inc(work_free[w % 2], 1)

            def norm(name):
                src, n, _, _, to = NORMS[name]
                for k in range(KD):
                    if k >= 2:
                        take(square_used)
                    act.activation(S[k % 2][:, 0:n], src[:, k, :], ACT.Square).then_inc(square_ready, 1)
                root(n, S[2])
                if to:
                    split(8, lambda k: S[3 + k % 2][:, 0:n], to, n=n)

            def split(tiles, source, to, first=0, n=T):
                for k in range(tiles):
                    take(whole_ready)
                    act.activation((A_hi if to == "A" else B_hi)[:, first + k, 0:n], source(k), ACT.Copy)\
                        .then_inc(hi_ready, 1)

            def head_norm(name):
                tiles, n, _, _ = HEAD_NORMS[name]
                for i in range(len(tiles) + 1):
                    if i < len(tiles):
                        act.activation(S[i % 2][:, 0:n], tiles[i], ACT.Square).then_inc(square_ready, 1)
                    if i >= 1:
                        if i >= 3:
                            take(normed)
                        root(n, S[2 + (i - 1) % 2])
                for _ in range(min(2, len(tiles))):
                    take(normed)

            def attention(kind):
                a = att(kind)
                us = units(a)
                p_slots = P_SLOTS[kind]
                base = (take_count(exp_ready), take_count(p_ready))
                v0 = at_["values"]
                i = 0
                for u in range(len(us) + 2):
                    if u < len(us):
                        h, q = us[u]
                        w = P * (a["k1"](q) - a["k0"](q))
                        for p in range(a["parts"]):
                            take(top_ready)
                            if u * a["parts"] >= len(p_slots):
                                act.wait_ge(p_ready, base[1] + u + 1 - len(p_slots) // a["parts"])
                            if kind == "swa":
                                act.activation(small[:, 32 + i % 4:33 + i % 4], c_("sinks", h), ACT.Exp,
                                               bias=small[:, 24 + i % 2:25 + i % 2])
                            act.activation(p_slots[i % len(p_slots)][:, 0:w], S[i % 2][:, 0:w], ACT.Exp,
                                           bias=small[:, 24 + i % 2:25 + i % 2],
                                           accum_out=small[:, 28 + i % 4:29 + i % 4]).then_inc(exp_ready, 1)
                            i += 1
                    if 1 <= u <= len(us):
                        h, q = us[u - 1]
                        w = P * (a["k1"](q) - a["k0"](q))
                        n = at_["turn"]
                        at_["turn"] += 1
                        act.wait_ge(turn_ready[n % 2], n // 2 + 1)
                        if u - 1 >= 2:
                            act.wait_ge(values_used, v0 + u - 2)
                        act.activation(S[6 + (u - 1) % 2][:, 0:w], bank[6 + n % 2][:, 0:w], ACT.Copy)\
                            .then_inc(turn_free[n % 2], 1)
                    if u >= 2 and us[u - 2][1] == QT - 1:
                        row, i_o, o = a["o"](us[u - 2][0])
                        tile(lambda b: act.activation(o[row:row + a["m"], i_o, :], b[row:row + a["m"], :], ACT.Copy))
                at_["values"] += len(us)
                counted[exp_ready.name] += i
                counted[p_ready.name] += len(us)
                at_["work"] += len(us) * a["parts"] + (HEADS if kind == "fox" else 0)

            counted = {exp_ready.name: 0, p_ready.name: 0}

            def take_count(s):
                return counted[s.name]

            act.dma_start(col[:, :], cols_in).then_inc(const_loaded, 16)
            act.dma_start(tab[:, :], tables_in[:, 0:512]).then_inc(const_loaded, 16)
            act.wait_ge(const_loaded, 16 * 3)
            act.activation(cact[:, :], c_("c", 0, 8), ACT.Silu).then_inc(cact_ready, 1)
            take(small_ready)
            act.activation(small[:, 4:6], small[:, 2:4], ACT.Exp).then_inc(small_done, 1)
            act.activation(wf_hi[:, :, :], c_("w_forget", 0, 64).rearrange("p (k h) -> p k h", k=KD), ACT.Copy)\
                .then_inc(small_done, 1)
            norm("first")
            stage_end()

            load(dist, "distance")
            load(recip_cnt_both, "pool_recip")
            for i in range(4):
                copy_to(Qt[:, i, :], scale=32 ** -0.5)
            for i in range(4):
                copy_to(Kt[:, i, :])
            for c in range(2):
                for q in range(QT):
                    copy_to(V[:, q, 256 * c:256 * c + 256], width=256)
            for i in range(2):
                copy_to(pool_in[:, i, 8:8 + T])
            for i in range(2):
                copy_to(c_gate_t[:, i, :])
            skip(2)
            for i in range(2):
                copy_to(b_gate_t[:, i, :])
            loaded()
            stage_end()

            split(2, lambda i: S[4 + i], "B", first=6)
            stage_end()
            at_["work"] += 2
            split(2, lambda i: S[2 + i], "B", first=4)
            stage_end()
            attention("diff")
            stage_end()
            head_norm("subln")
            split(4, lambda i: Ot[:, i, :], "B")
            stage_end()
            skip(8)
            stage_end()
            norm("ffn")
            stage_end()
            for g in FFN_GROUPS:
                for i in range(g):
                    tile(lambda b: act.activation(S[i % 2], b[:, :], ACT.Silu))
                    take(whole_ready)
                    skip(1)
                    act.activation(B_hi[:, i, :], S[2 + i % 2], ACT.Copy).then_inc(hi_ready, 1)
                stage_end()
                skip(8)
                stage_end()
            norm("final")
            stage_end()
            if LEVEL >= 2:
                load(upto, "upto")
                load(causal, "causal")
                norm("second")
                stage_end()
                for n_br, br in enumerate(BRANCHES):
                    for i in range(4):
                        copy_to(Qt[:, i, :])
                    if br == "fox":
                        for i in range(4):
                            copy_to(Kt[:, i, :])
                        for c in range(2):
                            for q in range(QT):
                                copy_to(V[:, q, 256 * c:256 * c + 256], width=256)
                        skip(QT)
                        take(small_ready)
                        step(act.activation(S[1][:, 0:32], S[0][:, 0:32], ACT.Exp))
                        act.activation(S[2][:, 0:32], S[1][:, 0:32], ACT.Ln, bias=small[:, 1:2]).then_inc(small_done, 1)
                        loaded()
                        stage_end()
                        at_["work"] += 1
                        head_norm("fox_q")
                        head_norm("fox_k")
                    elif br == "swa":
                        load(swa_nd, "swa_distance")
                        load(swa_mask, "swa_mask")
                        copy_to(Kt[:, 0, :])
                        for q in range(QT):
                            copy_to(V[:, q, 0:P], width=P)
                        loaded()
                        stage_end()
                        head_norm("swa_q")
                        head_norm("swa_k")
                    else:
                        act.dma_start(mem_t, mem_in.rearrange("(k p) t -> p k t", p=P)).then_inc(table_loaded, 16)
                        loads[0] += 1
                        loaded()
                        stage_end()
                        norm("mem")
                        stage_end()
                        for i in range(4):
                            copy_to(mem_kt[:, i, :], width=MEM)
                        for c in range(2):
                            for q in range(MEM // P):
                                copy_to(mem_v[:, q, 256 * c:256 * c + 256], width=256)
                        stage_end()
                        head_norm("mem_q")
                        head_norm("mem_k")
                    stage_end()
                    attention(br)
                    stage_end()
                    o = mem_o if br == "mem" else Ot
                    split(4, lambda i: o[:, i, :], "B")
                    stage_end()
                    for i in range(KD):
                        if i >= 2:
                            n = at_["tile"] - 3
                            act.wait_ge(lin_free[n % 4], n // 4 + 1)
                        tile(lambda b: act.activation(S[i % 2], b[:, :], ACT.Sigmoid, bias=c_("b_gate", KD * n_br + i)))
                        skip(1)
                    stage_end()
                split(8, lambda k: merged[:, k, :], "B")
                stage_end()
                skip(8)
                stage_end()
            if LEVEL >= 3:
                norm("peer")
                act.drain().then_inc(act_stage, 1)
                take(dve_stage)
                act.dma_start(keys.rearrange("p i k -> p (i k)"), keys_in).then_inc(table_loaded, 16)
                loads[0] += 1
                load(iota16, "iota16")
                load(iota, "iota")
                loaded()
                act.drain().then_inc(act_stage, 1)
                w = at_["work"]
                for h in range(HEADS):
                    if h >= 2:
                        n = w + QT * (h - 1) - 1
                        act.wait_ge(work_ready[n % 2], n // 2 + 1)
                    for half in range(2):
                        copy_to(peer_q[:, h % 2, half, :])
                at_["work"] += QT * HEADS
                take(small_ready)
                act.activation(eq[:, 512:1024], eq[:, 0:512], ACT.Exp).then_inc(small_done, 1)
                stage_end()
                for q in range(QT):
                    n = at_["turn"]
                    at_["turn"] += 1
                    act.wait_ge(turn_ready[n % 2], n // 2 + 1)
                    act.activation(picks_t[:, :, P * q:P * q + P],
                                   bank[6 + n % 2][:, 0:3 * P].rearrange("p (i t) -> p i t", i=3), ACT.Copy)\
                        .then_inc(turn_free[n % 2], 1)
                stage_end()
                act.drain().then_inc(g_copied, 4)
                for q in range(QT):
                    with act.Fori(0, P - 7, 8) as t:
                        for j in range(2):
                            act.wait_ge(hot_used, t + (P * q + 4 * j + 8))
                            act.activation(g_stage[:, :, bass.ds(t + 4 * j, 4)],
                                           bank[4 + j][:, :].rearrange("p (t e) -> p e t", t=4), ACT.Copy)\
                                .then_inc(g_copied, 4)
                    act.wait_ge(g_copied, 4 + P * (q + 1))
                    act.dma_start(g_dram[q, :, :, :], g_stage).then_inc(g_stored, 16)
                    act.wait_ge(g_stored, 16 * (q + 1))
                stage_end()
            if DENSE:
                def gelu(e, j):
                    act.wait_ge(a_ready, e + (j + 1))
                    act.activation(act_t[:, j, :], bank[0][:, :], ACT.Gelu).then_inc(gelu_ready, 1)
                    act.wait_ge(act_ready, e + (j + 1))
                    if not isinstance(e, int):
                        act.wait_ge(slab_used, e + (j + N_MID))
                    act.activation(B_hi[:, j, :], act_g[:, j, :], ACT.Copy).then_inc(act_hi_ready, 1)

                for j in range(2):
                    gelu(0, j)
                with act.Fori(2, KEYS - 1, 2) as e:
                    for j in range(2):
                        gelu(e, j)

        @block.vector
        def _(dve):
            take = Taken(dve).take
            at_ = {"tile": 0, "work": 0, "turn": 0, "exp": 0}
            own = [0]

            def step(ins):
                own[0] += 1
                ins.then_inc(dve_step, 1)
                dve.wait_ge(dve_step, own[0])

            def stage_end():
                dve.drain().then_inc(dve_stage, 1)
                take(act_stage)

            def tile(read):
                n = at_["tile"]
                at_["tile"] += 1
                dve.wait_ge(*tile_signal[n])
                read(bank[n % 4]).then_inc(lin_free[n % 4], 1)

            def skip(n):
                at_["tile"] += n

            def work(own_=True):
                w = at_["work"]
                at_["work"] += 1
                dve.wait_ge(work_ready[w % 2], w // 2 + 1)
                return w % 2, w // 2 + 1

            def root_inverse(n, to):
                w = at_["work"]
                at_["work"] += 1
                dve.wait_ge(work_free[w % 2], w // 2 + 1)
                step(dve.reciprocal(to[:, 0:n], to[:, 0:n]))

            def rest(k, source, to, first, n=T):
                take(hi_ready)
                hi, lo = (A_hi, A_lo) if to == "A" else (B_hi, B_lo)
                step(dve.tensor_tensor(lo[:, first + k, 0:n], source, hi[:, first + k, 0:n].bitcast(F32), ALU.subtract))

            def norm(name):
                src, n, gain, shift, to = NORMS[name]
                root_inverse(n, S[2])
                for k in range(KD + 1):
                    if k < KD:
                        y = S[3 + k % 2][:, 0:n] if to else src[:, k, :]
                        ins = dve.scalar_tensor_tensor(out=y, in0=src[:, k, :], scalar=gain(k), in1=S[2][:, 0:n],
                                                       op0=ALU.mult, op1=ALU.mult)
                        if shift:
                            step(ins)
                            ins = dve.tensor_scalar(y, y, shift(k), None, ALU.add)
                        if to:
                            ins.then_inc(whole_ready, 1)
                    if to and k >= 1:
                        rest(k - 1, S[3 + (k - 1) % 2][:, 0:n], to, 0, n)

            def split(tiles, source, to, first=0):
                for k in range(tiles):
                    rest(k, source(k), to, first)

            def head_norm(name):
                tiles, n, _, gain = HEAD_NORMS[name]
                for i, t in enumerate(tiles):
                    r = S[2 + i % 2]
                    root_inverse(n, r)
                    dve.scalar_tensor_tensor(out=t, in0=t, scalar=gain(i), in1=r[:, 0:n], op0=ALU.mult, op1=ALU.mult)\
                        .then_inc(normed, 1)

            def attention(kind):
                a = att(kind)
                us = units(a)
                p_slots = P_SLOTS[kind]
                n0, e0 = at_["turn"], at_["exp"]
                i = 0

                def logits(u):
                    nonlocal i
                    h, q = us[u]
                    w = P * (a["k1"](q) - a["k0"](q))
                    if q == 0 and kind == "fox":
                        b, n = work()
                        dve.tensor_copy(ck[:, h % 2, :], bank[4 + b][:, :]).then_inc(work_free[b], 1)
                        dve.wait_ge(work_free[b], n)
                    if q == 0 and kind == "swa":
                        step(dve.scalar_tensor_tensor(out=swa_bias[:, h % 2, :], in0=swa_nd, scalar=2.0 ** -(h + 1),
                                                      in1=swa_mask, op0=ALU.mult, op1=ALU.add))
                    for p in range(a["parts"]):
                        L = S[i % 2][:, 0:w]
                        top = small[:, 24 + i % 2:25 + i % 2]
                        b, n = work()
                        s = bank[4 + b][:, 0:w]
                        if i >= 2:
                            dve.wait_ge(exp_ready, e0 + i - 1)
                        if kind == "diff":
                            ins = dve.scalar_tensor_tensor(out=L, in0=dist[:, 384 - P * q:384 - P * q + T],
                                                           scalar=-(2.0 ** -(h + 1)), in1=s, op0=ALU.mult, op1=ALU.add)
                        elif kind == "fox":
                            ins = dve.scalar_tensor_tensor(out=L, in0=s, scalar=cq[:, q, h:h + 1],
                                                           in1=ck[:, h % 2, 0:w], op0=ALU.add, op1=ALU.subtract)
                        elif kind == "swa":
                            ins = dve.tensor_tensor(L, s, swa_bias[:, h % 2, 256 - w:256], ALU.add)
                        else:
                            ins = dve.tensor_copy(L, s)
                        ins.then_inc(work_free[b], 1)
                        dve.wait_ge(work_free[b], n)
                        if kind == "fox":
                            step(dve.tensor_tensor(L[:, w - P:w], L[:, w - P:w], causal, ALU.add))
                        if kind == "swa":
                            step(dve.tensor_reduce(small[:, 26 + i % 2:27 + i % 2], L, AX, ALU.max))
                            dve.tensor_scalar(top, small[:, 26 + i % 2:27 + i % 2], c_("sinks", h), -1.0, ALU.max, ALU.mult)\
                                .then_inc(top_ready, 1)
                        else:
                            dve.tensor_reduce(top, L, AX, ALU.max, negate=True).then_inc(top_ready, 1)
                        i += 1

                def normalise(u):
                    h, q = us[u]
                    w = P * (a["k1"](q) - a["k0"](q))
                    parts = a["parts"]
                    j = parts * u
                    dve.wait_ge(exp_ready, e0 + j + parts)
                    if u >= 2:
                        n = n0 + u - 2
                        dve.wait_ge(turn_ready[n % 2], n // 2 + 1)
                    sums = small[:, 28 + j % 4:28 + j % 4 + parts]
                    inv = small[:, 36 + 2 * (u % 2):36 + 2 * (u % 2) + parts]
                    if kind == "swa":
                        step(dve.tensor_tensor(sums, sums, small[:, 32 + j % 4:33 + j % 4], ALU.add))
                    step(dve.reciprocal(inv, sums))
                    p0 = p_slots[j % len(p_slots)]
                    if kind == "diff":
                        p1 = p_slots[(j + 1) % len(p_slots)]
                        step(dve.tensor_scalar(p1, p1, inv[:, 1:2], small[:, 6:7], ALU.mult, ALU.mult))
                        dve.scalar_tensor_tensor(out=S[4 + u % 2], in0=p0, scalar=inv[:, 0:1], in1=p1,
                                                 op0=ALU.mult, op1=ALU.add).then_inc(p_ready, 1)
                    else:
                        dve.tensor_scalar(S[4 + u % 2][:, 0:w], p0[:, 0:w], inv, None, ALU.mult).then_inc(p_ready, 1)

                for u in range(len(us) + 1):
                    if u < len(us):
                        logits(u)
                    if u >= 1:
                        normalise(u - 1)
                at_["turn"] += len(us)
                at_["exp"] += len(us) * a["parts"]
                skip(a["heads"])

            step(dve.memset(small[:, :], 0.0))
            dve.memset(small[:, 0:1], EPS)
            dve.memset(small[:, 1:2], 1.0)
            take(const_loaded, 16 * 3)
            lam = c_("lambda", 0, 128)
            for i in range(2):
                step(dve.tensor_tensor(S[5][:, 32 * i:32 * i + 32], lam[:, 64 * i:64 * i + 32],
                                       lam[:, 64 * i + 32:64 * i + 64], ALU.mult))
            dve.tensor_reduce(small[:, 2:4], S[5][:, 0:64].rearrange("p (i n) -> p i n", i=2), AX, ALU.add)\
                .then_inc(small_ready, 1)
            dve.tensor_scalar(small[:, 8:12], c_("g_subln", 0, 4), 1.0 - LAMBDA_INIT, None, ALU.mult)
            dve.tensor_scalar(small[:, 16:17], c_("g_fox_q"), HD ** -0.5, None, ALU.mult)
            dve.tensor_scalar(small[:, 17:18], c_("g_swa_q"), HD ** -0.5, None, ALU.mult)
            dve.tensor_scalar(small[:, 18:19], c_("g_mem_q"), P ** -0.5, None, ALU.mult)
            take(small_done, 2)
            step(dve.tensor_tensor(small[:, 7:8], small[:, 5:6], small[:, 4:5], ALU.subtract))
            dve.tensor_scalar(small[:, 6:7], small[:, 7:8], -LAMBDA_INIT, None, ALU.add)
            dve.tensor_tensor(wf_lo[:, :, :], c_("w_forget", 0, 64).rearrange("p (k h) -> p k h", k=KD),
                              wf_hi[:, :, :].bitcast(F32), ALU.subtract)
            take(ada_used, N_ADA)
            step(dve.tensor_tensor(mod[:, :], bank[7][:, 0:48], c_("b_ada", 0, 48), ALU.add))
            for i, g in enumerate(("g_mix", "g_ffn")):
                a = 8 + 24 * i
                step(dve.scalar_tensor_tensor(out=gs[:, i, :], in0=mod[:, a:a + 8], scalar=1.0, in1=c_(g, 0, 8),
                                              op0=ALU.add, op1=ALU.mult))
            norm("first")
            stage_end()

            for i in range(2):
                dve.memset(pool_in[:, i, 0:8], 0.0)
                dve.memset(pool_in[:, i, 8 + T:16 + T], 0.0)
                dve.memset(conv_in[:, i, 0:1], 0.0)
                dve.memset(conv_in[:, i, 1 + T:2 + T], 0.0)
            skip(4 + 4 + 8 + 2)
            n = at_["tile"]
            skip(2)
            for i in range(2):
                dve.wait_ge(lin_free[(n + i) % 4], (n + i) // 4 + 1)
                tile(lambda b: dve.tensor_tensor(conv_in[:, i, 1:1 + T], c_gate_t[:, i, :], b[:, :], ALU.mult))
            skip(2)
            stage_end()

            for i in range(2):
                w = [c_("conv", 2 * k + i) for k in range(3)]
                y = S[4 + i]
                step(dve.tensor_scalar(y, conv_in[:, i, 0:T], w[0], None, ALU.mult))
                step(dve.scalar_tensor_tensor(out=y, in0=conv_in[:, i, 1:1 + T], scalar=w[1], in1=y,
                                              op0=ALU.mult, op1=ALU.add))
                step(dve.scalar_tensor_tensor(out=y, in0=conv_in[:, i, 2:2 + T], scalar=w[2], in1=y,
                                              op0=ALU.mult, op1=ALU.add))
                dve.tensor_tensor(y, y, b_gate_t[:, i, :], ALU.mult).then_inc(whole_ready, 1)
            split(2, lambda i: S[4 + i], "B", first=6)
            for g in range(2):
                u = pool_in[:, g, :]
                a, b = pool_sum[:, 0, :], pool_sum[:, 1, :]
                step(dve.tensor_tensor(a[:, 1:528], u[:, 0:527], u[:, 1:528], ALU.add))
                step(dve.tensor_tensor(b[:, 2:527], a[:, 1:526], a[:, 3:528], ALU.add))
                if g:
                    step(dve.tensor_tensor(a[:, 4:525], b[:, 2:523], b[:, 6:527], ALU.add))
                    step(dve.tensor_tensor(b[:, 8:521], a[:, 4:517], a[:, 12:525], ALU.add))
                for r, sums in ((0, a), (1, b)):
                    rows = slice(64 * r, 64 * r + 64)
                    step(dve.tensor_tensor(S[g][rows, :], sums[rows, 8:8 + T], recip_cnt[g][rows, :], ALU.mult))
                    step(dve.tensor_tensor(S[g][rows, :], S[g][rows, :], u[rows, 8:8 + T], ALU.subtract))
            stage_end()

            for g in range(2):
                b, n = work()
                dve.tensor_scalar(S[2 + g], bank[4 + b][:, :], c_("pool_scale", g), None, ALU.mult)\
                    .then_inc(work_free[b], 1)
                dve.wait_ge(work_free[b], n)
                dve.drain().then_inc(whole_ready, 1)
            split(2, lambda i: S[2 + i], "B", first=4)
            stage_end()
            attention("diff")
            stage_end()
            head_norm("subln")
            for i in range(4):
                dve.drain().then_inc(whole_ready, 1)
            split(4, lambda i: Ot[:, i, :], "B")
            stage_end()

            def residual(gate=None):
                for m in range(KD):
                    if gate is None:
                        tile(lambda b: dve.tensor_tensor(X[:, m, :], b[:, :], X[:, m, :], ALU.add))
                    else:
                        tile(lambda b: dve.scalar_tensor_tensor(out=X[:, m, :], in0=b[:, :],
                                                                scalar=mod[:, gate + m:gate + m + 1],
                                                                in1=X[:, m, :], op0=ALU.mult, op1=ALU.add))

            residual(16)
            stage_end()
            norm("ffn")
            stage_end()
            for g in FFN_GROUPS:
                for i in range(g):
                    n = at_["tile"]
                    dve.wait_ge(lin_free[n % 4], n // 4 + 1)
                    skip(1)
                    tile(lambda b: dve.tensor_tensor(S[2 + i % 2], S[i % 2], b[:, :], ALU.mult))
                    dve.wait_ge(lin_free[(n + 1) % 4], (n + 1) // 4 + 1)
                    dve.drain().then_inc(whole_ready, 1)
                    rest(i, S[2 + i % 2], "B", 0)
                stage_end()
                residual(40)
                stage_end()
            norm("final")
            stage_end()
            if LEVEL >= 2:
                norm("second")
                stage_end()
                for br in BRANCHES:
                    skip(4)
                    if br == "fox":
                        skip(4 + 8)
                        x = S[3][:, 0:32]
                        for q in range(QT):
                            tile(lambda b: dve.tensor_tensor(x[:, HEADS * q:HEADS * q + HEADS], b[:, 0:HEADS],
                                                             c_("b_forget", 0, 8), ALU.add))
                        dve.wait_ge(lin_free[(at_["tile"] - 1) % 4], (at_["tile"] - 1) // 4 + 1)
                        dve.scalar_tensor_tensor(out=S[0][:, 0:32], in0=x, scalar=-1.0, in1=x,
                                                 op0=ALU.mult, op1=ALU.min).then_inc(small_ready, 1)
                        take(small_done)
                        dve.scalar_tensor_tensor(out=log_f.rearrange("p q h -> p (q h)"), in0=x, scalar=0.0,
                                                 in1=S[2][:, 0:32], op0=ALU.min, op1=ALU.subtract)
                        stage_end()
                        b, n = work()
                        dve.tensor_copy(cq.rearrange("p q h -> p (q h)"), bank[4 + b][:, 0:32])\
                            .then_inc(work_free[b], 1)
                        head_norm("fox_q")
                        head_norm("fox_k")
                    elif br == "swa":
                        skip(1 + QT)
                        stage_end()
                        head_norm("swa_q")
                        head_norm("swa_k")
                    else:
                        stage_end()
                        norm("mem")
                        stage_end()
                        skip(4 + 4)
                        stage_end()
                        head_norm("mem_q")
                        head_norm("mem_k")
                    stage_end()
                    attention(br)
                    stage_end()
                    o = mem_o if br == "mem" else Ot
                    for i in range(4):
                        dve.drain().then_inc(whole_ready, 1)
                    split(4, lambda i: o[:, i, :], "B")
                    stage_end()
                    for i in range(KD):
                        n = at_["tile"]
                        dve.wait_ge(lin_free[n % 4], n // 4 + 1)
                        skip(1)
                        if br == "fox":
                            tile(lambda b: dve.tensor_tensor(merged[:, i, :], S[i % 2], b[:, :], ALU.mult))
                        else:
                            tile(lambda b: dve.tensor_tensor(S[2], S[i % 2], b[:, :], ALU.mult))
                            dve.wait_ge(lin_free[(n + 1) % 4], (n + 1) // 4 + 1)
                            step(dve.tensor_tensor(merged[:, i, :], merged[:, i, :], S[2], ALU.add))
                    stage_end()
                for i in range(KD):
                    dve.drain().then_inc(whole_ready, 1)
                split(8, lambda k: merged[:, k, :], "B")
                stage_end()
                residual()
                stage_end()
            if LEVEL >= 3:
                norm("peer")
                dve.drain().then_inc(dve_stage, 1)
                take(act_stage, 2)

                def top16(sources, values, indices, rests, free=None):
                    for s, v in zip(sources, values):
                        ins = dve.max(v[:, 0:8], s)
                    step(ins)
                    for s, v, i in zip(sources, values, indices):
                        dve.max_index(i[:, 0:8], v[:, 0:8], s)
                    for s, v, r in zip(sources, values, rests):
                        ins = dve.match_replace(r, v[:, 0:8], s, -3.0e38)
                    if free:
                        ins.then_inc(free[0], 1)
                        dve.wait_ge(*free)
                    else:
                        step(ins)
                    for v, r in zip(values, rests):
                        ins = dve.max(v[:, 8:16], r)
                    step(ins)
                    for v, i, r in zip(values, indices, rests):
                        ins = dve.max_index(i[:, 8:16], v[:, 8:16], r)

                top_iu, sum_iu = top_i.bitcast(U32), sum_i.bitcast(U32)
                for h in range(HEADS):
                    skip(2)
                    for q in range(QT):
                        b, n = work()
                        c = cand[:, q % 2, :]
                        top16([bank[4 + b][:, KEYS * i:KEYS * i + KEYS] for i in range(2)],
                              [top_v[:, q, h, TOPK * i:TOPK * i + TOPK] for i in range(2)],
                              [top_iu[:, q, h, TOPK * i:TOPK * i + TOPK] for i in range(2)],
                              [rest_a[:, i, :] for i in range(2)], free=(work_free[b], n))
                        v = top_v[:, q, h, :]
                        step(dve.tensor_tensor(c.rearrange("p (i j) -> p i j", i=TOPK),
                                               v[:, 0:TOPK].unsqueeze(2).to_broadcast([P, TOPK, TOPK]),
                                               v[:, TOPK:2 * TOPK].unsqueeze(1).to_broadcast([P, TOPK, TOPK]),
                                               ALU.add))
                        top16([c], [sum_v[:, q, h, :]], [sum_iu[:, q, h, :]], [cand_rest])
                d = eq[:, 0:512].rearrange("p (g s) -> p g s", s=TOPK)
                ex = eq[:, 512:1024].rearrange("p (g s) -> p g s", s=TOPK)
                sv = sum_v.rearrange("p q h s -> p (q h) s")
                dve.tensor_tensor(d, sv, sv[:, :, 0:1].to_broadcast([P, QT * HEADS, TOPK]), ALU.subtract)\
                    .then_inc(small_ready, 1)
                take(small_done)
                gsum = eq[:, 1024:1024 + QT * HEADS]
                step(dve.tensor_reduce(gsum, ex, AX, ALU.add))
                step(dve.reciprocal(gsum, gsum))
                step(dve.tensor_tensor(picks[:, :, 2, :].rearrange("p q (h s) -> p q h s", h=HEADS),
                                       ex.rearrange("p (q h) s -> p q h s", q=QT),
                                       gsum.rearrange("p (q h) -> p q h", q=QT).unsqueeze(3)
                                       .to_broadcast([P, QT, HEADS, TOPK]), ALU.mult))
                iwu = iw.bitcast(U32)
                eq3 = eq.rearrange("p (s j) -> p s j", j=TOPK)
                eq4 = eq.rearrange("p (h s j) -> p h s j", h=HEADS, j=TOPK)
                for q in range(QT):
                    si = sum_iu[:, q, :, :].rearrange("p h s -> p (h s)")
                    dve.tensor_scalar(iwu[:, 0, :], si, 4, None, ALU.logical_shift_right)
                    dve.tensor_scalar(iwu[:, 1, :], si, 15, None, ALU.bitwise_and)
                    step(dve.tensor_copy(top_f, top_iu[:, q, :, :]))
                    dve.tensor_copy(sel_hi, iwu[:, 0, :])
                    step(dve.tensor_copy(sel_lo, iwu[:, 1, :]))
                    for i, sel in enumerate((sel_hi, sel_lo)):
                        step(dve.tensor_tensor(eq3, sel.unsqueeze(2).to_broadcast([P, P, TOPK]),
                                               iota16.unsqueeze(1).to_broadcast([P, P, TOPK]), ALU.is_equal))
                        step(dve.tensor_tensor(eq4, eq4, top_f[:, :, TOPK * i:TOPK * i + TOPK].unsqueeze(2)
                                               .to_broadcast([P, HEADS, TOPK, TOPK]), ALU.mult))
                        step(dve.tensor_reduce(picks[:, q, i, :], eq3, AX, ALU.add))
                stage_end()
                stage_end()
                with dve.Fori(0, T - 3, 4) as t:
                    for j in range(4):
                        dve.wait_ge(hot_used, t + (j + 1))
                        dve.tensor_scalar(hot[:, j, 0, :], iota, picks_t[:, 0, bass.ds(t + j, 1)], None, ALU.is_equal)
                        dve.tensor_scalar(hot[:, j, 1, :], iota, picks_t[:, 1, bass.ds(t + j, 1)],
                                          picks_t[:, 2, bass.ds(t + j, 1)], ALU.is_equal, ALU.mult)\
                            .then_inc(hot_ready, 1)
                stage_end()
            if DENSE:
                step(dve.memset(acc[:, :, :], 0.0))

                def add_part(e, j, i):
                    dve.wait_ge(part_ready, e * 2 + (2 * j - 1 + i))
                    dve.tensor_tensor(acc[:, i, :], bank[1][:, :], acc[:, i, :], ALU.add).then_inc(part_added, 1)

                def gated(e, j):
                    first = isinstance(e, int)
                    dve.wait_ge(gelu_ready, e + (j + 1))
                    dve.wait_ge(g_loaded[j], e * 8 + 16)
                    dve.tensor_tensor(act_g[:, j, :], act_t[:, j, :], g_in[:, j, :], ALU.mult).then_inc(act_ready, 1)
                    if not (first and j == 0):
                        add_part(e, j, 0)
                    dve.wait_ge(act_hi_ready, e + (j + 1))
                    if not first:
                        dve.wait_ge(slab_used, e + (j + N_MID))
                    dve.tensor_tensor(B_lo[:, j, :], act_g[:, j, :], B_hi[:, j, :].bitcast(F32), ALU.subtract)\
                        .then_inc(act_lo_ready, 1)
                    if not (first and j == 0):
                        add_part(e, j, 1)

                for j in range(2):
                    gated(0, j)
                with dve.Fori(2, KEYS - 1, 2) as e:
                    for j in range(2):
                        gated(e, j)
                for i in range(2):
                    add_part(KEYS, 0, i)
                dve.wait_ge(part_added, 2 * KEYS)
                for i in range(2):
                    dve.tensor_tensor(X[:, 6 + i, :], acc[:, i, :], X[:, 6 + i, :], ALU.add)
                dve.wait_ge(slab_used, N_MID + N_DENSE)
                for m in range(6):
                    dve.tensor_tensor(X[:, m, :], bank[2 + m][:, :], X[:, m, :], ALU.add)
            dve.drain().then_inc(x_done, 1)


def _slab(w):
    import numpy as np
    k = w.shape[0] // P
    a = w.reshape(k, P, w.shape[1]).transpose(1, 0, 2).reshape(P, -1)
    out = np.zeros((P, SLAB), np.float32)
    out[:, :a.shape[1]] = a
    return out


def _stream(i):
    import numpy as np
    slabs = []

    def columns(w, first=0, last=None):
        for a in range(first, w.shape[1] if last is None else last, 256):
            slabs.append(_slab(w[:, a:a + 256]))

    columns(i["w_ada"][0])
    w = i["w_in"][0]
    columns(w, 0, 1792)
    columns(w, 2048, 2304)
    columns(w, 2304, 2560)
    columns(w, 1792, 2048)
    columns(i["w_out"][0])
    wg, wd = i["w_gate_up"][0], i["w_down"][0]
    f = 0
    for g in FFN_GROUPS:
        for j in range(f, f + g):
            slabs.append(_slab(np.concatenate([wg[:, P * j:P * j + P], wg[:, DFF + P * j:DFF + P * j + P]], 1)))
        columns(wd[P * f:P * (f + g)])
        f += g
    w = i["w_in_2"][0]
    gates_at = 2824
    pairs = [h for n in range(4) for h in (n, n + 4)]
    w_o = [i["w_fox_o_2"][0],
           i["w_swa_o_2"][0].reshape(HEADS, HD, D)[pairs].reshape(HEADS * HD, D), i["w_mem_o_2"][0]]
    for n, br in enumerate(("fox", "swa", "mem")):
        if br == "fox":
            columns(w, 0, 1536)
        elif br == "swa":
            columns(w[:, 1544:2056].reshape(D, HEADS, HD)[:, pairs].reshape(D, HEADS * HD))
            columns(w, 2056, 2312)
        else:
            columns(w, 2312, 2824)
            columns(i["w_mem_kv_2"][0])
        for m in range(KD):
            a = gates_at + D * n + P * m
            s = _slab(w[:, a:a + P])
            s[:, D:D + 512] = _slab(w_o[n][:, P * m:P * m + P])[:, 0:512]
            slabs.append(s)
    columns(i["w_out_2"][0])
    columns(i["w_peer_q_2"][0])
    u = i["peer_u_2"][0].reshape(KEYS, KEYS, KD, P)
    v = i["peer_v_2"][0].reshape(KEYS, KEYS, D)
    experts = np.zeros((N_DENSE, P, 2, D), np.float32)
    experts[:KEYS, :, 0, :] = u.transpose(1, 3, 2, 0).reshape(KEYS, P, D)
    experts[1:, :, 1, :] = v.transpose(1, 0, 2)
    assert len(slabs) == N_ADA + N_MID, len(slabs)
    return np.concatenate([np.stack(slabs), experts.reshape(N_DENSE, P, SLAB)])


def _columns(i):
    import numpy as np

    def tiles(a):
        return a.reshape(-1, P).T

    def rows(a):
        return np.broadcast_to(a.reshape(1, -1), (P, a.size))

    def twice(a):
        return np.concatenate([a.reshape(-1)] * 2).reshape(P, 1)

    parts = {
        "c": tiles(i["c"]), "b_ada": tiles(i["b_ada"]), "g_mix": tiles(i["g_mix"]), "g_subln": tiles(i["g_subln"]),
        "pool_scale": tiles(i["pool_scale"]), "conv": tiles(i["conv_w"]), "g_ffn": tiles(i["g_ffn"]),
        "g_final": tiles(i["g_final"]), "g_norm1": tiles(i["norm1_g_2"]), "b_gate": tiles(i["b_gate_2"]),
        "g_fox_q": twice(i["fox_q_g_2"]), "g_fox_k": twice(i["fox_k_g_2"]), "g_swa_q": twice(i["swa_q_g_2"]),
        "g_swa_k": twice(i["swa_k_g_2"]), "g_mem": tiles(i["mem_norm_g_2"]), "g_mem_q": tiles(i["mem_q_g_2"]),
        "g_mem_k": tiles(i["mem_k_g_2"]), "g_norm2": tiles(i["norm2_g_2"]), "b_forget": rows(i["b_forget_2"]),
        "sinks": rows(i["swa_sinks_2"]),
        "lambda": rows(np.concatenate([i[n].reshape(-1) for n in ("lambda_q1", "lambda_k1", "lambda_q2", "lambda_k2")])),
        "w_forget": i["w_in_2"][0][:, 1536:1544].reshape(KD, P, HEADS).transpose(1, 0, 2).reshape(P, -1),
        "w_pool": i["w_pool"][0].reshape(2, P, 64).transpose(1, 0, 2).reshape(P, -1),
    }
    return np.ascontiguousarray(np.concatenate([parts[n] for n, _ in COLS], 1))


def _tables():
    import numpy as np
    p = np.arange(P)[:, None]
    out = {"ident": np.eye(P), "mean_all": np.full((P, P), 1.0 / D), "mean_128": np.full((P, P), 1.0 / P),
           "mean_64": (p // 64 == np.arange(P)[None] // 64) / 64.0,
           "distance": np.abs(p - np.arange(896)[None] + 384),
           "causal": np.where(np.arange(P)[None] <= p, 0.0, NEG_INF), "upto": p <= np.arange(512)[None],
           "iota": np.broadcast_to(np.arange(P)[None], (P, P)), "iota16": np.broadcast_to(np.arange(16)[None], (P, 16))}
    t = np.arange(T)
    counts = []
    for w in (2, 4, 8, 16):
        counts.append(np.clip(t + w - w // 2, 0, T) - np.clip(t - w // 2, 0, T))
    r = np.stack([1.0 / c for c in counts])
    out["pool_recip"] = np.concatenate([np.repeat(r[2 * g:2 * g + 2], 64, axis=0) for g in range(2)], 1)
    d = p + P - np.arange(256)[None]
    ok = (d >= 0) & (d < P)
    out["swa_distance"] = np.where(ok, -d, 0)
    out["swa_mask"] = np.where(ok, 0.0, NEG_INF)
    return np.ascontiguousarray(np.concatenate([out[n].astype(np.float32) for n, _ in TABLES], 1))


def kernel(**inputs):
    import numpy as np
    import concourse.bacc as bacc
    from concourse.bass_utils import run_bass_kernel_spmd

    i = {k: np.asarray(v) for k, v in inputs.items()}
    keys_t = np.stack([i["peer_keys1_2"][0], i["peer_keys2_2"][0]], 1).reshape(16, KEYS, P).transpose(2, 0, 1)\
        .reshape(P, 16 * KEYS)
    arrays = {"x_t": np.ascontiguousarray(i["x"][0].T), "weights": _stream(i), "columns": _columns(i),
              "tables": _tables(), "mem_t_in": np.ascontiguousarray(i["mem_2"][0].T),
              "keys_t": np.ascontiguousarray(keys_t)}
    nc = bacc.Bacc("TRN2", target_bir_lowering=False, num_devices=1)
    args = [nc.dram_tensor(n, a.shape, F32, kind="ExternalInput").ap() for n, a in arrays.items()]
    out = nc.dram_tensor("out_t", (D, T), F32, kind="ExternalOutput").ap()
    build(nc, *args, out)
    r = run_bass_kernel_spmd(nc, [arrays], core_ids=[0])
    return np.ascontiguousarray(r.results[0]["out_t"].T)[None]
```

```python
from contextlib import ExitStack

import concourse.bass as bass
from concourse import mybir

P = 128
T = 512
QT = T // P
D = 1024
KD = D // P
DFF = 2816
FT = DFF // P
FFN_GROUPS = (8, 8, 6)
HEADS = 8
HD = 64
MEM = 256
MEM_HEADS = 4
KEYS = 128
TOPK = 16
EPS = 1e-6
NEG_INF = -1e30
LAMBDA_INIT = 0.2

SLAB = 2048
N_ADA = 6 * D // 256
ADA_FIRST = 8
ADA_LATER_AT = 10
N_MID = 93
PAIRS = KEYS // 2
U_PICKS, U_TOKENS, U_STORE = 8, 8, 4
assert HEADS + U_PICKS + QT * (U_TOKENS + U_STORE) == PAIRS and P % (2 * U_TOKENS) == 0
U_AT = HEADS + U_PICKS

F32 = mybir.dt.float32
F32R = mybir.dt.float32r
U32 = mybir.dt.uint32
I32 = mybir.dt.int32
ALU = mybir.AluOpType
ACT = mybir.ActivationFunctionType
AX = mybir.AxisListType.X

COLS = [("b_ada", 48), ("g_mix", 8), ("g_subln", 4), ("pool_scale", 2), ("conv", 6), ("g_ffn", 8),
        ("g_final", 8), ("g_norm1", 8), ("b_gate", 24), ("g_fox_q", 1), ("g_fox_k", 1), ("g_swa_q", 1),
        ("g_swa_k", 1), ("g_mem", 8), ("g_mem_q", 1), ("g_mem_k", 1), ("g_norm2", 8), ("b_forget", 8),
        ("sinks", 8), ("lambda", 128), ("w_forget", 64), ("w_pool", 128)]
COL_AT = {}
N_COLS = 0
for _name, _width in COLS:
    COL_AT[_name] = (N_COLS, N_COLS + _width)
    N_COLS += _width

TABLES = [("ident", 128), ("mean_all", 128), ("mean_64", 128), ("mean_128", 128), ("distance", 896),
          ("pool_recip", 1024), ("causal", 128), ("upto", 512), ("swa_distance", 256), ("swa_mask", 256), ("iota", 128),
          ("iota16", 16)]
TABLE_AT = {}
N_TABLE = 0
for _name, _width in TABLES:
    TABLE_AT[_name] = (N_TABLE, N_TABLE + _width)
    N_TABLE += _width

LEVEL, DENSE = 3, True
ARENA = 19170


class Taken:

    def __init__(self, eng):
        self.eng = eng
        self.count = {}

    def take(self, sem, k=1):
        self.count[sem.name] = self.count.get(sem.name, 0) + k
        self.eng.wait_ge(sem, self.count[sem.name])


def build(nc, x_in, stream, cols_in, tables_in, mem_in, keys_in, out):
    g_dram = nc.dram_tensor("gates_dram", [QT, P, KEYS, P], F32, kind="Internal").ap()
    gelu_dram = nc.dram_tensor("gelu_dram", [PAIRS, P, 2 * T], F32, kind="Internal").ap()

    with ExitStack() as ctx:
        def sb(name, shape, dt=F32):
            return ctx.enter_context(nc.sbuf_tensor(name, shape, dt))

        def sem(name):
            return ctx.enter_context(nc.semaphore(name))

        X = sb("X", [P, KD, T])
        A_hi = sb("A_hi", [P, KD, T], F32R)
        A_lo = sb("A_lo", [P, KD, T], F32R)
        with nc.sbuf_tensor("B_plain", [P, KD, T], F32) as B_plain:
            pass
        B_hi = sb("B_hi", [P, KD, T], F32R)
        with nc.sbuf_tensor("B_lo_plain", [P, KD, T], F32) as B_lo_plain:
            pass
        B_lo = sb("B_lo", [P, KD, T], F32R)
        raw = sb("raw", [P, 2, SLAB])
        with nc.sbuf_tensor("W_plain", [P, 4, SLAB], F32) as W_plain:
            pass
        W_hi = sb("W_hi", [P, 2, SLAB], F32R)
        W_lo = sb("W_lo", [P, 2, SLAB], F32R)
        tab = sb("tab", [P, 512])
        col = sb("col", [P, N_COLS])
        wf_hi = sb("wf_hi", [P, KD, HEADS], F32R)
        wf_lo = sb("wf_lo", [P, KD, HEADS], F32R)
        mod = sb("mod", [P, 48])
        gs = sb("gs", [P, 2, KD])
        small = sb("small", [P, 48])
        zero = sb("zero", [P, 1])
        arena = sb("arena", [P, ARENA])
        bank = [ctx.enter_context(nc.psum_tensor(f"bank{i}", [P, 512], F32)) for i in range(8)]

        def at(start, *shape):
            size = 1
            for n in shape:
                size *= n
            v = arena[:, start:start + size]
            if len(shape) == 2:
                v = v.rearrange("p (a b) -> p a b", b=shape[1])
            if len(shape) == 3:
                v = v.rearrange("p (a b c) -> p a b c", b=shape[1], c=shape[2])
            return v

        ident, mean_all, mean_64, mean_128 = (tab[:, i * P:(i + 1) * P] for i in range(4))

        def c_(name, i=0, n=1):
            a = COL_AT[name][0] + i
            return col[:, a:a + n]

        S = [at(512 * i, 512) for i in range(8)]
        Qt, Kt = at(4096, 4, T), at(6144, 4, T)
        V = at(8192, QT, 512)
        Ot = at(10240, 4, T)
        pool_in = at(12288, 2, 528)
        conv_in = at(13344, 2, 514)
        b_gate_t, c_gate_t = at(14372, 2, T), at(15396, 2, T)
        dist = at(16420, 896)
        pool_sum = at(17316, 2, 528)
        c_row = at(15396, 1024)
        merged = at(12288, KD, T)
        upto = at(16384, 512)
        ck = at(16896, 2, 512)
        causal = at(17920, P)
        log_f, cq = at(18048, QT, HEADS), at(18080, QT, HEADS)
        swa_nd, swa_mask, swa_bias = at(16384, 256), at(16640, 256), at(16896, 2, 256)
        mem_t = at(8192, KD, MEM)
        mem_kt, mem_v = at(6144, MEM_HEADS, MEM), at(10240, 2, 512)
        mem_o = at(8192, MEM_HEADS, T)
        recip_cnt = [at(4096 * 0 + 512 * 6, 512), at(512 * 7, 512)]
        keys = at(0, 16, KEYS)
        peer_q = at(2048, 2, 2, T)
        top_v = at(4096, QT, HEADS, 2 * TOPK)
        top_i = at(5120, QT, HEADS, 2 * TOPK)
        sum_v = at(6144, QT, HEADS, TOPK)
        sum_i = at(6656, QT, HEADS, TOPK)
        rest_a = at(7168, 2, KEYS)
        cand = at(7424, 2, 256)
        cand_rest = at(7936, 256)
        iota16 = at(8192, TOPK)
        sel_hi, sel_lo = at(8208, P), at(8336, P)
        top_f = at(8464, HEADS, 2 * TOPK)
        eq = at(8720, 2048)
        picks = at(10768, QT, 3, P)
        iw = at(12304, 2, P)
        picks_t = at(16384, 3, T)
        iota = at(17920, KEYS)
        hot = at(18048, 4, 2, KEYS)
        g_stage = at(0, KEYS, P)
        gate_t = [(B_plain if i < 4 else B_lo_plain)[:, 4 + i % 4, :] for i in range(KD)]
        gelu_in, g_in, prod = at(0, 2, 2 * T), at(2048, 2, 2 * T), at(4096, 2, 2 * T)
        gelu_out = B_plain[:, 0:4, :]

        slab_loaded = [sem("slab_loaded0"), sem("slab_loaded1")]
        ada_loaded = [sem(f"ada_loaded{i}") for i in range(4)]
        ada_used = sem("ada_used")
        ada_times_c = sem("ada_times_c")
        zero_ready = sem("zero_ready")
        slab_half = sem("slab_half")
        slab_split = sem("slab_split")
        slab_used = sem("slab_used")
        const_loaded, table_loaded = sem("const_loaded"), sem("table_loaded")
        lin_ready = [sem(f"lin_ready{i}") for i in range(4)]
        lin_free = [sem(f"lin_free{i}") for i in range(4)]
        work_ready = [sem(f"work_ready{i}") for i in range(2)]
        work_free = [sem(f"work_free{i}") for i in range(2)]
        turn_ready = [sem(f"turn_ready{i}") for i in range(2)]
        turn_free = [sem(f"turn_free{i}") for i in range(2)]
        act_stage, dve_stage = sem("act_stage"), sem("dve_stage")
        act_step, dve_step = sem("act_step"), sem("dve_step")
        lo_ready = sem("lo_ready")
        gate_ready = sem("gate_ready")
        c_loaded, c_ready = sem("c_loaded"), sem("c_ready")
        square_ready, square_used = sem("square_ready"), sem("square_used")
        root_ready = sem("root_ready")
        normed = sem("normed")
        whole_ready = sem("whole_ready")
        hi_ready = sem("hi_ready")
        top_ready = sem("top_ready")
        exp_ready = sem("exp_ready")
        p_ready = sem("p_ready")
        values_used = sem("values_used")
        small_ready, small_done = sem("small_ready"), sem("small_done")
        hot_ready, hot_used = sem("hot_ready"), sem("hot_used")
        g_copied, g_stored = sem("g_copied"), sem("g_stored")
        pair_loaded = [sem("pair_loaded0"), sem("pair_loaded1")]
        gelu_stored = [sem("gelu_stored0"), sem("gelu_stored1")]
        a_ready, gelu_ready, act_ready = sem("a_ready"), sem("gelu_ready"), sem("act_ready")
        act_hi_ready, act_lo_ready = sem("act_hi_ready"), sem("act_lo_ready")
        x_done, stored = sem("x_done"), sem("stored")

        block = ctx.enter_context(nc.Block())
        NORMS = {
            "first": (X, T, lambda k: gs[:, 0, k:k + 1], lambda k: mod[:, k:k + 1], "A"),
            "ffn": (X, T, lambda k: gs[:, 1, k:k + 1], lambda k: mod[:, 24 + k:25 + k], "A"),
            "final": (X, T, lambda k: c_("g_final", k), None, None),
            "second": (X, T, lambda k: c_("g_norm1", k), None, "A"),
            "mem": (mem_t, MEM, lambda k: c_("g_mem", k), None, "B"),
            "peer": (X, T, lambda k: c_("g_norm2", k), None, "A"),
        }
        HEAD_NORMS = {
            "subln": ([Ot[:, i, :] for i in range(4)], T, mean_64, lambda i: small[:, 8 + i:9 + i]),
            "fox_q": ([Qt[:, i, :] for i in range(4)], T, mean_64, lambda i: small[:, 16:17]),
            "fox_k": ([Kt[:, i, :] for i in range(4)], T, mean_64, lambda i: c_("g_fox_k")),
            "swa_q": ([Qt[:, i, :] for i in range(4)], T, mean_64, lambda i: small[:, 17:18]),
            "swa_k": ([Kt[:, 0, :]], T, mean_64, lambda i: c_("g_swa_k")),
            "mem_q": ([Qt[:, i, :] for i in range(4)], T, mean_128, lambda i: small[:, 18:19]),
            "mem_k": ([mem_kt[:, i, :] for i in range(4)], MEM, mean_128, lambda i: c_("g_mem_k")),
        }

        def att(kind):
            if kind == "diff":
                return dict(heads=HEADS, parts=2, k0=lambda q: 0, k1=lambda q: QT,
                            q=lambda h, p: (Qt[64 * (h % 2) + 32 * p:64 * (h % 2) + 32 * p + 32, h // 2, :]),
                            k=lambda h, p: (Kt[64 * (h % 2) + 32 * p:64 * (h % 2) + 32 * p + 32, h // 2, :]),
                            v=lambda h, j: V[:, j, HD * h:HD * h + HD], m=HD,
                            o=lambda h: (64 * (h % 2), h // 2, Ot))
            if kind == "fox":
                return dict(heads=HEADS, parts=1, k0=lambda q: 0, k1=lambda q: q + 1,
                            q=lambda h, p: Qt[64 * (h % 2):64 * (h % 2) + 64, h // 2, :],
                            k=lambda h, p: Kt[64 * (h % 2):64 * (h % 2) + 64, h // 2, :],
                            v=lambda h, j: V[:, j, HD * h:HD * h + HD], m=HD,
                            o=lambda h: (64 * (h % 2), h // 2, Ot))
            if kind == "swa":
                return dict(heads=HEADS, parts=1, k0=lambda q: max(q - 1, 0), k1=lambda q: q + 1,
                            q=lambda h, p: Qt[64 * (h // 4):64 * (h // 4) + 64, h % 4, :],
                            k=lambda h, p: Kt[64 * (h // 4):64 * (h // 4) + 64, 0, :],
                            v=lambda h, j: V[:, j, HD * (h // 4):HD * (h // 4) + HD], m=HD,
                            o=lambda h: (64 * (h // 4), h % 4, Ot))
            return dict(heads=MEM_HEADS, parts=1, k0=lambda q: 0, k1=lambda q: MEM // P,
                        q=lambda h, p: Qt[:, h, :], k=lambda h, p: mem_kt[:, h, :],
                        v=lambda h, j: mem_v[:, j, P * h:P * h + P], m=P, o=lambda h: (0, h, mem_o))

        def units(a):
            return [(h, q) for h in range(a["heads"]) for q in range(QT)]

        BRANCHES = ("fox", "swa", "mem")

        P_SLOTS = {"diff": [S[2], S[3], at(14372, 512), at(14884, 512)]}
        for _kind in BRANCHES:
            P_SLOTS[_kind] = [S[2], S[3]]
        recip_cnt_both = at(512 * 6, 1024)

        def ada_rows(slab):
            return slab.rearrange("p (m i) -> p m i", m=2)

        c_rows = c_row.unsqueeze(1).to_broadcast([P, 2, D])

        def ada_place(s):
            return W_plain[:, s - 2, :] if 2 <= s < 6 else raw[:, s % 2, :]

        tile_signal = []

        @block.sync
        def _(sp):
            base = N_ADA + N_MID + PAIRS

            for s in range(2):
                sp.dma_start(raw[:, s, :], stream[s, :, :]).then_inc(slab_loaded[s], 16)
            sp.dma_start(X[:, :, :], x_in.rearrange("(k p) t -> p k t", p=P)).then_inc(const_loaded, 16)
            for s in range(4):
                sp.dma_start(W_plain[:, s, :], stream[2 + s, :, :]).then_inc(ada_loaded[s], 16)

            def load_slab(n, place):
                sp.dma_start(raw[:, place, :], stream[n, :, :]).then_inc(slab_loaded[place], 16)

            for s in range(6, ADA_FIRST + 2):
                sp.wait_ge(ada_used, s - 5 if s < ADA_FIRST else s - 1)
                load_slab(s, s % 2)
            for s in range(2, ADA_LATER_AT):
                sp.wait_ge(slab_split, s - 1)
                load_slab(ADA_FIRST + s, s % 2)
            for s in range(ADA_FIRST, N_ADA + 2):
                if s < ADA_FIRST + 2:
                    sp.wait_ge(slab_split, ADA_LATER_AT - 1 + s - ADA_FIRST)
                else:
                    sp.wait_ge(ada_used, s - 1)
                load_slab(ADA_LATER_AT + s, s % 2)
            tail = (base - N_ADA) % 2
            with sp.Fori(N_ADA + ADA_LATER_AT + 2, base - tail - 1, 2) as s:
                for j in range(2):
                    sp.wait_ge(slab_split, s + (j - 1 - N_ADA))
                    sp.dma_start(raw[:, j, :], stream[s + j, :, :]).then_inc(slab_loaded[j], 16)
            for s in range(base - tail, base):
                sp.wait_ge(slab_split, s - 1 - N_ADA)
                sp.dma_start(raw[:, s % 2, :], stream[s, :, :]).then_inc(slab_loaded[s % 2], 16)

            def value_slab(s, j):
                slot = (base + j) % 2
                sp.wait_ge(slab_split, s + (j + base - N_ADA - 1))
                sp.dma_start(raw[:, slot, :], stream[s + (base + j), :, :]).then_inc(slab_loaded[slot], 16)

            def pair(s, j):
                if isinstance(s, int):
                    sp.wait_ge(g_stored, 16 * QT)
                else:
                    sp.wait_ge(act_ready, s + (j - 1))
                sp.wait_ge(gelu_stored[j], s * 8 + 16)
                sp.dma_start(gelu_in[:, j, :], gelu_dram[s + j, :, :]).then_inc(pair_loaded[j], 16)
                sp.dma_start(g_in[:, j, :].rearrange("p (q x) -> p q x", q=QT),
                             g_dram[:, :, bass.ds(s * 2 + 2 * j, 2), :].rearrange("q p e t -> p q (e t)"))\
                    .then_inc(pair_loaded[j], 16)

            for j in range(2):
                value_slab(0, j)
            for j in range(2):
                pair(0, j)
            with sp.Fori(2, PAIRS - 1, 2) as s:
                for j in range(2):
                    value_slab(s, j)
                    pair(s, j)
            sp.wait_ge(x_done, 1)
            sp.dma_start(out.rearrange("(k p) t -> p k t", p=P), X[:, :, :]).then_inc(stored, 16)
            sp.wait_ge(stored, 16)

        @block.gpsimd
        def _(pool):
            def split(s, j, ada=N_ADA - 4):
                pool.wait_ge(slab_loaded[j], s * 8 + (8 * ada + 16))
                if not isinstance(s, int) or s >= 2:
                    pool.wait_ge(slab_used, s + (j - 1))
                pool.tensor_tensor(W_hi[:, j, :], raw[:, j, :], zero[:, :].to_broadcast([P, SLAB]), ALU.add).then_inc(slab_half, 1)
                pool.wait_ge(slab_half, s + (j + 1))
                pool.tensor_tensor(W_lo[:, j, :], raw[:, j, :], W_hi[:, j, :].bitcast(F32),
                                   ALU.subtract).then_inc(slab_split, 1)

            pool.memset(zero[:, :], 0.0).then_inc(zero_ready, 1)
            pool.wait_ge(zero_ready, 1)
            n = N_MID + 2 * PAIRS
            for s in range(0, ADA_LATER_AT, 2):
                for j in range(2):
                    split(s, j, ADA_FIRST - 4)
            pool.wait_ge(c_ready, 2)
            for s in range(ADA_FIRST, N_ADA):
                pool.wait_ge(slab_loaded[s % 2], 8 * (s - s % 2 + ADA_LATER_AT - 4) + 16)
                w = ada_rows(raw[:, s % 2, :])
                pool.tensor_tensor(w, w, c_rows, ALU.mult).then_inc(ada_times_c, 1)
            with pool.Fori(ADA_LATER_AT, n - n % 2 - 1, 2) as s:
                for j in range(2):
                    split(s, j)
            if n % 2:
                split(n - 1, 0)

        @block.tensor
        def _(pe):
            take = Taken(pe).take
            at_ = {"slab": 0, "lin": 0, "work": 0, "turn": 0, "values": 0}
            ready_in = [0, 0, 0, 0]
            mm = pe.matmul

            def stage():
                take(act_stage)
                take(dve_stage)

            def lin():
                n = at_["lin"]
                at_["lin"] += 1
                if n >= 4:
                    pe.wait_ge(lin_free[n % 4], n // 4)
                return n % 4

            def lin_done(last, b):
                ready_in[b] += 1
                tile_signal.append((lin_ready[b], ready_in[b]))
                last.then_inc(lin_ready[b], 1)

            def slab_done(last):
                tile_signal.append((slab_used, at_["slab"]))
                last.then_inc(slab_used, 1)

            def work():
                n = at_["work"]
                at_["work"] += 1
                if n >= 2:
                    pe.wait_ge(work_free[n % 2], n // 2)
                return n % 2

            def turn():
                n = at_["turn"]
                at_["turn"] += 1
                if n >= 2:
                    pe.wait_ge(turn_free[n % 2], n // 2)
                return n % 2

            def slab():
                s = at_["slab"]
                at_["slab"] += 1
                pe.wait_ge(slab_split, s + 1)
                return (N_ADA + s) % 2

            def product(to, pairs):
                n = len(pairs)
                for i, ((lh, ll), (rh, rl)) in enumerate(pairs):
                    mm(to, lh, rh, start=i == 0, stop=False)
                    mm(to, lh, rl, start=False, stop=False)
                    last = mm(to, ll, rh, start=False, stop=i == n - 1)
                return last

            def w_tile(slot, a, n=P):
                return W_hi[:, slot, a:a + n], W_lo[:, slot, a:a + n]

            def act_tile(which, k, a=0, n=T):
                hi, lo = (A_hi, A_lo) if which == "A" else (B_hi, B_lo)
                return hi[:, k, a:a + n], lo[:, k, a:a + n]

            def features_on_partitions(which, n_slabs, kts=KD, n=T):
                for _ in range(n_slabs):
                    slot = slab()
                    for m in range(2):
                        b = lin()
                        last = product(bank[b][:, 0:n], [(w_tile(slot, 256 * k + P * m), act_tile(which, k, 0, n))
                                                         for k in range(kts)])
                        if m == 0:
                            lin_done(last, b)
                    slab_done(last)

            def behind_split(which, ks=range(KD), waits=range(KD), n_slabs=1, stride=256):
                slots = [slab() for _ in range(n_slabs)]
                per_slab = stride // P
                banks = [lin() for _ in range(n_slabs * per_slab)]
                for k in ks:
                    if k in waits:
                        take(lo_ready)
                    for i, b in enumerate(banks):
                        lh, ll = w_tile(slots[i // per_slab], stride * k + P * (i % per_slab))
                        rh, rl = act_tile(which, k)
                        mm(bank[b][:, :], lh, rh, start=k == ks[0], stop=False, skip_group_check=True)
                        mm(bank[b][:, :], lh, rl, start=False, stop=False, skip_group_check=True)
                        last = mm(bank[b][:, :], ll, rh, start=False, stop=k == ks[-1], skip_group_check=True)
                        if k == ks[-1]:
                            if i % per_slab < per_slab - 1:
                                lin_done(last, b)
                            else:
                                tile_signal.append((slab_used, at_["slab"] - n_slabs + 1 + i // per_slab))
                                last.then_inc(slab_used, 1)

            def tokens_on_partitions(which, n_slabs, blocks, first=0, width=256):
                for _ in range(n_slabs):
                    if width == 256:
                        slot = slab()
                    else:
                        slot = (N_ADA + at_["slab"] - 1) % 2
                    for q in range(blocks):
                        b = lin()
                        last = product(bank[b][:, 0:width], [(act_tile(which, k, P * q, P),
                                                              w_tile(slot, 256 * k + first, width)) for k in range(KD)])
                        if q < blocks - 1:
                            lin_done(last, b)
                    slab_done(last)

            def norm(name):
                n = NORMS[name][1]
                b = work()
                for k in range(KD):
                    take(square_ready)
                    last = mm(bank[4 + b][:, 0:n], mean_all, S[k % 2][:, 0:n], start=k == 0, stop=k == KD - 1)
                    if k < KD - 2:
                        last.then_inc(square_used, 1)
                last.then_inc(work_ready[b], 1)

            def head_norm(name):
                tiles, n, mean, _ = HEAD_NORMS[name]
                for i in range(len(tiles)):
                    take(square_ready)
                    b = work()
                    mm(bank[4 + b][:, 0:n], mean, S[i % 2][:, 0:n], start=True, stop=True).then_inc(work_ready[b], 1)

            def attention(kind):
                a = att(kind)
                us = units(a)
                n0 = at_["turn"]
                o_bank = {}
                gate = {"signals": []}

                def scores(u):
                    h, q = us[u]
                    if kind == "fox" and q == 0:
                        b = work()
                        for j in range(QT):
                            last = mm(bank[4 + b][:, P * j:T], log_f[:, j, h:h + 1].to_broadcast([P, P]),
                                      upto[:, 0:T - P * j], start=j == 0, stop=j == QT - 1, skip_group_check=True)
                        last.then_inc(work_ready[b], 1)
                    for p in range(a["parts"]):
                        b = work()
                        w = P * (a["k1"](q) - a["k0"](q))
                        mm(bank[4 + b][:, 0:w], a["q"](h, p)[:, P * q:P * q + P],
                           a["k"](h, p)[:, P * a["k0"](q):P * a["k1"](q)], start=True, stop=True)\
                            .then_inc(work_ready[b], 1)

                def turns(u):
                    h, q = us[u]
                    take(p_ready)
                    b = turn()
                    for j in range(a["k1"](q) - a["k0"](q)):
                        last = pe.transpose(bank[6 + b][:, P * j:P * j + P], S[4 + u % 2][:, P * j:P * j + P], ident)
                    last.then_inc(turn_ready[b], 1)

                def values(u):
                    h, q = us[u]
                    pe.wait_ge(turn_free[(n0 + u) % 2], (n0 + u) // 2 + 1)
                    if q == 0:
                        o_bank[h] = lin()
                    row = a["o"](h)[0]
                    for j in range(a["k0"](q), a["k1"](q)):
                        jj = j - a["k0"](q)
                        last = mm(bank[o_bank[h]][row:row + a["m"], P * q:P * q + P], a["v"](h, j),
                                  S[6 + u % 2][:, P * jj:P * jj + P], start=jj == 0, stop=j == a["k1"](q) - 1)
                    last.then_inc(values_used, 1)
                    at_["values"] += 1
                    if kind == "diff":
                        if q == QT - 1:
                            tile_signal.append((values_used, at_["values"]))
                        return
                    per_head = KD // a["heads"]
                    for i in range(2 * per_head * q, 2 * per_head * (q + 1)):
                        m, k = per_head * h + i // KD, i % KD
                        if k == 0:
                            gate["bank"] = lin()
                            if m % 2 == 0:
                                gate["slot"] = slab()
                        to = bank[gate["bank"]][:, :]
                        (lh, ll), (rh, rl) = w_tile(gate["slot"], 256 * k + P * (m % 2)), act_tile("A", k)
                        mm(to, lh, rh, start=k == 0, stop=False, skip_group_check=True)
                        mm(to, lh, rl, start=False, stop=False, skip_group_check=True)
                        last = mm(to, ll, rh, start=False, stop=k == KD - 1, skip_group_check=True)
                        if k == KD - 1:
                            (slab_done(last) if m % 2 else lin_done(last, gate["bank"]))
                            gate["signals"].append(tile_signal.pop())
                    if q == QT - 1:
                        tile_signal.append((values_used, at_["values"]))
                        tile_signal.extend(gate["signals"])
                        gate["signals"] = []


                for u in range(len(us) + 3):
                    if u < len(us):
                        scores(u)
                    if 2 <= u <= len(us) + 1:
                        turns(u - 2)
                    if u >= 3:
                        values(u - 3)

            take(const_loaded, 16 * 3)
            norm("first")
            behind_split("A")
            stage()
            features_on_partitions("A", 3)
            tokens_on_partitions("A", 2, QT)
            features_on_partitions("A", 4)
            stage()
            stage()
            for g in range(2):
                b = work()
                for r in range(2):
                    last = mm(bank[4 + b][64 * r:64 * r + 64, :], c_("w_pool", 64 * g, 64)[64 * r:64 * r + 64, :],
                              S[g][64 * r:64 * r + 64, :], start=True, stop=True, skip_group_check=True)
                last.then_inc(work_ready[b], 1)
            stage()
            attention("diff")
            stage()
            head_norm("subln")
            behind_split("B", ks=(4, 5, 6, 7, 0, 1, 2, 3), waits=range(4))
            stage()
            features_on_partitions("B", 3)
            stage()
            norm("ffn")
            for n, g in enumerate(FFN_GROUPS):
                if n == 0:
                    behind_split("A")
                    stage()
                features_on_partitions("A", g - (n == 0))
                behind_split("B", ks=range(g))
                stage()
                features_on_partitions("B", 3, kts=g)
                stage()
            norm("final")
            stage()
            if LEVEL >= 2:
                norm("second")
                behind_split("A")
                stage()
                for br in BRANCHES:
                    features_on_partitions("A", 2 - (br == "fox"))
                    if br == "fox":
                        features_on_partitions("A", 2)
                        tokens_on_partitions("A", 2, QT)
                        for q in range(QT):
                            b = lin()
                            lin_done(product(bank[b][:, 0:HEADS], [(act_tile("A", k, P * q, P),
                                                                    (wf_hi[:, k, :], wf_lo[:, k, :]))
                                                                   for k in range(KD)]), b)
                        stage()
                        b = work()
                        for q in range(QT):
                            for j in range(q + 1):
                                last = mm(bank[4 + b][:, HEADS * q:HEADS * q + HEADS],
                                          upto[:, 0:P] if j == q else upto[:, P:2 * P], log_f[:, j, :],
                                          start=j == 0, stop=j == q)
                        last.then_inc(work_ready[b], 1)
                        head_norm("fox_q")
                        head_norm("fox_k")
                    elif br == "swa":
                        slot = slab()
                        b = lin()
                        lin_done(product(bank[b][:, :], [(w_tile(slot, 256 * k), act_tile("A", k))
                                                         for k in range(KD)]), b)
                        tokens_on_partitions("A", 1, QT, first=P, width=P)
                        stage()
                        head_norm("swa_q")
                        head_norm("swa_k")
                    else:
                        stage()
                        norm("mem")
                        stage()
                        features_on_partitions("B", 2, n=MEM)
                        tokens_on_partitions("B", 2, MEM // P)
                        stage()
                        head_norm("mem_q")
                        head_norm("mem_k")
                    stage()
                    attention(br)
                    behind_split("B", ks=range(4), n_slabs=1, stride=512)
                    stage()
                    stage()
                    slot = slab()
                    for m in range(4):
                        b = lin()
                        last = product(bank[b][:, :], [(w_tile(slot, 512 * k + P * m), act_tile("B", k))
                                                       for k in range(4)])
                        if m < 3:
                            lin_done(last, b)
                    slab_done(last)
                    stage()
                behind_split("B")
                stage()
                features_on_partitions("B", 3)
                stage()
            if LEVEL >= 3:
                norm("peer")
                behind_split("A", n_slabs=1)
                stage()
                take(act_stage)

                def u_half(s, odd, j, before=N_MID, token=None):
                    slot = (N_ADA + before + odd + (s if isinstance(s, int) else 0)) % 2
                    pe.wait_ge(slab_split, s + (odd + before + 1))
                    if not isinstance(s, int) or s + odd > 0:
                        pe.wait_ge(gelu_ready, s * 2 + (2 * odd + j - 1))
                    for k in range(KD):
                        (lh, ll), (rh, rl) = w_tile(slot, D * j + P * k), act_tile("A", k)
                        mm(bank[6 + j][:, :], lh, rh, start=k == 0, stop=False)
                        mm(bank[6 + j][:, :], lh, rl, start=False, stop=False)
                        last = mm(bank[6 + j][:, :], ll, rh, start=False, stop=k == KD - 1)
                        if k == KD - 1:
                            last.then_inc(slab_used if j else a_ready, 1)
                        if token:
                            token(k)

                def u_slabs(first, n):
                    for s in range(first, first + n):
                        for j in range(2):
                            u_half(s, 0, j)

                for h in range(HEADS):
                    if h:
                        features_on_partitions("A", 1)
                    n = at_["lin"] - 2
                    for i in range(2):
                        pe.wait_ge(lin_free[(n + i) % 4], (n + i) // 4 + 1)
                    for q in range(QT):
                        b = work()
                        for half in range(2):
                            last = mm(bank[4 + b][:, KEYS * half:KEYS * half + KEYS],
                                      peer_q[:, h % 2, half, P * q:P * q + P], keys[:, 2 * h + half, :],
                                      start=True, stop=True)
                        last.then_inc(work_ready[b], 1)
                        if q in (1, 2):
                            u_half(h, 0, q - 1, before=at_["slab"] - h)
                    at_["slab"] += 1
                u_slabs(HEADS, U_PICKS)
                stage()
                for q in range(QT):
                    b = turn()
                    for i in range(3):
                        last = pe.transpose(bank[6 + b][:, P * i:P * i + P], picks[:, q, i, :], ident)
                    last.then_inc(turn_ready[b], 1)
                stage()

                pe.drain().then_inc(hot_used, 4)
                for q in range(QT):
                    per_half = P // (2 * U_TOKENS)
                    first = U_AT + (U_TOKENS + U_STORE) * q
                    with pe.Fori(0, U_TOKENS - 1, 2) as s:
                        t = s * (2 * per_half)
                        for half in range(4):
                            def token(k):
                                j = per_half * half + k
                                if j % 4 == 0:
                                    pe.wait_ge(g_copied, t + (P * q + j + 4))
                                pe.wait_ge(hot_ready, t + (P * q + j + 1))
                                mm(bank[4 + j // 4 % 2][:, P * (j % 4):P * (j % 4) + P], hot[:, j % 4, 0, :],
                                   hot[:, j % 4, 1, :], start=True, stop=True).then_inc(hot_used, 1)

                            u_half(s, first + half // 2, half % 2, token=token)
                    u_slabs(first + U_TOKENS, U_STORE)

                def outputs_of(s, odd, first=False, final=False):
                    slot = (N_ADA + N_MID + PAIRS + odd) % 2
                    pe.wait_ge(slab_split, s + (odd + N_MID + PAIRS + 1))
                    pe.wait_ge(act_lo_ready, s + (odd + 1))
                    for j in range(2):
                        for m in range(KD):
                            lh, ll = w_tile(slot, D * j + P * m)
                            rh, rl = act_tile("B", 4 + 2 * odd + j)
                            mm(bank[m][:, :], lh, rh, start=first and j == 0, stop=False, skip_group_check=True)
                            mm(bank[m][:, :], lh, rl, start=False, stop=False, skip_group_check=True)
                            last = mm(bank[m][:, :], ll, rh, start=False, stop=final and j == 1, skip_group_check=True)
                    last.then_inc(slab_used, 1)

                pe.wait_ge(g_copied, T + 8)
                pe.wait_ge(gelu_ready, KEYS)
                outputs_of(0, 0, first=True)
                outputs_of(0, 1)
                with pe.Fori(2, PAIRS - 3, 2) as s:
                    for odd in range(2):
                        outputs_of(s, odd)
                outputs_of(PAIRS - 2, 0)
                outputs_of(PAIRS - 2, 1, final=True)

        @block.scalar
        def _(act):
            take = Taken(act).take
            at_ = {"tile": 0, "work": 0, "turn": 0, "values": 0}
            own = [0]

            def step(ins):
                own[0] += 1
                ins.then_inc(act_step, 1)
                act.wait_ge(act_step, own[0])

            def stage_end():
                act.drain().then_inc(act_stage, 1)
                take(dve_stage)

            def load(to, name):
                a, b = TABLE_AT[name]
                act.dma_start(to, tables_in[:, a:b]).then_inc(table_loaded, 16)
                loads[0] += 1

            loads = [0]

            def loaded():
                act.wait_ge(table_loaded, 16 * loads[0])

            def tile(read, skip=0):
                n = at_["tile"]
                at_["tile"] += 1
                act.wait_ge(*tile_signal[n])
                read(bank[n % 4]).then_inc(lin_free[n % 4], 1)

            def copy_to(to, width=T, scale=1.0):
                tile(lambda b: act.activation(to, b[:, 0:width], ACT.Copy, scale=scale))

            def skip(n):
                at_["tile"] += n

            def root(n, to):
                w = at_["work"]
                at_["work"] += 1
                act.wait_ge(work_ready[w % 2], w // 2 + 1)
                act.activation(to[:, 0:n], bank[4 + w % 2][:, 0:n], ACT.Ln, bias=small[:, 0:1])\
                    .then_inc(work_free[w % 2], 1)
                act.wait_ge(work_free[w % 2], w // 2 + 1)
                act.activation(to[:, 0:n], to[:, 0:n], ACT.Exp, scale=-0.5).then_inc(root_ready, 1)

            def norm(name, before=None):
                src, n, _, _, to = NORMS[name]
                for k in range(KD):
                    if k >= 2:
                        take(square_used)
                    act.activation(S[k % 2][:, 0:n], src[:, k, :], ACT.Square).then_inc(square_ready, 1)
                root(n, S[2])
                if before:
                    before()
                if to:
                    split(8, lambda k: S[3 + k % 2][:, 0:n], to, n=n)

            def split(tiles, source, to, first=0, n=T):
                for k in range(tiles):
                    take(whole_ready)
                    act.activation((A_hi if to == "A" else B_hi)[:, first + k, 0:n], source(k), ACT.Copy)\
                        .then_inc(hi_ready, 1)

            def head_norm(name):
                tiles, n, _, _ = HEAD_NORMS[name]
                for i in range(len(tiles) + 1):
                    if i < len(tiles):
                        act.activation(S[i % 2][:, 0:n], tiles[i], ACT.Square).then_inc(square_ready, 1)
                    if i >= 1:
                        if i >= 3:
                            take(normed)
                        root(n, S[2 + (i - 1) % 2])
                for _ in range(min(2, len(tiles))):
                    take(normed)

            def attention(kind):
                a = att(kind)
                us = units(a)
                p_slots = P_SLOTS[kind]
                base = (take_count(exp_ready), take_count(p_ready))
                v0 = at_["values"]
                i = 0
                per_head = KD // a["heads"]
                for u in range(len(us) + 3):
                    if u < len(us):
                        h, q = us[u]
                        w = P * (a["k1"](q) - a["k0"](q))
                        for p in range(a["parts"]):
                            take(top_ready)
                            if u * a["parts"] >= len(p_slots):
                                act.wait_ge(p_ready, base[1] + u + 1 - len(p_slots) // a["parts"])
                            if kind == "swa":
                                act.activation(small[:, 32 + i % 4:33 + i % 4], c_("sinks", h), ACT.Exp,
                                               bias=small[:, 24 + i % 2:25 + i % 2])
                            act.activation(p_slots[i % len(p_slots)][:, 0:w], S[i % 2][:, 0:w], ACT.Exp,
                                           bias=small[:, 24 + i % 2:25 + i % 2],
                                           accum_out=small[:, 28 + i % 4:29 + i % 4]).then_inc(exp_ready, 1)
                            i += 1
                    if 1 <= u <= len(us):
                        h, q = us[u - 1]
                        w = P * (a["k1"](q) - a["k0"](q))
                        n = at_["turn"]
                        at_["turn"] += 1
                        act.wait_ge(turn_ready[n % 2], n // 2 + 1)
                        if u - 1 >= 2:
                            act.wait_ge(values_used, v0 + u - 2)
                        act.activation(S[6 + (u - 1) % 2][:, 0:w], bank[6 + n % 2][:, 0:w], ACT.Copy)\
                            .then_inc(turn_free[n % 2], 1)
                    if kind != "diff" and u >= 3 and us[u - 3][1] == QT - 1:
                        for m in range(per_head * us[u - 3][0], per_head * (us[u - 3][0] + 1)):
                            tile(lambda b: act.activation(gate_t[m], b[:, :], ACT.Copy))
                    if 2 <= u <= len(us) + 1 and us[u - 2][1] == QT - 1:
                        row, i_o, o = a["o"](us[u - 2][0])
                        tile(lambda b: act.activation(o[row:row + a["m"], i_o, :], b[row:row + a["m"], :], ACT.Copy))
                    if kind == "diff" and u % 2 and u < len(us):
                        modulation(ADA_FIRST + u // 2)
                at_["values"] += len(us)
                counted[exp_ready.name] += i
                counted[p_ready.name] += len(us)
                at_["work"] += len(us) * a["parts"] + (HEADS if kind == "fox" else 0)

            counted = {exp_ready.name: 0, p_ready.name: 0}

            def take_count(s):
                return counted[s.name]

            def modulation(s):
                act.wait_ge(ada_times_c, s + 1)
                for m in range(2):
                    w = (ada_place(s) if s < ADA_FIRST else raw[:, s % 2, :])[:, D * m:D * m + D]
                    ins = act.activation(w, w, ACT.Copy, accum_out=mod[:, 2 * s + m:2 * s + m + 1])
                ins.then_inc(ada_used, 1)

            def silu_of_c(n):
                act.dma_start(c_row, cols_in[:, N_COLS:N_COLS + D]).then_inc(c_loaded, 16)
                act.wait_ge(c_loaded, 16 * n)
                act.activation(c_row, c_row, ACT.Silu).then_inc(c_ready, 1)

            silu_of_c(1)
            act.dma_start(col[:, :], cols_in[:, 0:N_COLS]).then_inc(const_loaded, 16)
            act.dma_start(tab[:, :], tables_in[:, 0:512]).then_inc(const_loaded, 16)
            act.wait_ge(const_loaded, 16 * 3)
            take(small_ready)
            act.activation(small[:, 4:6], small[:, 2:4], ACT.Exp).then_inc(small_done, 1)
            act.activation(wf_hi[:, :, :], c_("w_forget", 0, 64).rearrange("p (k h) -> p k h", k=KD), ACT.Copy)\
                .then_inc(small_done, 1)
            norm("first", lambda: [modulation(s) for s in range(ADA_FIRST)])
            stage_end()

            load(dist, "distance")
            load(recip_cnt_both, "pool_recip")
            for i in range(4):
                copy_to(Qt[:, i, :], scale=32 ** -0.5)
            for i in range(4):
                copy_to(Kt[:, i, :])
            for c in range(2):
                for q in range(QT):
                    copy_to(V[:, q, 256 * c:256 * c + 256], width=256)
            for i in range(2):
                copy_to(pool_in[:, i, 8:8 + T])
            for i in range(2):
                copy_to(c_gate_t[:, i, :])
            skip(2)
            for i in range(2):
                copy_to(b_gate_t[:, i, :])
            loaded()
            stage_end()

            split(2, lambda i: S[4 + i], "B", first=6)
            stage_end()
            silu_of_c(2)
            at_["work"] += 2
            split(2, lambda i: S[2 + i], "B", first=4)
            stage_end()
            attention("diff")
            stage_end()
            head_norm("subln")
            split(4, lambda i: Ot[:, i, :], "B")
            stage_end()
            skip(8)
            stage_end()
            norm("ffn")
            stage_end()
            for g in FFN_GROUPS:
                for i in range(g):
                    tile(lambda b: act.activation(S[i % 2], b[:, :], ACT.Silu))
                    take(whole_ready)
                    skip(1)
                    act.activation(B_hi[:, i, :], S[2 + i % 2], ACT.Copy).then_inc(hi_ready, 1)
                stage_end()
                skip(8)
                stage_end()
            norm("final")
            stage_end()
            if LEVEL >= 2:
                load(upto, "upto")
                load(causal, "causal")
                norm("second")
                stage_end()
                for n_br, br in enumerate(BRANCHES):
                    for i in range(4):
                        copy_to(Qt[:, i, :])
                    if br == "fox":
                        for i in range(4):
                            copy_to(Kt[:, i, :])
                        for c in range(2):
                            for q in range(QT):
                                copy_to(V[:, q, 256 * c:256 * c + 256], width=256)
                        skip(QT)
                        take(small_ready)
                        step(act.activation(S[1][:, 0:32], S[0][:, 0:32], ACT.Exp))
                        act.activation(S[2][:, 0:32], S[1][:, 0:32], ACT.Ln, bias=small[:, 1:2]).then_inc(small_done, 1)
                        loaded()
                        stage_end()
                        at_["work"] += 1
                        head_norm("fox_q")
                        head_norm("fox_k")
                    elif br == "swa":
                        load(swa_nd, "swa_distance")
                        load(swa_mask, "swa_mask")
                        copy_to(Kt[:, 0, :])
                        for q in range(QT):
                            copy_to(V[:, q, 0:P], width=P)
                        loaded()
                        stage_end()
                        head_norm("swa_q")
                        head_norm("swa_k")
                    else:
                        act.dma_start(mem_t, mem_in.rearrange("(k p) t -> p k t", p=P)).then_inc(table_loaded, 16)
                        loads[0] += 1
                        loaded()
                        stage_end()
                        norm("mem")
                        stage_end()
                        for i in range(4):
                            copy_to(mem_kt[:, i, :], width=MEM)
                        for c in range(2):
                            for q in range(MEM // P):
                                copy_to(mem_v[:, q, 256 * c:256 * c + 256], width=256)
                        stage_end()
                        head_norm("mem_q")
                        head_norm("mem_k")
                    stage_end()
                    attention(br)
                    stage_end()
                    o = mem_o if br == "mem" else Ot
                    split(4, lambda i: o[:, i, :], "B")
                    stage_end()
                    for i in range(KD):
                        act.activation(gate_t[i], gate_t[i], ACT.Sigmoid, bias=c_("b_gate", KD * n_br + i))\
                            .then_inc(gate_ready, 1)
                    skip(KD)
                    stage_end()
                split(8, lambda k: merged[:, k, :], "B")
                stage_end()
                skip(8)
                stage_end()
            if LEVEL >= 3:
                norm("peer")
                act.drain().then_inc(act_stage, 1)
                take(dve_stage)
                act.dma_start(keys.rearrange("p i k -> p (i k)"), keys_in).then_inc(table_loaded, 16)
                loads[0] += 1
                load(iota16, "iota16")
                load(iota, "iota")
                loaded()
                act.drain().then_inc(act_stage, 1)

                def gelus(s, odd=0, tokens=None):
                    p = (s + odd) % 2 if isinstance(s, int) else odd % 2
                    out_ = gelu_out[:, 2 * p:2 * p + 2, :]
                    for j in range(2):
                        if tokens:
                            tokens(j)
                        if j == 0:
                            act.wait_ge(a_ready, s + (odd + 1))
                            if not isinstance(s, int) or s >= 2:
                                act.wait_ge(gelu_stored[p], s * 8 + (odd - p) * 8)
                        else:
                            n = 2 * s + 2 + N_MID - HEADS if isinstance(s, int) and s < HEADS else s + (odd + 1 + N_MID)
                            act.wait_ge(slab_used, n)
                        act.activation(out_[:, j, :], bank[6 + j][:, :], ACT.Gelu).then_inc(gelu_ready, 1)
                    act.wait_ge(gelu_ready, s * 2 + (2 * odd + 2))
                    act.dma_start(gelu_dram[s + odd, :, :], out_.rearrange("p j t -> p (j t)"))\
                        .then_inc(gelu_stored[p], 16)

                w = at_["work"]
                for h in range(HEADS):
                    if h >= 2:
                        n = w + QT * (h - 1) - 1
                        act.wait_ge(work_ready[n % 2], n // 2 + 1)
                    for half in range(2):
                        copy_to(peer_q[:, h % 2, half, :])
                    gelus(h)
                at_["work"] += QT * HEADS
                take(small_ready)
                act.activation(eq[:, 512:1024], eq[:, 0:512], ACT.Exp).then_inc(small_done, 1)
                for s in range(HEADS, HEADS + U_PICKS):
                    gelus(s)
                stage_end()
                for q in range(QT):
                    n = at_["turn"]
                    at_["turn"] += 1
                    act.wait_ge(turn_ready[n % 2], n // 2 + 1)
                    act.activation(picks_t[:, :, P * q:P * q + P],
                                   bank[6 + n % 2][:, 0:3 * P].rearrange("p (i t) -> p i t", i=3), ACT.Copy)\
                        .then_inc(turn_free[n % 2], 1)
                stage_end()
                act.drain().then_inc(g_copied, 8)
                for q in range(QT):
                    per_half = P // (2 * U_TOKENS)
                    first = U_AT + (U_TOKENS + U_STORE) * q
                    with act.Fori(0, U_TOKENS - 1, 2) as s:
                        t = s * (2 * per_half)

                        def tokens(half):
                            for i in range(per_half // 4):
                                j = per_half * half + 4 * i
                                act.wait_ge(hot_used, t + (P * q + j + 8))
                                act.activation(g_stage[:, :, bass.ds(t + j, 4)],
                                               bank[4 + j // 4 % 2][:, :].rearrange("p (t e) -> p e t", t=4), ACT.Copy)\
                                    .then_inc(g_copied, 4)

                        for odd in range(2):
                            gelus(s, first + odd, lambda j: tokens(2 * odd + j))
                    act.wait_ge(g_copied, 8 + P * (q + 1))
                    act.dma_start(g_dram[q, :, :, :], g_stage).then_inc(g_stored, 16)
                    for s in range(first + U_TOKENS, first + U_TOKENS + U_STORE):
                        gelus(s)
                    act.wait_ge(g_stored, 16 * (q + 1))

                def operand(s, j):
                    act.wait_ge(act_ready, s + (j + 1))
                    if not isinstance(s, int):
                        act.wait_ge(slab_used, s + (j + N_MID + PAIRS - 1))
                    act.activation(B_hi[:, 4 + 2 * j:6 + 2 * j, :], prod[:, j, :].rearrange("p (i t) -> p i t", i=2),
                                   ACT.Copy).then_inc(act_hi_ready, 1)

                for j in range(2):
                    operand(0, j)
                with act.Fori(2, PAIRS - 1, 2) as s:
                    for j in range(2):
                        operand(s, j)

        @block.vector
        def _(dve):
            take = Taken(dve).take
            at_ = {"tile": 0, "work": 0, "turn": 0, "exp": 0}
            own = [0]

            def step(ins):
                own[0] += 1
                ins.then_inc(dve_step, 1)
                dve.wait_ge(dve_step, own[0])

            def stage_end():
                dve.drain().then_inc(dve_stage, 1)
                take(act_stage)

            def tile(read):
                n = at_["tile"]
                at_["tile"] += 1
                dve.wait_ge(*tile_signal[n])
                read(bank[n % 4]).then_inc(lin_free[n % 4], 1)

            def skip(n):
                at_["tile"] += n

            def work(own_=True):
                w = at_["work"]
                at_["work"] += 1
                dve.wait_ge(work_ready[w % 2], w // 2 + 1)
                return w % 2, w // 2 + 1

            def rest(k, source, to, first, n=T, followed=True):
                take(hi_ready)
                hi, lo = (A_hi, A_lo) if to == "A" else (B_hi, B_lo)
                ins = dve.tensor_tensor(lo[:, first + k, 0:n], source, hi[:, first + k, 0:n].bitcast(F32), ALU.subtract)
                if followed:
                    ins.then_inc(lo_ready, 1)
                    take(lo_ready)
                else:
                    step(ins)

            def norm(name, before=None):
                src, n, gain, shift, to = NORMS[name]
                at_["work"] += 1
                take(root_ready)
                if before:
                    before()
                for k in range(KD + 1):
                    if k < KD:
                        y = S[3 + k % 2][:, 0:n] if to else src[:, k, :]
                        ins = dve.scalar_tensor_tensor(out=y, in0=src[:, k, :], scalar=gain(k), in1=S[2][:, 0:n],
                                                       op0=ALU.mult, op1=ALU.mult)
                        if shift:
                            step(ins)
                            ins = dve.tensor_scalar(y, y, shift(k), None, ALU.add)
                        if to:
                            ins.then_inc(whole_ready, 1)
                    if to and k >= 1:
                        rest(k - 1, S[3 + (k - 1) % 2][:, 0:n], to, 0, n, name != "mem")

            def split(tiles, source, to, first=0, followed=True):
                for k in range(tiles):
                    rest(k, source(k), to, first, followed=followed)

            def head_norm(name):
                tiles, n, _, gain = HEAD_NORMS[name]
                for i, t in enumerate(tiles):
                    r = S[2 + i % 2]
                    at_["work"] += 1
                    take(root_ready)
                    dve.scalar_tensor_tensor(out=t, in0=t, scalar=gain(i), in1=r[:, 0:n], op0=ALU.mult, op1=ALU.mult)\
                        .then_inc(normed, 1)

            def attention(kind):
                a = att(kind)
                us = units(a)
                p_slots = P_SLOTS[kind]
                n0, e0 = at_["turn"], at_["exp"]
                i = 0

                def logits(u):
                    nonlocal i
                    h, q = us[u]
                    w = P * (a["k1"](q) - a["k0"](q))
                    if q == 0 and kind == "fox":
                        b, n = work()
                        dve.tensor_copy(ck[:, h % 2, :], bank[4 + b][:, :]).then_inc(work_free[b], 1)
                        dve.wait_ge(work_free[b], n)
                    if q == 0 and kind == "swa":
                        step(dve.scalar_tensor_tensor(out=swa_bias[:, h % 2, :], in0=swa_nd, scalar=2.0 ** -(h + 1),
                                                      in1=swa_mask, op0=ALU.mult, op1=ALU.add))
                    for p in range(a["parts"]):
                        L = S[i % 2][:, 0:w]
                        top = small[:, 24 + i % 2:25 + i % 2]
                        b, n = work()
                        s = bank[4 + b][:, 0:w]
                        if i >= 2:
                            dve.wait_ge(exp_ready, e0 + i - 1)
                        if kind == "diff":
                            ins = dve.scalar_tensor_tensor(out=L, in0=dist[:, 384 - P * q:384 - P * q + T],
                                                           scalar=-(2.0 ** -(h + 1)), in1=s, op0=ALU.mult, op1=ALU.add)
                        elif kind == "fox":
                            ins = dve.scalar_tensor_tensor(out=L, in0=s, scalar=cq[:, q, h:h + 1],
                                                           in1=ck[:, h % 2, 0:w], op0=ALU.add, op1=ALU.subtract)
                        elif kind == "swa":
                            ins = dve.tensor_tensor(L, s, swa_bias[:, h % 2, 256 - w:256], ALU.add)
                        else:
                            ins = dve.tensor_copy(L, s)
                        ins.then_inc(work_free[b], 1)
                        dve.wait_ge(work_free[b], n)
                        if kind == "fox":
                            step(dve.tensor_tensor(L[:, w - P:w], L[:, w - P:w], causal, ALU.add))
                        if kind == "swa":
                            step(dve.tensor_reduce(small[:, 26 + i % 2:27 + i % 2], L, AX, ALU.max))
                            dve.tensor_scalar(top, small[:, 26 + i % 2:27 + i % 2], c_("sinks", h), -1.0, ALU.max, ALU.mult)\
                                .then_inc(top_ready, 1)
                        else:
                            dve.tensor_reduce(top, L, AX, ALU.max, negate=True).then_inc(top_ready, 1)
                        i += 1

                def normalise(u):
                    h, q = us[u]
                    w = P * (a["k1"](q) - a["k0"](q))
                    parts = a["parts"]
                    j = parts * u
                    dve.wait_ge(exp_ready, e0 + j + parts)
                    if u >= 2:
                        n = n0 + u - 2
                        dve.wait_ge(turn_ready[n % 2], n // 2 + 1)
                    sums = small[:, 28 + j % 4:28 + j % 4 + parts]
                    inv = small[:, 36 + 2 * (u % 2):36 + 2 * (u % 2) + parts]
                    if kind == "swa":
                        step(dve.tensor_tensor(sums, sums, small[:, 32 + j % 4:33 + j % 4], ALU.add))
                    step(dve.reciprocal(inv, sums))
                    p0 = p_slots[j % len(p_slots)]
                    if kind == "diff":
                        p1 = p_slots[(j + 1) % len(p_slots)]
                        step(dve.tensor_scalar(p1, p1, inv[:, 1:2], small[:, 6:7], ALU.mult, ALU.mult))
                        dve.scalar_tensor_tensor(out=S[4 + u % 2], in0=p0, scalar=inv[:, 0:1], in1=p1,
                                                 op0=ALU.mult, op1=ALU.add).then_inc(p_ready, 1)
                    else:
                        dve.tensor_scalar(S[4 + u % 2][:, 0:w], p0[:, 0:w], inv, None, ALU.mult).then_inc(p_ready, 1)

                for u in range(len(us) + 1):
                    if u < len(us):
                        logits(u)
                    if u >= 1:
                        normalise(u - 1)
                at_["turn"] += len(us)
                at_["exp"] += len(us) * a["parts"]
                skip(a["heads"] if kind == "diff" else a["heads"] + KD)

            step(dve.memset(small[:, :], 0.0))
            dve.memset(small[:, 0:1], EPS)
            dve.memset(small[:, 1:2], 1.0)
            take(const_loaded, 16 * 3)
            lam = c_("lambda", 0, 128)
            for i in range(2):
                step(dve.tensor_tensor(S[5][:, 32 * i:32 * i + 32], lam[:, 64 * i:64 * i + 32],
                                       lam[:, 64 * i + 32:64 * i + 64], ALU.mult))
            dve.tensor_reduce(small[:, 2:4], S[5][:, 0:64].rearrange("p (i n) -> p i n", i=2), AX, ALU.add)\
                .then_inc(small_ready, 1)
            dve.tensor_scalar(small[:, 8:12], c_("g_subln", 0, 4), 1.0 - LAMBDA_INIT, None, ALU.mult)
            dve.tensor_scalar(small[:, 16:17], c_("g_fox_q"), HD ** -0.5, None, ALU.mult)
            dve.tensor_scalar(small[:, 17:18], c_("g_swa_q"), HD ** -0.5, None, ALU.mult)
            dve.tensor_scalar(small[:, 18:19], c_("g_mem_q"), P ** -0.5, None, ALU.mult)
            take(small_done, 2)
            step(dve.tensor_tensor(small[:, 7:8], small[:, 5:6], small[:, 4:5], ALU.subtract))
            dve.tensor_scalar(small[:, 6:7], small[:, 7:8], -LAMBDA_INIT, None, ALU.add)
            dve.tensor_tensor(wf_lo[:, :, :], c_("w_forget", 0, 64).rearrange("p (k h) -> p k h", k=KD),
                              wf_hi[:, :, :].bitcast(F32), ALU.subtract)

            def gain(i, g):
                a = 8 + 24 * i
                return dve.scalar_tensor_tensor(out=gs[:, i, :], in0=mod[:, a:a + 8], scalar=1.0, in1=c_(g, 0, 8),
                                                op0=ALU.add, op1=ALU.mult)

            dve.wait_ge(c_ready, 1)
            for s in range(ADA_FIRST):
                if 2 <= s < 6:
                    dve.wait_ge(ada_loaded[s - 2], 16)
                else:
                    dve.wait_ge(slab_loaded[s % 2], 16 if s < 2 else 32)
                w = ada_rows(ada_place(s))
                dve.tensor_tensor(w, w, c_rows, ALU.mult).then_inc(ada_times_c, 1)

            def first_modulation():
                take(ada_used, ADA_FIRST)
                n = 2 * ADA_FIRST
                step(dve.tensor_tensor(mod[:, 0:n], mod[:, 0:n], c_("b_ada", 0, n), ALU.add))
                step(gain(0, "g_mix"))

            norm("first", first_modulation)
            stage_end()

            for i in range(2):
                dve.memset(pool_in[:, i, 0:8], 0.0)
                dve.memset(pool_in[:, i, 8 + T:16 + T], 0.0)
                dve.memset(conv_in[:, i, 0:1], 0.0)
                dve.memset(conv_in[:, i, 1 + T:2 + T], 0.0)
            skip(4 + 4 + 8 + 2)
            n = at_["tile"]
            skip(2)
            for i in range(2):
                dve.wait_ge(lin_free[(n + i) % 4], (n + i) // 4 + 1)
                tile(lambda b: dve.tensor_tensor(conv_in[:, i, 1:1 + T], c_gate_t[:, i, :], b[:, :], ALU.mult))
            skip(2)
            stage_end()

            for i in range(2):
                w = [c_("conv", 2 * k + i) for k in range(3)]
                y = S[4 + i]
                step(dve.tensor_scalar(y, conv_in[:, i, 0:T], w[0], None, ALU.mult))
                step(dve.scalar_tensor_tensor(out=y, in0=conv_in[:, i, 1:1 + T], scalar=w[1], in1=y,
                                              op0=ALU.mult, op1=ALU.add))
                step(dve.scalar_tensor_tensor(out=y, in0=conv_in[:, i, 2:2 + T], scalar=w[2], in1=y,
                                              op0=ALU.mult, op1=ALU.add))
                dve.tensor_tensor(y, y, b_gate_t[:, i, :], ALU.mult).then_inc(whole_ready, 1)
            split(2, lambda i: S[4 + i], "B", first=6, followed=False)
            for g in range(2):
                u = pool_in[:, g, :]
                a, b = pool_sum[:, 0, :], pool_sum[:, 1, :]
                step(dve.tensor_tensor(a[:, 1:528], u[:, 0:527], u[:, 1:528], ALU.add))
                step(dve.tensor_tensor(b[:, 2:527], a[:, 1:526], a[:, 3:528], ALU.add))
                if g:
                    step(dve.tensor_tensor(a[:, 4:525], b[:, 2:523], b[:, 6:527], ALU.add))
                    step(dve.tensor_tensor(b[:, 8:521], a[:, 4:517], a[:, 12:525], ALU.add))
                for r, sums in ((0, a), (1, b)):
                    rows = slice(64 * r, 64 * r + 64)
                    step(dve.tensor_tensor(S[g][rows, :], sums[rows, 8:8 + T], recip_cnt[g][rows, :], ALU.mult))
                    step(dve.tensor_tensor(S[g][rows, :], S[g][rows, :], u[rows, 8:8 + T], ALU.subtract))
            stage_end()

            for g in range(2):
                b, n = work()
                dve.tensor_scalar(S[2 + g], bank[4 + b][:, :], c_("pool_scale", g), None, ALU.mult)\
                    .then_inc(work_free[b], 1)
                dve.wait_ge(work_free[b], n)
                dve.drain().then_inc(whole_ready, 1)
            split(2, lambda i: S[2 + i], "B", first=4, followed=False)
            stage_end()
            attention("diff")
            take(ada_used, N_ADA - ADA_FIRST)
            n = 2 * ADA_FIRST
            step(dve.tensor_tensor(mod[:, n:48], mod[:, n:48], c_("b_ada", n, 48 - n), ALU.add))
            gain(1, "g_ffn")
            stage_end()
            head_norm("subln")
            for i in range(4):
                dve.drain().then_inc(whole_ready, 1)
            split(4, lambda i: Ot[:, i, :], "B")
            stage_end()

            def residual(gate=None):
                for m in range(KD):
                    if gate is None:
                        tile(lambda b: dve.tensor_tensor(X[:, m, :], b[:, :], X[:, m, :], ALU.add))
                    else:
                        tile(lambda b: dve.scalar_tensor_tensor(out=X[:, m, :], in0=b[:, :],
                                                                scalar=mod[:, gate + m:gate + m + 1],
                                                                in1=X[:, m, :], op0=ALU.mult, op1=ALU.add))

            residual(16)
            stage_end()
            norm("ffn")
            stage_end()
            for g in FFN_GROUPS:
                for i in range(g):
                    n = at_["tile"]
                    dve.wait_ge(lin_free[n % 4], n // 4 + 1)
                    skip(1)
                    tile(lambda b: dve.tensor_tensor(S[2 + i % 2], S[i % 2], b[:, :], ALU.mult))
                    dve.wait_ge(lin_free[(n + 1) % 4], (n + 1) // 4 + 1)
                    dve.drain().then_inc(whole_ready, 1)
                    rest(i, S[2 + i % 2], "B", 0)
                stage_end()
                residual(40)
                stage_end()
            norm("final")
            stage_end()
            if LEVEL >= 2:
                norm("second")
                stage_end()
                for br in BRANCHES:
                    skip(4)
                    if br == "fox":
                        skip(4 + 8)
                        x = S[3][:, 0:32]
                        for q in range(QT):
                            tile(lambda b: dve.tensor_tensor(x[:, HEADS * q:HEADS * q + HEADS], b[:, 0:HEADS],
                                                             c_("b_forget", 0, 8), ALU.add))
                        dve.wait_ge(lin_free[(at_["tile"] - 1) % 4], (at_["tile"] - 1) // 4 + 1)
                        dve.scalar_tensor_tensor(out=S[0][:, 0:32], in0=x, scalar=-1.0, in1=x,
                                                 op0=ALU.mult, op1=ALU.min).then_inc(small_ready, 1)
                        take(small_done)
                        dve.scalar_tensor_tensor(out=log_f.rearrange("p q h -> p (q h)"), in0=x, scalar=0.0,
                                                 in1=S[2][:, 0:32], op0=ALU.min, op1=ALU.subtract)
                        stage_end()
                        b, n = work()
                        dve.tensor_copy(cq.rearrange("p q h -> p (q h)"), bank[4 + b][:, 0:32])\
                            .then_inc(work_free[b], 1)
                        head_norm("fox_q")
                        head_norm("fox_k")
                    elif br == "swa":
                        skip(1 + QT)
                        stage_end()
                        head_norm("swa_q")
                        head_norm("swa_k")
                    else:
                        stage_end()
                        norm("mem")
                        stage_end()
                        skip(4 + 4)
                        stage_end()
                        head_norm("mem_q")
                        head_norm("mem_k")
                    stage_end()
                    attention(br)
                    stage_end()
                    o = mem_o if br == "mem" else Ot
                    for i in range(4):
                        dve.drain().then_inc(whole_ready, 1)
                    split(4, lambda i: o[:, i, :], "B")
                    stage_end()
                    for i in range(KD):
                        take(gate_ready)
                        n = at_["tile"]
                        if br == "fox":
                            tile(lambda b: dve.tensor_tensor(merged[:, i, :], gate_t[i], b[:, :], ALU.mult))
                        else:
                            tile(lambda b: dve.tensor_tensor(S[2], gate_t[i], b[:, :], ALU.mult))
                            dve.wait_ge(lin_free[n % 4], n // 4 + 1)
                            step(dve.tensor_tensor(merged[:, i, :], merged[:, i, :], S[2], ALU.add))
                    stage_end()
                for i in range(KD):
                    dve.drain().then_inc(whole_ready, 1)
                split(8, lambda k: merged[:, k, :], "B")
                stage_end()
                residual()
                stage_end()
            if LEVEL >= 3:
                norm("peer")
                dve.drain().then_inc(dve_stage, 1)
                take(act_stage, 2)

                def top16(sources, values, indices, rests, free=None):
                    for s, v in zip(sources, values):
                        ins = dve.max(v[:, 0:8], s)
                    step(ins)
                    for s, v, i in zip(sources, values, indices):
                        dve.max_index(i[:, 0:8], v[:, 0:8], s)
                    for s, v, r in zip(sources, values, rests):
                        ins = dve.match_replace(r, v[:, 0:8], s, -3.0e38)
                    if free:
                        ins.then_inc(free[0], 1)
                        dve.wait_ge(*free)
                    else:
                        step(ins)
                    for v, r in zip(values, rests):
                        ins = dve.max(v[:, 8:16], r)
                    step(ins)
                    for v, i, r in zip(values, indices, rests):
                        ins = dve.max_index(i[:, 8:16], v[:, 8:16], r)

                top_iu, sum_iu = top_i.bitcast(U32), sum_i.bitcast(U32)
                for h in range(HEADS):
                    skip(2)
                    for q in range(QT):
                        b, n = work()
                        c = cand[:, q % 2, :]
                        top16([bank[4 + b][:, KEYS * i:KEYS * i + KEYS] for i in range(2)],
                              [top_v[:, q, h, TOPK * i:TOPK * i + TOPK] for i in range(2)],
                              [top_iu[:, q, h, TOPK * i:TOPK * i + TOPK] for i in range(2)],
                              [rest_a[:, i, :] for i in range(2)], free=(work_free[b], n))
                        v = top_v[:, q, h, :]
                        step(dve.tensor_tensor(c.rearrange("p (i j) -> p i j", i=TOPK),
                                               v[:, 0:TOPK].unsqueeze(2).to_broadcast([P, TOPK, TOPK]),
                                               v[:, TOPK:2 * TOPK].unsqueeze(1).to_broadcast([P, TOPK, TOPK]),
                                               ALU.add))
                        top16([c], [sum_v[:, q, h, :]], [sum_iu[:, q, h, :]], [cand_rest])
                d = eq[:, 0:512].rearrange("p (g s) -> p g s", s=TOPK)
                ex = eq[:, 512:1024].rearrange("p (g s) -> p g s", s=TOPK)
                sv = sum_v.rearrange("p q h s -> p (q h) s")
                dve.tensor_tensor(d, sv, sv[:, :, 0:1].to_broadcast([P, QT * HEADS, TOPK]), ALU.subtract)\
                    .then_inc(small_ready, 1)
                take(small_done)
                gsum = eq[:, 1024:1024 + QT * HEADS]
                step(dve.tensor_reduce(gsum, ex, AX, ALU.add))
                step(dve.reciprocal(gsum, gsum))
                step(dve.tensor_tensor(picks[:, :, 2, :].rearrange("p q (h s) -> p q h s", h=HEADS),
                                       ex.rearrange("p (q h) s -> p q h s", q=QT),
                                       gsum.rearrange("p (q h) -> p q h", q=QT).unsqueeze(3)
                                       .to_broadcast([P, QT, HEADS, TOPK]), ALU.mult))
                iwu = iw.bitcast(U32)
                eq3 = eq.rearrange("p (s j) -> p s j", j=TOPK)
                eq4 = eq.rearrange("p (h s j) -> p h s j", h=HEADS, j=TOPK)
                for q in range(QT):
                    si = sum_iu[:, q, :, :].rearrange("p h s -> p (h s)")
                    dve.tensor_scalar(iwu[:, 0, :], si, 4, None, ALU.logical_shift_right)
                    dve.tensor_scalar(iwu[:, 1, :], si, 15, None, ALU.bitwise_and)
                    step(dve.tensor_copy(top_f, top_iu[:, q, :, :]))
                    dve.tensor_copy(sel_hi, iwu[:, 0, :])
                    step(dve.tensor_copy(sel_lo, iwu[:, 1, :]))
                    for i, sel in enumerate((sel_hi, sel_lo)):
                        step(dve.tensor_tensor(eq3, sel.unsqueeze(2).to_broadcast([P, P, TOPK]),
                                               iota16.unsqueeze(1).to_broadcast([P, P, TOPK]), ALU.is_equal))
                        step(dve.tensor_tensor(eq4, eq4, top_f[:, :, TOPK * i:TOPK * i + TOPK].unsqueeze(2)
                                               .to_broadcast([P, HEADS, TOPK, TOPK]), ALU.mult))
                        step(dve.tensor_reduce(picks[:, q, i, :], eq3, AX, ALU.add))
                stage_end()
                stage_end()
                with dve.Fori(0, T - 3, 4) as t:
                    for j in range(4):
                        dve.wait_ge(hot_used, t + (j + 1))
                        dve.tensor_scalar(hot[:, j, 0, :], iota, picks_t[:, 0, bass.ds(t + j, 1)], None, ALU.is_equal)
                        dve.tensor_scalar(hot[:, j, 1, :], iota, picks_t[:, 1, bass.ds(t + j, 1)],
                                          picks_t[:, 2, bass.ds(t + j, 1)], ALU.is_equal, ALU.mult)\
                            .then_inc(hot_ready, 1)

                def gated(s, j):
                    dve.wait_ge(pair_loaded[j], s * 16 + 32)
                    dve.tensor_tensor(prod[:, j, :].rearrange("p (i q t) -> p i q t", i=2, q=QT),
                                      gelu_in[:, j, :].rearrange("p (i q t) -> p i q t", i=2, q=QT),
                                      g_in[:, j, :].rearrange("p (q i t) -> p i q t", i=2, q=QT), ALU.mult)\
                        .then_inc(act_ready, 1)
                    dve.wait_ge(act_hi_ready, s + (j + 1))
                    dve.tensor_tensor(B_lo[:, 4 + 2 * j:6 + 2 * j, :], prod[:, j, :].rearrange("p (i t) -> p i t", i=2),
                                      B_hi[:, 4 + 2 * j:6 + 2 * j, :].bitcast(F32), ALU.subtract)\
                        .then_inc(act_lo_ready, 1)

                for j in range(2):
                    gated(0, j)
                with dve.Fori(2, PAIRS - 1, 2) as s:
                    for j in range(2):
                        gated(s, j)
                dve.wait_ge(slab_used, N_MID + 2 * PAIRS)
                for m in range(KD):
                    dve.tensor_tensor(X[:, m, :], bank[m][:, :], X[:, m, :], ALU.add)
            dve.drain().then_inc(x_done, 1)


def _slab(w):
    import numpy as np
    k = w.shape[0] // P
    a = w.reshape(k, P, w.shape[1]).transpose(1, 0, 2).reshape(P, -1)
    out = np.zeros((P, SLAB), np.float32)
    out[:, :a.shape[1]] = a
    return out


def _stream(i):
    import numpy as np
    slabs = []

    def columns(w, first=0, last=None):
        for a in range(first, w.shape[1] if last is None else last, 256):
            slabs.append(_slab(w[:, a:a + 256]))

    ada = i["w_ada"][0].T.reshape(N_ADA, 2, P, D).transpose(0, 2, 1, 3).reshape(N_ADA, P, SLAB)
    slabs.extend(ada[:ADA_FIRST])
    w = i["w_in"][0]
    columns(w, 0, 1792)
    columns(w, 2048, 2304)
    columns(w, 2304, 2560)
    columns(w, 1792, 2048)
    assert len(slabs) == ADA_FIRST + ADA_LATER_AT
    slabs.extend(ada[ADA_FIRST:])
    columns(i["w_out"][0])
    wg, wd = i["w_gate_up"][0], i["w_down"][0]
    f = 0
    for g in FFN_GROUPS:
        for j in range(f, f + g):
            slabs.append(_slab(np.concatenate([wg[:, P * j:P * j + P], wg[:, DFF + P * j:DFF + P * j + P]], 1)))
        columns(wd[P * f:P * (f + g)])
        f += g
    w = i["w_in_2"][0]
    gates_at = 2824
    pairs = [h for n in range(4) for h in (n, n + 4)]
    w_o = [i["w_fox_o_2"][0],
           i["w_swa_o_2"][0].reshape(HEADS, HD, D)[pairs].reshape(HEADS * HD, D), i["w_mem_o_2"][0]]
    for n, br in enumerate(("fox", "swa", "mem")):
        if br == "fox":
            columns(w, 0, 1536)
        elif br == "swa":
            columns(w[:, 1544:2056].reshape(D, HEADS, HD)[:, pairs].reshape(D, HEADS * HD))
            columns(w, 2056, 2312)
        else:
            columns(w, 2312, 2824)
            columns(i["w_mem_kv_2"][0])
        columns(w, gates_at + D * n, gates_at + D * (n + 1))
        for m in range(2):
            slabs.append(_slab(w_o[n][:, 512 * m:512 * m + 512]))
    columns(i["w_out_2"][0])
    u = i["peer_u_2"][0].reshape(KEYS, PAIRS, 2, KD, P)
    u = np.ascontiguousarray(u.transpose(1, 4, 2, 3, 0)).reshape(PAIRS, P, SLAB)
    v = i["peer_v_2"][0].reshape(KEYS, PAIRS, SLAB).transpose(1, 0, 2)
    for h in range(HEADS):
        slabs.append(_slab(i["w_peer_q_2"][0][:, 256 * h:256 * h + 256]))
        slabs.append(u[h])
    assert len(slabs) == N_ADA + N_MID + HEADS, len(slabs)
    return np.concatenate([np.stack(slabs), u[HEADS:], v])


def _columns(i):
    import numpy as np

    def tiles(a):
        return a.reshape(-1, P).T

    def rows(a):
        return np.broadcast_to(a.reshape(1, -1), (P, a.size))

    def twice(a):
        return np.concatenate([a.reshape(-1)] * 2).reshape(P, 1)

    parts = {
        "b_ada": tiles(i["b_ada"]), "g_mix": tiles(i["g_mix"]), "g_subln": tiles(i["g_subln"]),
        "pool_scale": tiles(i["pool_scale"]), "conv": tiles(i["conv_w"]), "g_ffn": tiles(i["g_ffn"]),
        "g_final": tiles(i["g_final"]), "g_norm1": tiles(i["norm1_g_2"]), "b_gate": tiles(i["b_gate_2"]),
        "g_fox_q": twice(i["fox_q_g_2"]), "g_fox_k": twice(i["fox_k_g_2"]), "g_swa_q": twice(i["swa_q_g_2"]),
        "g_swa_k": twice(i["swa_k_g_2"]), "g_mem": tiles(i["mem_norm_g_2"]), "g_mem_q": tiles(i["mem_q_g_2"]),
        "g_mem_k": tiles(i["mem_k_g_2"]), "g_norm2": tiles(i["norm2_g_2"]), "b_forget": rows(i["b_forget_2"]),
        "sinks": rows(i["swa_sinks_2"]),
        "lambda": rows(np.concatenate([i[n].reshape(-1) for n in ("lambda_q1", "lambda_k1", "lambda_q2", "lambda_k2")])),
        "w_forget": i["w_in_2"][0][:, 1536:1544].reshape(KD, P, HEADS).transpose(1, 0, 2).reshape(P, -1),
        "w_pool": i["w_pool"][0].reshape(2, P, 64).transpose(1, 0, 2).reshape(P, -1),
    }
    return np.ascontiguousarray(np.concatenate([parts[n] for n, _ in COLS] + [rows(i["c"])], 1))


def _tables():
    import numpy as np
    p = np.arange(P)[:, None]
    out = {"ident": np.eye(P), "mean_all": np.full((P, P), 1.0 / D), "mean_128": np.full((P, P), 1.0 / P),
           "mean_64": (p // 64 == np.arange(P)[None] // 64) / 64.0,
           "distance": np.abs(p - np.arange(896)[None] + 384),
           "causal": np.where(np.arange(P)[None] <= p, 0.0, NEG_INF), "upto": p <= np.arange(512)[None],
           "iota": np.broadcast_to(np.arange(P)[None], (P, P)), "iota16": np.broadcast_to(np.arange(16)[None], (P, 16))}
    t = np.arange(T)
    counts = []
    for w in (2, 4, 8, 16):
        counts.append(np.clip(t + w - w // 2, 0, T) - np.clip(t - w // 2, 0, T))
    r = np.stack([1.0 / c for c in counts])
    out["pool_recip"] = np.concatenate([np.repeat(r[2 * g:2 * g + 2], 64, axis=0) for g in range(2)], 1)
    d = p + P - np.arange(256)[None]
    ok = (d >= 0) & (d < P)
    out["swa_distance"] = np.where(ok, -d, 0)
    out["swa_mask"] = np.where(ok, 0.0, NEG_INF)
    return np.ascontiguousarray(np.concatenate([out[n].astype(np.float32) for n, _ in TABLES], 1))


def kernel(**inputs):
    import numpy as np
    import concourse.bacc as bacc
    from concourse.bass_utils import run_bass_kernel_spmd

    i = {k: np.asarray(v) for k, v in inputs.items()}
    keys_t = np.stack([i["peer_keys1_2"][0], i["peer_keys2_2"][0]], 1).reshape(16, KEYS, P).transpose(2, 0, 1)\
        .reshape(P, 16 * KEYS)
    arrays = {"x_t": np.ascontiguousarray(i["x"][0].T), "weights": _stream(i), "columns": _columns(i),
              "tables": _tables(), "mem_t_in": np.ascontiguousarray(i["mem_2"][0].T),
              "keys_t": np.ascontiguousarray(keys_t)}
    nc = bacc.Bacc("TRN2", target_bir_lowering=False, num_devices=1)
    args = [nc.dram_tensor(n, a.shape, F32, kind="ExternalInput").ap() for n, a in arrays.items()]
    out = nc.dram_tensor("out_t", (D, T), F32, kind="ExternalOutput").ap()
    build(nc, *args, out)
    r = run_bass_kernel_spmd(nc, [arrays], core_ids=[0])
    return np.ascontiguousarray(r.results[0]["out_t"].T)[None]
```

```python
from contextlib import ExitStack

import concourse.bass as bass
from concourse import mybir

P = 128
T = 512
QT = T // P
D = 1024
KD = D // P
DFF = 2816
FT = DFF // P
FFN_GROUPS = (8, 8, 6)
HEADS = 8
HD = 64
MEM = 256
MEM_HEADS = 4
KEYS = 128
TOPK = 16
EPS = 1e-6
NEG_INF = -1e30
LAMBDA_INIT = 0.2

SLAB = 2048
N_ADA = 6 * D // 256
ADA_FIRST = 8
ADA_LATER_AT = 10
N_MID = 93
PAIRS = KEYS // 2
GT = 64
GB = T // GT
U_PICKS, U_TOKENS, U_BETWEEN = 8, 4, 2
assert HEADS + U_PICKS + GB * (U_TOKENS + U_BETWEEN) == PAIRS and GT % (8 * U_TOKENS) == 0
U_AT = HEADS + U_PICKS

F32 = mybir.dt.float32
F32R = mybir.dt.float32r
U32 = mybir.dt.uint32
I32 = mybir.dt.int32
ALU = mybir.AluOpType
ACT = mybir.ActivationFunctionType
AX = mybir.AxisListType.X

COLS = [("b_ada", 48), ("g_mix", 8), ("g_subln", 4), ("pool_scale", 2), ("conv", 6), ("g_ffn", 8),
        ("g_final", 8), ("g_norm1", 8), ("b_gate", 24), ("g_fox_q", 1), ("g_fox_k", 1), ("g_swa_q", 1),
        ("g_swa_k", 1), ("g_mem", 8), ("g_mem_q", 1), ("g_mem_k", 1), ("g_norm2", 8), ("b_forget", 8),
        ("sinks", 8), ("lambda", 128), ("w_forget", 64), ("w_pool", 128)]
COL_AT = {}
N_COLS = 0
for _name, _width in COLS:
    COL_AT[_name] = (N_COLS, N_COLS + _width)
    N_COLS += _width

TABLES = [("ident", 128), ("mean_all", 128), ("mean_64", 128), ("mean_128", 128), ("distance", 896),
          ("pool_recip", 1024), ("causal", 128), ("upto", 512), ("swa_distance", 256), ("swa_mask", 256), ("iota", 128),
          ("iota16", 16)]
TABLE_AT = {}
N_TABLE = 0
for _name, _width in TABLES:
    TABLE_AT[_name] = (N_TABLE, N_TABLE + _width)
    N_TABLE += _width

ARENA = 19170


class Taken:

    def __init__(self, eng):
        self.eng = eng
        self.count = {}

    def take(self, sem, k=1):
        self.count[sem.name] = self.count.get(sem.name, 0) + k
        self.eng.wait_ge(sem, self.count[sem.name])


def build(nc, x_in, stream, cols_in, tables_in, mem_in, keys_in, out):
    g_dram = nc.dram_tensor("gates_dram", [GB, P, KEYS, GT], F32, kind="Internal").ap()
    gelu_dram = nc.dram_tensor("gelu_dram", [PAIRS, P, 2 * T], F32, kind="Internal").ap()

    with ExitStack() as ctx:
        def sb(name, shape, dt=F32):
            return ctx.enter_context(nc.sbuf_tensor(name, shape, dt))

        def sem(name):
            return ctx.enter_context(nc.semaphore(name))

        X = sb("X", [P, KD, T])
        A_hi = sb("A_hi", [P, KD, T], F32R)
        A_lo = sb("A_lo", [P, KD, T], F32R)
        with nc.sbuf_tensor("B_plain", [P, KD, T], F32) as B_plain:
            pass
        B_hi = sb("B_hi", [P, KD, T], F32R)
        with nc.sbuf_tensor("B_lo_plain", [P, KD, T], F32) as B_lo_plain:
            pass
        B_lo = sb("B_lo", [P, KD, T], F32R)
        raw = sb("raw", [P, 2, SLAB])
        with nc.sbuf_tensor("W_plain", [P, 4, SLAB], F32) as W_plain:
            pass
        W_hi = sb("W_hi", [P, 2, SLAB], F32R)
        W_lo = sb("W_lo", [P, 2, SLAB], F32R)
        tab = sb("tab", [P, 512])
        col = sb("col", [P, N_COLS])
        wf_hi = sb("wf_hi", [P, KD, HEADS], F32R)
        wf_lo = sb("wf_lo", [P, KD, HEADS], F32R)
        mod = sb("mod", [P, 48])
        gs = sb("gs", [P, 2, KD])
        small = sb("small", [P, 48])
        zero = sb("zero", [P, 1])
        arena = sb("arena", [P, ARENA])
        bank = [ctx.enter_context(nc.psum_tensor(f"bank{i}", [P, 512], F32)) for i in range(8)]

        def at(start, *shape):
            size = 1
            for n in shape:
                size *= n
            v = arena[:, start:start + size]
            if len(shape) == 2:
                v = v.rearrange("p (a b) -> p a b", b=shape[1])
            if len(shape) == 3:
                v = v.rearrange("p (a b c) -> p a b c", b=shape[1], c=shape[2])
            return v

        ident, mean_all, mean_64, mean_128 = (tab[:, i * P:(i + 1) * P] for i in range(4))

        def c_(name, i=0, n=1):
            a = COL_AT[name][0] + i
            return col[:, a:a + n]

        S = [at(512 * i, 512) for i in range(8)]
        Qt, Kt = at(4096, 4, T), at(6144, 4, T)
        V = at(8192, QT, 512)
        Ot = at(10240, 4, T)
        pool_in = at(12288, 2, 528)
        conv_in = at(13344, 2, 514)
        b_gate_t, c_gate_t = at(14372, 2, T), at(15396, 2, T)
        dist = at(16420, 896)
        pool_sum = at(17316, 2, 528)
        c_row = at(15396, 1024)
        merged = at(12288, KD, T)
        upto = at(16384, 512)
        ck = at(16896, 2, 512)
        causal = at(17920, P)
        log_f, cq = at(18048, QT, HEADS), at(18080, QT, HEADS)
        swa_nd, swa_mask, swa_bias = at(16384, 256), at(16640, 256), at(16896, 2, 256)
        mem_t = at(8192, KD, MEM)
        mem_kt, mem_v = at(6144, MEM_HEADS, MEM), at(10240, 2, 512)
        mem_o = at(8192, MEM_HEADS, T)
        recip_cnt = [at(4096 * 0 + 512 * 6, 512), at(512 * 7, 512)]
        keys = at(0, 16, KEYS)
        peer_q = at(2048, 2, 2, T)
        top_v = at(4096, QT, HEADS, 2 * TOPK)
        top_i = at(5120, QT, HEADS, 2 * TOPK)
        sum_v = at(6144, QT, HEADS, TOPK)
        sum_i = at(6656, QT, HEADS, TOPK)
        rest_a = at(7168, 2, KEYS)
        cand = at(7424, 2, 256)
        cand_rest = at(7936, 256)
        iota16 = at(8192, TOPK)
        sel_hi, sel_lo = at(8208, P), at(8336, P)
        top_f = at(8464, HEADS, 2 * TOPK)
        eq = at(8720, 2048)
        picks = at(10768, QT, 3, P)
        iw = at(12304, 2, P)
        picks_t = at(16384, 3, T)
        iota = at(17920, KEYS)
        hot = at(18048, 4, 2, KEYS)
        g_stage = at(0, 2, KEYS * GT)
        gate_t = [(B_plain if i < 4 else B_lo_plain)[:, 4 + i % 4, :] for i in range(KD)]
        gelu_in, g_in, prod = at(0, 2, 2 * T), at(2048, 2, 2 * T), at(4096, 2, 2 * T)
        gelu_out = B_plain[:, 0:4, :]

        slab_loaded = [sem("slab_loaded0"), sem("slab_loaded1")]
        ada_loaded = [sem(f"ada_loaded{i}") for i in range(4)]
        ada_used = sem("ada_used")
        ada_times_c = sem("ada_times_c")
        zero_ready = sem("zero_ready")
        slab_half = sem("slab_half")
        slab_split = sem("slab_split")
        slab_used = sem("slab_used")
        const_loaded, table_loaded = sem("const_loaded"), sem("table_loaded")
        lin_ready = [sem(f"lin_ready{i}") for i in range(4)]
        lin_free = [sem(f"lin_free{i}") for i in range(4)]
        work_ready = [sem(f"work_ready{i}") for i in range(2)]
        work_free = [sem(f"work_free{i}") for i in range(2)]
        turn_ready = [sem(f"turn_ready{i}") for i in range(2)]
        turn_free = [sem(f"turn_free{i}") for i in range(2)]
        act_stage, dve_stage = sem("act_stage"), sem("dve_stage")
        act_step, dve_step = sem("act_step"), sem("dve_step")
        lo_ready = sem("lo_ready")
        gate_ready = sem("gate_ready")
        c_loaded, c_ready = sem("c_loaded"), sem("c_ready")
        square_ready = sem("square_ready")
        norm_square = sem("norm_square")
        square_added = sem("square_added")
        x_normed = sem("x_normed")
        normed = sem("normed")
        whole_ready = sem("whole_ready")
        hi_ready = sem("hi_ready")
        top_ready = sem("top_ready")
        exp_ready = sem("exp_ready")
        p_ready = sem("p_ready")
        values_used = sem("values_used")
        diff_ready = sem("diff_ready")
        small_ready, small_done = sem("small_ready"), sem("small_done")
        hot_ready, hot_used = sem("hot_ready"), sem("hot_used")
        g_copied, g_stored = sem("g_copied"), [sem("g_stored0"), sem("g_stored1")]
        pair_loaded = [sem("pair_loaded0"), sem("pair_loaded1")]
        gelu_stored = [sem("gelu_stored0"), sem("gelu_stored1")]
        a_ready, gelu_ready, act_ready = sem("a_ready"), sem("gelu_ready"), sem("act_ready")
        act_hi_ready, act_lo_ready = sem("act_hi_ready"), sem("act_lo_ready")
        x_done, stored = sem("x_done"), sem("stored")

        block = ctx.enter_context(nc.Block())
        NORMS = {
            "first": (X, T, lambda k: gs[:, 0, k:k + 1], lambda k: mod[:, k:k + 1], "A"),
            "ffn": (X, T, lambda k: gs[:, 1, k:k + 1], lambda k: mod[:, 24 + k:25 + k], "A"),
            "final": (X, T, lambda k: c_("g_final", k), None, None),
            "second": (X, T, lambda k: c_("g_norm1", k), None, "A"),
            "mem": (mem_t, MEM, lambda k: c_("g_mem", k), None, "B"),
            "peer": (X, T, lambda k: c_("g_norm2", k), None, "A"),
        }
        HEAD_NORMS = {
            "subln": ([Ot[:, i, :] for i in range(4)], T, mean_64, lambda i: small[:, 8 + i:9 + i]),
            "fox_q": ([Qt[:, i, :] for i in range(4)], T, mean_64, lambda i: small[:, 16:17]),
            "fox_k": ([Kt[:, i, :] for i in range(4)], T, mean_64, lambda i: c_("g_fox_k")),
            "swa_q": ([Qt[:, i, :] for i in range(4)], T, mean_64, lambda i: small[:, 17:18]),
            "swa_k": ([Kt[:, 0, :]], T, mean_64, lambda i: c_("g_swa_k")),
            "mem_q": ([Qt[:, i, :] for i in range(4)], T, mean_128, lambda i: small[:, 18:19]),
            "mem_k": ([mem_kt[:, i, :] for i in range(4)], MEM, mean_128, lambda i: c_("g_mem_k")),
        }

        def att(kind):
            if kind == "diff":
                return dict(heads=HEADS, parts=2, k0=lambda q: 0, k1=lambda q: QT,
                            q=lambda h, p: (Qt[64 * (h % 2) + 32 * p:64 * (h % 2) + 32 * p + 32, h // 2, :]),
                            k=lambda h, p: (Kt[64 * (h % 2) + 32 * p:64 * (h % 2) + 32 * p + 32, h // 2, :]),
                            v=lambda h, j: V[:, j, HD * h:HD * h + HD], m=HD,
                            o=lambda h: (64 * (h % 2), h // 2, Ot))
            if kind == "fox":
                return dict(heads=HEADS, parts=1, k0=lambda q: 0, k1=lambda q: q + 1,
                            q=lambda h, p: Qt[64 * (h % 2):64 * (h % 2) + 64, h // 2, :],
                            k=lambda h, p: Kt[64 * (h % 2):64 * (h % 2) + 64, h // 2, :],
                            v=lambda h, j: V[:, j, HD * h:HD * h + HD], m=HD,
                            o=lambda h: (64 * (h % 2), h // 2, Ot))
            if kind == "swa":
                return dict(heads=HEADS, parts=1, k0=lambda q: max(q - 1, 0), k1=lambda q: q + 1,
                            q=lambda h, p: Qt[64 * (h // 4):64 * (h // 4) + 64, h % 4, :],
                            k=lambda h, p: Kt[64 * (h // 4):64 * (h // 4) + 64, 0, :],
                            v=lambda h, j: V[:, j, HD * (h // 4):HD * (h // 4) + HD], m=HD,
                            o=lambda h: (64 * (h // 4), h % 4, Ot))
            return dict(heads=MEM_HEADS, parts=1, k0=lambda q: 0, k1=lambda q: MEM // P,
                        q=lambda h, p: Qt[:, h, :], k=lambda h, p: mem_kt[:, h, :],
                        v=lambda h, j: mem_v[:, j, P * h:P * h + P], m=P, o=lambda h: (0, h, mem_o))

        def units(a):
            return [(h, q) for h in range(a["heads"]) for q in range(QT)]

        BRANCHES = ("fox", "swa", "mem")

        P_SLOTS = {"diff": [S[2], S[3], at(14372, 512), at(14884, 512)]}
        for _kind in BRANCHES:
            P_SLOTS[_kind] = [S[2], S[3]]
        L_SLOTS = {_kind: [S[0], S[1]] for _kind in BRANCHES}
        L_SLOTS["diff"] = [S[0], S[1], at(12288, 512), at(12800, 512)]
        recip_counts = at(512 * 6, 1024)

        def ada_rows(slab):
            return slab.rearrange("p (m i) -> p m i", m=2)

        c_rows = c_row.unsqueeze(1).to_broadcast([P, 2, D])

        def ada_place(s):
            return W_plain[:, s - 2, :] if 2 <= s < 6 else raw[:, s % 2, :]

        tile_signal = []

        @block.sync
        def _(sp):
            base = N_ADA + N_MID + PAIRS

            sp.dma_start(c_row, cols_in[:, N_COLS:N_COLS + D]).then_inc(c_loaded, 16)
            for s in range(2):
                sp.dma_start(raw[:, s, :], stream[s, :, :]).then_inc(slab_loaded[s], 16)
            sp.dma_start(X[:, :, :], x_in.rearrange("(k p) t -> p k t", p=P)).then_inc(const_loaded, 16)
            for s in range(4):
                sp.dma_start(W_plain[:, s, :], stream[2 + s, :, :]).then_inc(ada_loaded[s], 16)

            def load_slab(n, place):
                sp.dma_start(raw[:, place, :], stream[n, :, :]).then_inc(slab_loaded[place], 16)

            for s in range(6, ADA_FIRST + 2):
                sp.wait_ge(ada_used, s - 5 if s < ADA_FIRST else s - 1)
                load_slab(s, s % 2)
            for s in range(2, ADA_LATER_AT):
                sp.wait_ge(slab_split, s - 1)
                load_slab(ADA_FIRST + s, s % 2)
            for s in range(ADA_FIRST, N_ADA + 2):
                if s < ADA_FIRST + 2:
                    sp.wait_ge(slab_split, ADA_LATER_AT - 1 + s - ADA_FIRST)
                else:
                    sp.wait_ge(ada_used, s - 1)
                load_slab(ADA_LATER_AT + s, s % 2)
            tail = (base - N_ADA) % 2
            with sp.Fori(N_ADA + ADA_LATER_AT + 2, base - tail - 1, 2) as s:
                for j in range(2):
                    sp.wait_ge(slab_split, s + (j - 1 - N_ADA))
                    sp.dma_start(raw[:, j, :], stream[s + j, :, :]).then_inc(slab_loaded[j], 16)
            for s in range(base - tail, base):
                sp.wait_ge(slab_split, s - 1 - N_ADA)
                sp.dma_start(raw[:, s % 2, :], stream[s, :, :]).then_inc(slab_loaded[s % 2], 16)

            def value_slab(s, j):
                slot = (base + j) % 2
                sp.wait_ge(slab_split, s + (j + base - N_ADA - 1))
                sp.dma_start(raw[:, slot, :], stream[s + (base + j), :, :]).then_inc(slab_loaded[slot], 16)

            def pair(s, j):
                if isinstance(s, int):
                    sp.wait_ge(g_stored[j], 8 * GB)
                    sp.wait_ge(g_stored[1 - j], 8 * GB)
                else:
                    sp.wait_ge(act_ready, s + (j - 1))
                sp.wait_ge(gelu_stored[j], s * 8 + 16)
                sp.dma_start(gelu_in[:, j, :], gelu_dram[s + j, :, :]).then_inc(pair_loaded[j], 16)
                sp.dma_start(g_in[:, j, :].rearrange("p (q x) -> p q x", q=GB),
                             g_dram[:, :, bass.ds(s * 2 + 2 * j, 2), :].rearrange("q p e t -> p q (e t)"))\
                    .then_inc(pair_loaded[j], 16)

            for j in range(2):
                value_slab(0, j)
            for j in range(2):
                pair(0, j)
            with sp.Fori(2, PAIRS - 1, 2) as s:
                for j in range(2):
                    value_slab(s, j)
                    pair(s, j)
            sp.wait_ge(x_done, 1)
            sp.dma_start(out.rearrange("(k p) t -> p k t", p=P), X[:, :, :]).then_inc(stored, 16)
            sp.wait_ge(stored, 16)

        @block.gpsimd
        def _(pool):
            def split(s, j, ada=N_ADA - 4):
                pool.wait_ge(slab_loaded[j], s * 8 + (8 * ada + 16))
                if not isinstance(s, int) or s >= 2:
                    pool.wait_ge(slab_used, s + (j - 1))
                pool.tensor_tensor(W_hi[:, j, :], raw[:, j, :], zero[:, :].to_broadcast([P, SLAB]), ALU.add).then_inc(slab_half, 1)
                pool.wait_ge(slab_half, s + (j + 1))
                pool.tensor_tensor(W_lo[:, j, :], raw[:, j, :], W_hi[:, j, :].bitcast(F32),
                                   ALU.subtract).then_inc(slab_split, 1)

            pool.memset(zero[:, :], 0.0).then_inc(zero_ready, 1)
            pool.wait_ge(zero_ready, 1)
            n = N_MID + 2 * PAIRS
            for s in range(0, ADA_LATER_AT, 2):
                for j in range(2):
                    split(s, j, ADA_FIRST - 4)
            pool.wait_ge(c_ready, 2)
            for s in range(ADA_FIRST, N_ADA):
                pool.wait_ge(slab_loaded[s % 2], 8 * (s - s % 2 + ADA_LATER_AT - 4) + 16)
                w = ada_rows(raw[:, s % 2, :])
                pool.tensor_tensor(w, w, c_rows, ALU.mult).then_inc(ada_times_c, 1)
            with pool.Fori(ADA_LATER_AT, n - n % 2 - 1, 2) as s:
                for j in range(2):
                    split(s, j)
            if n % 2:
                split(n - 1, 0)

        @block.tensor
        def _(pe):
            take = Taken(pe).take
            at_ = {"slab": 0, "lin": 0, "work": 0, "turn": 0, "values": 0}
            ready_in = [0, 0, 0, 0]
            mm = pe.matmul

            def stage():
                take(act_stage)
                take(dve_stage)

            def lin():
                n = at_["lin"]
                at_["lin"] += 1
                if n >= 4:
                    pe.wait_ge(lin_free[n % 4], n // 4)
                return n % 4

            def lin_done(last, b):
                ready_in[b] += 1
                tile_signal.append((lin_ready[b], ready_in[b]))
                last.then_inc(lin_ready[b], 1)

            def slab_done(last):
                tile_signal.append((slab_used, at_["slab"]))
                last.then_inc(slab_used, 1)

            def work():
                n = at_["work"]
                at_["work"] += 1
                if n >= 2:
                    pe.wait_ge(work_free[n % 2], n // 2)
                return n % 2

            def turn():
                n = at_["turn"]
                at_["turn"] += 1
                if n >= 2:
                    pe.wait_ge(turn_free[n % 2], n // 2)
                return n % 2

            def slab():
                s = at_["slab"]
                at_["slab"] += 1
                pe.wait_ge(slab_split, s + 1)
                return (N_ADA + s) % 2

            def product(to, pairs):
                n = len(pairs)
                for i, ((lh, ll), (rh, rl)) in enumerate(pairs):
                    mm(to, lh, rh, start=i == 0, stop=False)
                    mm(to, lh, rl, start=False, stop=False)
                    last = mm(to, ll, rh, start=False, stop=i == n - 1)
                return last

            def w_tile(slot, a, n=P):
                return W_hi[:, slot, a:a + n], W_lo[:, slot, a:a + n]

            def act_tile(which, k, a=0, n=T):
                hi, lo = (A_hi, A_lo) if which == "A" else (B_hi, B_lo)
                return hi[:, k, a:a + n], lo[:, k, a:a + n]

            def features_on_partitions(which, n_slabs, kts=KD, n=T, beside=iter(())):
                for _ in range(n_slabs):
                    slot = slab()
                    for m in range(2):
                        b = lin()
                        last = product(bank[b][:, 0:n], [(w_tile(slot, 256 * k + P * m), act_tile(which, k, 0, n))
                                                         for k in range(kts)])
                        lin_done(last, b) if m == 0 else slab_done(last)
                        next(beside, None)

            def behind_split(which, ks=range(KD), waits=range(KD), n_slabs=1, stride=256):
                slots = [slab() for _ in range(n_slabs)]
                per_slab = stride // P
                banks = [lin() for _ in range(n_slabs * per_slab)]
                for k in ks:
                    if k in waits:
                        take(lo_ready)
                    for i, b in enumerate(banks):
                        lh, ll = w_tile(slots[i // per_slab], stride * k + P * (i % per_slab))
                        rh, rl = act_tile(which, k)
                        mm(bank[b][:, :], lh, rh, start=k == ks[0], stop=False, skip_group_check=True)
                        mm(bank[b][:, :], lh, rl, start=False, stop=False, skip_group_check=True)
                        last = mm(bank[b][:, :], ll, rh, start=False, stop=k == ks[-1], skip_group_check=True)
                        if k == ks[-1]:
                            if i % per_slab < per_slab - 1:
                                lin_done(last, b)
                            else:
                                tile_signal.append((slab_used, at_["slab"] - n_slabs + 1 + i // per_slab))
                                last.then_inc(slab_used, 1)

            def tokens_on_partitions(which, n_slabs, blocks, first=0, width=256, beside=iter(())):
                for _ in range(n_slabs):
                    if width == 256:
                        slot = slab()
                    else:
                        slot = (N_ADA + at_["slab"] - 1) % 2
                    for q in range(blocks):
                        b = lin()
                        last = product(bank[b][:, 0:width], [(act_tile(which, k, P * q, P),
                                                              w_tile(slot, 256 * k + first, width)) for k in range(KD)])
                        lin_done(last, b) if q < blocks - 1 else slab_done(last)
                        next(beside, None)

            def norm(name):
                n = NORMS[name][1]
                take(square_added, KD - 1)
                b = work()
                mm(bank[4 + b][:, 0:n], mean_all, S[5][:, 0:n], start=True, stop=True).then_inc(work_ready[b], 1)

            def head_norm(*names):
                def mean_of(g, mean, n):
                    take(square_ready)
                    b = work()
                    mm(bank[4 + b][:, 0:n], mean, S[g % 2][:, 0:n], start=True, stop=True).then_inc(work_ready[b], 1)

                g = 0
                for name in names:
                    tiles, n, mean, _ = HEAD_NORMS[name]
                    for _ in tiles:
                        yield mean_of(g, mean, n)
                        g += 1

            def attention(kind):
                a = att(kind)
                us = units(a)
                n0 = at_["turn"]
                o_bank = {}
                gate = {"signals": []}

                def scores(u):
                    h, q = us[u]
                    if kind == "fox" and q == 0:
                        b = work()
                        for j in range(QT):
                            last = mm(bank[4 + b][:, P * j:T], log_f[:, j, h:h + 1].to_broadcast([P, P]),
                                      upto[:, 0:T - P * j], start=j == 0, stop=j == QT - 1, skip_group_check=True)
                        last.then_inc(work_ready[b], 1)
                    for p in range(a["parts"]):
                        b = work()
                        w = P * (a["k1"](q) - a["k0"](q))
                        if kind == "diff":
                            rows = slice(64 * (h % 2) + 32 * p, 64 * (h % 2) + 32 * p + 32)
                            queries, keys_ = act_tile("B", h // 2, P * q, P), act_tile("A", h // 2)
                            product(bank[4 + b][:, :], [([x[rows, :] for x in queries], [x[rows, :] for x in keys_])])\
                                .then_inc(work_ready[b], 1)
                            continue
                        mm(bank[4 + b][:, 0:w], a["q"](h, p)[:, P * q:P * q + P],
                           a["k"](h, p)[:, P * a["k0"](q):P * a["k1"](q)], start=True, stop=True)\
                            .then_inc(work_ready[b], 1)

                def turns(u):
                    h, q = us[u]
                    take(p_ready)
                    b = turn()
                    for j in range(a["k1"](q) - a["k0"](q)):
                        last = pe.transpose(bank[6 + b][:, P * j:P * j + P], S[4 + u % 2][:, P * j:P * j + P], ident)
                    last.then_inc(turn_ready[b], 1)

                def values(u):
                    h, q = us[u]
                    pe.wait_ge(turn_free[(n0 + u) % 2], (n0 + u) // 2 + 1)
                    if q == 0:
                        o_bank[h] = lin()
                    row = a["o"](h)[0]
                    for j in range(a["k0"](q), a["k1"](q)):
                        jj = j - a["k0"](q)
                        last = mm(bank[o_bank[h]][row:row + a["m"], P * q:P * q + P], a["v"](h, j),
                                  S[6 + u % 2][:, P * jj:P * jj + P], start=jj == 0, stop=j == a["k1"](q) - 1)
                    last.then_inc(values_used, 1)
                    at_["values"] += 1
                    if kind == "diff":
                        if q == QT - 1:
                            tile_signal.append((values_used, at_["values"]))
                        return
                    per_head = KD // a["heads"]
                    for i in range(2 * per_head * q, 2 * per_head * (q + 1)):
                        m, k = per_head * h + i // KD, i % KD
                        if k == 0:
                            gate["bank"] = lin()
                            if m % 2 == 0:
                                gate["slot"] = slab()
                        to = bank[gate["bank"]][:, :]
                        (lh, ll), (rh, rl) = w_tile(gate["slot"], 256 * k + P * (m % 2)), act_tile("A", k)
                        mm(to, lh, rh, start=k == 0, stop=False, skip_group_check=True)
                        mm(to, lh, rl, start=False, stop=False, skip_group_check=True)
                        last = mm(to, ll, rh, start=False, stop=k == KD - 1, skip_group_check=True)
                        if k == KD - 1:
                            (slab_done(last) if m % 2 else lin_done(last, gate["bank"]))
                            gate["signals"].append(tile_signal.pop())
                    if q == QT - 1:
                        tile_signal.append((values_used, at_["values"]))
                        tile_signal.extend(gate["signals"])
                        gate["signals"] = []


                for u in range(len(us) + 3):
                    if u < len(us):
                        scores(u)
                    if 2 <= u <= len(us) + 1:
                        turns(u - 2)
                    if u >= 3:
                        values(u - 3)

            take(const_loaded, 16 * 3)
            norm("first")
            behind_split("A")
            stage()
            features_on_partitions("A", 3)
            features_on_partitions("A", 4)
            pe.wait_ge(diff_ready, 1)
            for g in range(2):
                b = work()
                for r in range(2):
                    last = mm(bank[4 + b][64 * r:64 * r + 64, :], c_("w_pool", 64 * g, 64)[64 * r:64 * r + 64, :],
                              S[g][64 * r:64 * r + 64, :], start=True, stop=True, skip_group_check=True)
                last.then_inc(work_ready[b], 1)
            tokens_on_partitions("A", 2, QT)
            stage()
            attention("diff")
            stage()
            for _ in head_norm("subln"):
                pass
            behind_split("B", ks=(4, 5, 6, 7, 0, 1, 2, 3), waits=range(4))
            stage()
            features_on_partitions("B", 3)
            stage()
            norm("ffn")
            for n, g in enumerate(FFN_GROUPS):
                if n == 0:
                    behind_split("A")
                    stage()
                features_on_partitions("A", g - (n == 0))
                behind_split("B", ks=range(g))
                stage()
                features_on_partitions("B", 3, kts=g)
                stage()
            norm("final")
            stage()
            norm("second")
            behind_split("A")
            stage()
            for br in BRANCHES:
                features_on_partitions("A", 2 if br == "swa" else 1)
                if br == "fox":
                    features_on_partitions("A", 2)
                    tokens_on_partitions("A", 2, QT, beside=head_norm("fox_q", "fox_k"))
                    for q in range(QT):
                        b = lin()
                        lin_done(product(bank[b][:, 0:HEADS], [(act_tile("A", k, P * q, P),
                                                                (wf_hi[:, k, :], wf_lo[:, k, :]))
                                                               for k in range(KD)]), b)
                    stage()
                    b = work()
                    for q in range(QT):
                        for j in range(q + 1):
                            last = mm(bank[4 + b][:, HEADS * q:HEADS * q + HEADS],
                                      upto[:, 0:P] if j == q else upto[:, P:2 * P], log_f[:, j, :],
                                      start=j == 0, stop=j == q)
                    last.then_inc(work_ready[b], 1)
                elif br == "swa":
                    slot = slab()
                    b = lin()
                    lin_done(product(bank[b][:, :], [(w_tile(slot, 256 * k), act_tile("A", k))
                                                     for k in range(KD)]), b)
                    beside = head_norm("swa_q", "swa_k")
                    tokens_on_partitions("A", 1, QT, first=P, width=P, beside=beside)
                    next(beside)
                else:
                    norm("mem")
                    features_on_partitions("A", 1)
                    stage()
                    beside = head_norm("mem_q", "mem_k")
                    features_on_partitions("B", 2, n=MEM, beside=beside)
                    tokens_on_partitions("B", 2, MEM // P, beside=beside)
                stage()
                attention(br)
                behind_split("B", ks=range(4), n_slabs=1, stride=512)
                stage()
                stage()
                slot = slab()
                for m in range(4):
                    b = lin()
                    last = product(bank[b][:, :], [(w_tile(slot, 512 * k + P * m), act_tile("B", k))
                                                   for k in range(4)])
                    if m < 3:
                        lin_done(last, b)
                slab_done(last)
                stage()
            behind_split("B")
            stage()
            features_on_partitions("B", 3)
            stage()
            norm("peer")
            behind_split("A", n_slabs=1)
            stage()
            take(act_stage)

            def u_half(s, odd, j, before=N_MID, token=None):
                slot = (N_ADA + before + odd + (s if isinstance(s, int) else 0)) % 2
                pe.wait_ge(slab_split, s + (odd + before + 1))
                if not isinstance(s, int) or s + odd > 0:
                    pe.wait_ge(gelu_ready, s * 2 + (2 * odd + j - 1))
                for k in range(KD):
                    (lh, ll), (rh, rl) = w_tile(slot, D * j + P * k), act_tile("A", k)
                    mm(bank[6 + j][:, :], lh, rh, start=k == 0, stop=False)
                    mm(bank[6 + j][:, :], lh, rl, start=False, stop=False)
                    last = mm(bank[6 + j][:, :], ll, rh, start=False, stop=k == KD - 1)
                    if k == KD - 1:
                        last.then_inc(slab_used if j else a_ready, 1)
                    if token:
                        token(k)

            def u_slabs(first, n):
                for s in range(first, first + n):
                    for j in range(2):
                        u_half(s, 0, j)

            for h in range(HEADS):
                if h:
                    features_on_partitions("A", 1)
                n = at_["lin"] - 2
                for i in range(2):
                    pe.wait_ge(lin_free[(n + i) % 4], (n + i) // 4 + 1)
                for q in range(QT):
                    b = work()
                    for half in range(2):
                        last = mm(bank[4 + b][:, KEYS * half:KEYS * half + KEYS],
                                  peer_q[:, h % 2, half, P * q:P * q + P], keys[:, 2 * h + half, :],
                                  start=True, stop=True)
                    last.then_inc(work_ready[b], 1)
                    if q in (1, 2):
                        u_half(h, 0, q - 1, before=at_["slab"] - h)
                at_["slab"] += 1
            u_slabs(HEADS, U_PICKS)
            stage()
            for q in range(QT):
                b = turn()
                for i in range(3):
                    last = pe.transpose(bank[6 + b][:, P * i:P * i + P], picks[:, q, i, :], ident)
                last.then_inc(turn_ready[b], 1)
            stage()

            pe.drain().then_inc(hot_used, 4)
            for q in range(GB):
                per_half = GT // (2 * U_TOKENS)
                first = U_AT + (U_TOKENS + U_BETWEEN) * q
                with pe.Fori(0, U_TOKENS - 1, 2) as s:
                    t = s * (2 * per_half)
                    for half in range(4):
                        def token(k):
                            j = per_half * half + k
                            if j % 4 == 0:
                                pe.wait_ge(g_copied, t + (GT * q + j + 4))
                            pe.wait_ge(hot_ready, t + (GT * q + j + 1))
                            mm(bank[4 + j // 4 % 2][:, P * (j % 4):P * (j % 4) + P], hot[:, j % 4, 0, :],
                               hot[:, j % 4, 1, :], start=True, stop=True).then_inc(hot_used, 1)

                        u_half(s, first + half // 2, half % 2, token=token)
                u_slabs(first + U_TOKENS, U_BETWEEN)

            def outputs_of(s, odd, first=False, final=False):
                slot = (N_ADA + N_MID + PAIRS + odd) % 2
                pe.wait_ge(slab_split, s + (odd + N_MID + PAIRS + 1))
                pe.wait_ge(act_lo_ready, s + (odd + 1))
                for j in range(2):
                    for m in range(KD):
                        lh, ll = w_tile(slot, D * j + P * m)
                        rh, rl = act_tile("B", 4 + 2 * odd + j)
                        mm(bank[m][:, :], lh, rh, start=first and j == 0, stop=False, skip_group_check=True)
                        mm(bank[m][:, :], lh, rl, start=False, stop=False, skip_group_check=True)
                        last = mm(bank[m][:, :], ll, rh, start=False, stop=final and j == 1, skip_group_check=True)
                last.then_inc(slab_used, 1)

            pe.wait_ge(g_copied, T + 8)
            pe.wait_ge(gelu_ready, KEYS)
            outputs_of(0, 0, first=True)
            outputs_of(0, 1)
            with pe.Fori(2, PAIRS - 3, 2) as s:
                for odd in range(2):
                    outputs_of(s, odd)
            outputs_of(PAIRS - 2, 0)
            outputs_of(PAIRS - 2, 1, final=True)

        @block.scalar
        def _(act):
            take = Taken(act).take
            at_ = {"tile": 0, "work": 0, "turn": 0, "values": 0, "probs": 0}
            own = [0]

            def step(ins):
                own[0] += 1
                ins.then_inc(act_step, 1)
                act.wait_ge(act_step, own[0])

            def stage_end():
                act.drain().then_inc(act_stage, 1)
                take(dve_stage)

            def load(to, name):
                a, b = TABLE_AT[name]
                act.dma_start(to, tables_in[:, a:b]).then_inc(table_loaded, 16)
                loads[0] += 1

            loads = [0]

            def loaded():
                act.wait_ge(table_loaded, 16 * loads[0])

            def tile(read, skip=0):
                n = at_["tile"]
                at_["tile"] += 1
                act.wait_ge(*tile_signal[n])
                read(bank[n % 4]).then_inc(lin_free[n % 4], 1)

            def copy_to(to, width=T, scale=1.0):
                tile(lambda b: act.activation(to, b[:, 0:width], ACT.Copy, scale=scale))

            def skip(n):
                at_["tile"] += n

            def root(n, to):
                w = at_["work"]
                at_["work"] += 1
                act.wait_ge(work_ready[w % 2], w // 2 + 1)
                act.activation(to[:, 0:n], bank[4 + w % 2][:, 0:n], ACT.Sqrt, bias=small[:, 0:1])\
                    .then_inc(work_free[w % 2], 1)

            def squares(name, ready=None):
                src, n, _, _, _ = NORMS[name]
                step(act.activation(small[:, 40:41], small[:, 0:1], ACT.Sqrt))
                for k in range(KD):
                    if ready:
                        ready(k)
                    if k in (2, 4, 5, 6, 7):
                        take(square_added)
                    act.activation(S[k % 2][:, 0:n], src[:, k, :], ACT.Square).then_inc(norm_square, 1)
                for _ in range(2):
                    take(square_added)

            def after_residual():
                n0 = at_["tile"]
                skip(KD)
                return lambda k: act.wait_ge(lin_free[(n0 + k) % 4], (n0 + k) // 4 + 1)

            def norm(name):
                src, n, _, _, to = NORMS[name]
                root(n, S[2])
                if to:
                    split(8, lambda k: S[3 + k % 2][:, 0:n], to, n=n)

            def split(tiles, source, to, first=0, n=T):
                for k in range(tiles):
                    take(whole_ready)
                    act.activation((A_hi if to == "A" else B_hi)[:, first + k, 0:n], source(k), ACT.Copy)\
                        .then_inc(hi_ready, 1)

            def head_norm(*names):
                tiles = [(t, HEAD_NORMS[name][1]) for name in names for t in HEAD_NORMS[name][0]]
                for i in range(len(tiles) + 1):
                    if i < len(tiles):
                        t, n = tiles[i]
                        act.activation(S[i % 2][:, 0:n], t, ACT.Square).then_inc(square_ready, 1)
                    if i >= 1:
                        if i >= 3:
                            take(normed)
                        root(tiles[i - 1][1], S[2 + (i - 1) % 2])
                    if i == len(tiles):
                        for _ in range(min(2, len(tiles))):
                            take(normed)
                    yield

            def attention(kind):
                a = att(kind)
                us = units(a)
                p_slots = P_SLOTS[kind]
                p_before = at_["probs"]
                v0 = at_["values"]
                i = 0
                per_head = KD // a["heads"]
                for u in range(len(us) + 3):
                    if u < len(us):
                        h, q = us[u]
                        w = P * (a["k1"](q) - a["k0"](q))
                        for p in range(a["parts"]):
                            take(top_ready)
                            if u * a["parts"] >= len(p_slots):
                                act.wait_ge(p_ready, p_before + u + 1 - len(p_slots) // a["parts"])
                            if kind == "swa":
                                act.activation(small[:, 32 + i % 4:33 + i % 4], c_("sinks", h), ACT.Exp,
                                               bias=small[:, 24 + i % 2:25 + i % 2])
                            places = len(L_SLOTS[kind])
                            act.activation(p_slots[i % len(p_slots)][:, 0:w], L_SLOTS[kind][i % places][:, 0:w],
                                           ACT.Exp, bias=small[:, 24 + i % places:25 + i % places],
                                           accum_out=small[:, 28 + i % 4:29 + i % 4]).then_inc(exp_ready, 1)
                            i += 1
                    if 1 <= u <= len(us):
                        h, q = us[u - 1]
                        w = P * (a["k1"](q) - a["k0"](q))
                        n = at_["turn"]
                        at_["turn"] += 1
                        act.wait_ge(turn_ready[n % 2], n // 2 + 1)
                        if u - 1 >= 2:
                            act.wait_ge(values_used, v0 + u - 2)
                        act.activation(S[6 + (u - 1) % 2][:, 0:w], bank[6 + n % 2][:, 0:w], ACT.Copy)\
                            .then_inc(turn_free[n % 2], 1)
                    if kind != "diff" and u >= 3 and us[u - 3][1] == QT - 1:
                        for m in range(per_head * us[u - 3][0], per_head * (us[u - 3][0] + 1)):
                            tile(lambda b: act.activation(gate_t[m], b[:, :], ACT.Copy))
                    if 2 <= u <= len(us) + 1 and us[u - 2][1] == QT - 1:
                        row, i_o, o = a["o"](us[u - 2][0])
                        tile(lambda b: act.activation(o[row:row + a["m"], i_o, :], b[row:row + a["m"], :], ACT.Copy))
                    if kind == "diff" and u % 2 and u < len(us):
                        modulation(ADA_FIRST + u // 2)
                at_["values"] += len(us)
                at_["probs"] += len(us)
                at_["work"] += len(us) * a["parts"] + (HEADS if kind == "fox" else 0)

            def modulation(s):
                act.wait_ge(ada_times_c, s + 1)
                for m in range(2):
                    w = (ada_place(s) if s < ADA_FIRST else raw[:, s % 2, :])[:, D * m:D * m + D]
                    ins = act.activation(w, w, ACT.Copy, accum_out=mod[:, 2 * s + m:2 * s + m + 1])
                ins.then_inc(ada_used, 1)

            def silu_of_c(n):
                if n > 1:
                    act.dma_start(c_row, cols_in[:, N_COLS:N_COLS + D]).then_inc(c_loaded, 16)
                act.wait_ge(c_loaded, 16 * n)
                act.activation(c_row, c_row, ACT.Silu).then_inc(c_ready, 1)

            act.dma_start(col[:, :], cols_in[:, 0:N_COLS]).then_inc(const_loaded, 16)
            act.dma_start(tab[:, :], tables_in[:, 0:512]).then_inc(const_loaded, 16)
            silu_of_c(1)
            for s in range(2):
                modulation(s)
            act.wait_ge(const_loaded, 16 * 3)
            take(small_ready)
            act.activation(small[:, 4:6], small[:, 2:4], ACT.Exp).then_inc(small_done, 1)
            act.activation(wf_hi[:, :, :], c_("w_forget", 0, 64).rearrange("p (k h) -> p k h", k=KD), ACT.Copy)\
                .then_inc(small_done, 1)
            squares("first")
            for s in range(2, ADA_FIRST):
                modulation(s)
            norm("first")
            stage_end()

            load(dist, "distance")
            load(recip_counts, "pool_recip")
            for i in range(2):
                copy_to(pool_in[:, i, 8:8 + T])
            for i in range(2):
                copy_to(c_gate_t[:, i, :])
            skip(2)
            for i in range(2):
                copy_to(b_gate_t[:, i, :])
            for i in range(4):
                n = at_["tile"]
                copy_to(Qt[:, i, :], scale=32 ** -0.5)
                act.wait_ge(lin_free[n % 4], n // 4 + 1)
                act.activation(B_hi[:, i, :], Qt[:, i, :], ACT.Copy).then_inc(hi_ready, 1)
            split(2, lambda i: S[4 + i], "B", first=6)
            for i in range(4):
                copy_to(Kt[:, i, :])
            at_["work"] += 2
            for c in range(2):
                for q in range(QT):
                    copy_to(V[:, q, 256 * c:256 * c + 256], width=256)
                if c == 0:
                    split(2, lambda i: S[2 + i], "B", first=4)
            for i in range(4):
                act.activation(A_hi[:, i, :], Kt[:, i, :], ACT.Copy).then_inc(hi_ready, 1)
            loaded()
            stage_end()
            silu_of_c(2)
            attention("diff")
            stage_end()
            for _ in head_norm("subln"):
                pass
            split(4, lambda i: Ot[:, i, :], "B")
            stage_end()
            squares("ffn", after_residual())
            stage_end()
            norm("ffn")
            stage_end()
            for g in FFN_GROUPS:
                for i in range(g):
                    tile(lambda b: act.activation(S[i % 2], b[:, :], ACT.Silu))
                    take(whole_ready)
                    skip(1)
                    act.activation(B_hi[:, i, :], S[2 + i % 2], ACT.Copy).then_inc(hi_ready, 1)
                stage_end()
                if g == FFN_GROUPS[-1]:
                    squares("final", after_residual())
                else:
                    skip(8)
                stage_end()
            norm("final")
            load(upto, "upto")
            load(causal, "causal")
            squares("second", lambda k: take(x_normed))
            stage_end()
            norm("second")
            stage_end()
            for n_br, br in enumerate(BRANCHES):
                if br == "mem":
                    act.dma_start(mem_t, mem_in.rearrange("(k p) t -> p k t", p=P)).then_inc(table_loaded, 16)
                    loads[0] += 1
                    loaded()
                    squares("mem")
                for i in range(4):
                    if br == "mem" and i == 2:
                        norm("mem")
                    copy_to(Qt[:, i, :])
                if br == "fox":
                    for i in range(4):
                        copy_to(Kt[:, i, :])
                    beside = head_norm("fox_q", "fox_k")
                    for c in range(2):
                        for q in range(QT):
                            next(beside)
                            copy_to(V[:, q, 256 * c:256 * c + 256], width=256)
                    next(beside)
                    skip(QT)
                    take(small_ready)
                    step(act.activation(S[1][:, 0:32], S[0][:, 0:32], ACT.Exp))
                    act.activation(S[2][:, 0:32], S[1][:, 0:32], ACT.Ln, bias=small[:, 1:2]).then_inc(small_done, 1)
                    loaded()
                    stage_end()
                    at_["work"] += 1
                elif br == "swa":
                    load(swa_nd, "swa_distance")
                    load(swa_mask, "swa_mask")
                    copy_to(Kt[:, 0, :])
                    beside = head_norm("swa_q", "swa_k")
                    for q in range(QT):
                        next(beside)
                        copy_to(V[:, q, 0:P], width=P)
                    for _ in beside:
                        pass
                    loaded()
                else:
                    stage_end()
                    beside = head_norm("mem_q", "mem_k")
                    for i in range(4):
                        next(beside)
                        copy_to(mem_kt[:, i, :], width=MEM)
                    for c in range(2):
                        for q in range(MEM // P):
                            next(beside)
                            copy_to(mem_v[:, q, 256 * c:256 * c + 256], width=256)
                    next(beside)
                    for _ in beside:
                        pass
                stage_end()
                attention(br)
                stage_end()
                o = mem_o if br == "mem" else Ot
                split(4, lambda i: o[:, i, :], "B")
                stage_end()
                for i in range(KD):
                    act.activation(gate_t[i], gate_t[i], ACT.Sigmoid, bias=c_("b_gate", KD * n_br + i))\
                        .then_inc(gate_ready, 1)
                skip(KD)
                stage_end()
            split(8, lambda k: merged[:, k, :], "B")
            stage_end()
            squares("peer", after_residual())
            stage_end()
            norm("peer")
            act.drain().then_inc(act_stage, 1)
            take(dve_stage)
            act.dma_start(keys.rearrange("p i k -> p (i k)"), keys_in).then_inc(table_loaded, 16)
            loads[0] += 1
            load(iota16, "iota16")
            load(iota, "iota")
            loaded()
            act.drain().then_inc(act_stage, 1)

            def gelus(s, odd=0, tokens=None):
                p = (s + odd) % 2 if isinstance(s, int) else odd % 2
                out_ = gelu_out[:, 2 * p:2 * p + 2, :]
                for j in range(2):
                    if tokens:
                        tokens(j)
                    if j == 0:
                        act.wait_ge(a_ready, s + (odd + 1))
                        if not isinstance(s, int) or s >= 2:
                            act.wait_ge(gelu_stored[p], s * 8 + (odd - p) * 8)
                    else:
                        n = 2 * s + 2 + N_MID - HEADS if isinstance(s, int) and s < HEADS else s + (odd + 1 + N_MID)
                        act.wait_ge(slab_used, n)
                    act.activation(out_[:, j, :], bank[6 + j][:, :], ACT.Gelu).then_inc(gelu_ready, 1)
                act.wait_ge(gelu_ready, s * 2 + (2 * odd + 2))
                act.dma_start(gelu_dram[s + odd, :, :], out_.rearrange("p j t -> p (j t)"))\
                    .then_inc(gelu_stored[p], 16)

            w = at_["work"]
            for h in range(HEADS):
                if h >= 2:
                    n = w + QT * (h - 1) - 1
                    act.wait_ge(work_ready[n % 2], n // 2 + 1)
                for half in range(2):
                    copy_to(peer_q[:, h % 2, half, :])
                gelus(h)
            at_["work"] += QT * HEADS
            take(small_ready)
            act.activation(eq[:, 512:1024], eq[:, 0:512], ACT.Exp).then_inc(small_done, 1)
            for s in range(HEADS, HEADS + U_PICKS):
                gelus(s)
            stage_end()
            for q in range(QT):
                n = at_["turn"]
                at_["turn"] += 1
                act.wait_ge(turn_ready[n % 2], n // 2 + 1)
                act.activation(picks_t[:, :, P * q:P * q + P],
                               bank[6 + n % 2][:, 0:3 * P].rearrange("p (i t) -> p i t", i=3), ACT.Copy)\
                    .then_inc(turn_free[n % 2], 1)
            stage_end()
            act.drain().then_inc(g_copied, 8)
            for q in range(GB):
                if q >= 2:
                    act.wait_ge(g_stored[q % 2], 16 * (q // 2))
                stage = g_stage[:, q % 2, :].rearrange("p (e t) -> p e t", t=GT)
                per_half = GT // (2 * U_TOKENS)
                first = U_AT + (U_TOKENS + U_BETWEEN) * q
                with act.Fori(0, U_TOKENS - 1, 2) as s:
                    t = s * (2 * per_half)

                    def tokens(half):
                        for i in range(per_half // 4):
                            j = per_half * half + 4 * i
                            act.wait_ge(hot_used, t + (GT * q + j + 8))
                            act.activation(stage[:, :, bass.ds(t + j, 4)],
                                           bank[4 + j // 4 % 2][:, :].rearrange("p (t e) -> p e t", t=4), ACT.Copy)\
                                .then_inc(g_copied, 4)

                    for odd in range(2):
                        gelus(s, first + odd, lambda j: tokens(2 * odd + j))
                act.wait_ge(g_copied, 8 + GT * (q + 1))
                act.dma_start(g_dram[q].rearrange("p e t -> p (e t)"), g_stage[:, q % 2, :])\
                    .then_inc(g_stored[q % 2], 16)
                for s in range(first + U_TOKENS, first + U_TOKENS + U_BETWEEN):
                    gelus(s)

            def operand(s, j):
                act.wait_ge(act_ready, s + (j + 1))
                if not isinstance(s, int):
                    act.wait_ge(slab_used, s + (j + N_MID + PAIRS - 1))
                act.activation(B_hi[:, 4 + 2 * j:6 + 2 * j, :], prod[:, j, :].rearrange("p (i t) -> p i t", i=2),
                               ACT.Copy).then_inc(act_hi_ready, 1)

            for j in range(2):
                operand(0, j)
            with act.Fori(2, PAIRS - 1, 2) as s:
                for j in range(2):
                    operand(s, j)

        @block.vector
        def _(dve):
            take = Taken(dve).take
            at_ = {"tile": 0, "work": 0, "turn": 0, "exp": 0, "normed": 0}
            own = [0]

            def step(ins):
                own[0] += 1
                ins.then_inc(dve_step, 1)
                dve.wait_ge(dve_step, own[0])

            def stage_end():
                dve.drain().then_inc(dve_stage, 1)
                take(act_stage)

            def tile(read):
                n = at_["tile"]
                at_["tile"] += 1
                dve.wait_ge(*tile_signal[n])
                read(bank[n % 4]).then_inc(lin_free[n % 4], 1)

            def skip(n):
                at_["tile"] += n

            def work():
                w = at_["work"]
                at_["work"] += 1
                dve.wait_ge(work_ready[w % 2], w // 2 + 1)
                return w % 2, w // 2 + 1

            def root_inverse(n, to):
                w = at_["work"]
                at_["work"] += 1
                dve.wait_ge(work_free[w % 2], w // 2 + 1)
                step(dve.reciprocal(to[:, 0:n], to[:, 0:n]))

            def rest(k, source, to, first, n=T, followed=True):
                take(hi_ready)
                hi, lo = (A_hi, A_lo) if to == "A" else (B_hi, B_lo)
                ins = dve.tensor_tensor(lo[:, first + k, 0:n], source, hi[:, first + k, 0:n].bitcast(F32), ALU.subtract)
                if followed:
                    ins.then_inc(lo_ready, 1)
                    take(lo_ready)
                else:
                    step(ins)

            def add_squares(k, n=T):
                take(norm_square)
                if k:
                    dve.tensor_tensor(S[5][:, 0:n], S[0][:, 0:n] if k == 1 else S[5][:, 0:n], S[k % 2][:, 0:n], ALU.add)\
                        .then_inc(square_added, 1)
                    take(square_added)

            def norm(name, before=None):
                src, n, gain, shift, to = NORMS[name]
                root_inverse(n, S[2])
                if before:
                    before()
                for k in range(KD + 1):
                    if k < KD:
                        y = S[3 + k % 2][:, 0:n] if to else src[:, k, :]
                        ins = dve.scalar_tensor_tensor(out=y, in0=src[:, k, :], scalar=gain(k), in1=S[2][:, 0:n],
                                                       op0=ALU.mult, op1=ALU.mult)
                        if shift:
                            step(ins)
                            ins = dve.tensor_scalar(y, y, shift(k), None, ALU.add)
                        if to:
                            ins.then_inc(whole_ready, 1)
                    if name == "final":
                        if k < KD:
                            ins.then_inc(x_normed, 1)
                        if k >= 1:
                            add_squares(k - 1)
                    if to and k >= 1:
                        rest(k - 1, S[3 + (k - 1) % 2][:, 0:n], to, 0, n, name != "mem")

            def split(tiles, source, to, first=0, followed=True):
                for k in range(tiles):
                    rest(k, source(k), to, first, followed=followed)

            def head_norm(*names):
                tiles = [(t, HEAD_NORMS[name][1], HEAD_NORMS[name][3](i))
                         for name in names for i, t in enumerate(HEAD_NORMS[name][0])]
                for i, (t, n, gain) in enumerate(tiles):
                    r = S[2 + i % 2]
                    root_inverse(n, r)
                    dve.scalar_tensor_tensor(out=t, in0=t, scalar=gain, in1=r[:, 0:n], op0=ALU.mult, op1=ALU.mult)\
                        .then_inc(normed, 1)
                at_["normed"] += len(tiles)
                dve.wait_ge(normed, at_["normed"])

            def attention(kind):
                a = att(kind)
                us = units(a)
                p_slots = P_SLOTS[kind]
                n0, e0 = at_["turn"], at_["exp"]
                i = 0

                def logits(u):
                    nonlocal i
                    h, q = us[u]
                    w = P * (a["k1"](q) - a["k0"](q))
                    if q == 0 and kind == "fox":
                        b, n = work()
                        dve.tensor_copy(ck[:, h % 2, :], bank[4 + b][:, :]).then_inc(work_free[b], 1)
                        dve.wait_ge(work_free[b], n)
                    if q == 0 and kind == "swa":
                        step(dve.scalar_tensor_tensor(out=swa_bias[:, h % 2, :], in0=swa_nd, scalar=2.0 ** -(h + 1),
                                                      in1=swa_mask, op0=ALU.mult, op1=ALU.add))
                    for p in range(a["parts"]):
                        places = len(L_SLOTS[kind])
                        L = L_SLOTS[kind][i % places][:, 0:w]
                        top = small[:, 24 + i % places:25 + i % places]
                        b, n = work()
                        s = bank[4 + b][:, 0:w]
                        if i >= places:
                            dve.wait_ge(exp_ready, e0 + i + 1 - places)
                        if kind == "diff":
                            ins = dve.scalar_tensor_tensor(out=L, in0=dist[:, 384 - P * q:384 - P * q + T],
                                                           scalar=-(2.0 ** -(h + 1)), in1=s, op0=ALU.mult, op1=ALU.add)
                        elif kind == "fox":
                            ins = dve.scalar_tensor_tensor(out=L, in0=s, scalar=cq[:, q, h:h + 1],
                                                           in1=ck[:, h % 2, 0:w], op0=ALU.add, op1=ALU.subtract)
                        elif kind == "swa":
                            ins = dve.tensor_tensor(L, s, swa_bias[:, h % 2, 256 - w:256], ALU.add)
                        else:
                            ins = dve.tensor_copy(L, s)
                        ins.then_inc(work_free[b], 1)
                        dve.wait_ge(work_free[b], n)
                        if kind == "fox":
                            step(dve.tensor_tensor(L[:, w - P:w], L[:, w - P:w], causal, ALU.add))
                        if kind == "swa":
                            step(dve.tensor_reduce(small[:, 26 + i % 2:27 + i % 2], L, AX, ALU.max))
                            dve.tensor_scalar(top, small[:, 26 + i % 2:27 + i % 2], c_("sinks", h), -1.0, ALU.max, ALU.mult)\
                                .then_inc(top_ready, 1)
                        else:
                            dve.tensor_reduce(top, L, AX, ALU.max, negate=True).then_inc(top_ready, 1)
                        i += 1

                def normalise(u):
                    h, q = us[u]
                    w = P * (a["k1"](q) - a["k0"](q))
                    parts = a["parts"]
                    j = parts * u
                    dve.wait_ge(exp_ready, e0 + j + parts)
                    if u >= 2:
                        n = n0 + u - 2
                        dve.wait_ge(turn_ready[n % 2], n // 2 + 1)
                    sums = small[:, 28 + j % 4:28 + j % 4 + parts]
                    inv = small[:, 36 + 2 * (u % 2):36 + 2 * (u % 2) + parts]
                    if kind == "swa":
                        step(dve.tensor_tensor(sums, sums, small[:, 32 + j % 4:33 + j % 4], ALU.add))
                    step(dve.reciprocal(inv, sums))
                    p0 = p_slots[j % len(p_slots)]
                    if kind == "diff":
                        p1 = p_slots[(j + 1) % len(p_slots)]
                        step(dve.tensor_scalar(p1, p1, inv[:, 1:2], small[:, 6:7], ALU.mult, ALU.mult))
                        dve.scalar_tensor_tensor(out=S[4 + u % 2], in0=p0, scalar=inv[:, 0:1], in1=p1,
                                                 op0=ALU.mult, op1=ALU.add).then_inc(p_ready, 1)
                    else:
                        dve.tensor_scalar(S[4 + u % 2][:, 0:w], p0[:, 0:w], inv, None, ALU.mult).then_inc(p_ready, 1)

                for u in range(len(us) + 1):
                    if u < len(us):
                        logits(u)
                    if u >= 1:
                        normalise(u - 1)
                at_["turn"] += len(us)
                at_["exp"] += len(us) * a["parts"]
                skip(a["heads"] if kind == "diff" else a["heads"] + KD)

            step(dve.memset(small[:, :], 0.0))
            dve.memset(small[:, 0:1], EPS)
            dve.memset(small[:, 1:2], 1.0)

            def ada_product(s):
                if 2 <= s < 6:
                    dve.wait_ge(ada_loaded[s - 2], 16)
                else:
                    dve.wait_ge(slab_loaded[s % 2], 16 if s < 2 else 32)
                w = ada_rows(ada_place(s))
                dve.tensor_tensor(w, w, c_rows, ALU.mult).then_inc(ada_times_c, 1)

            dve.wait_ge(c_ready, 1)
            for s in range(2):
                ada_product(s)
            take(const_loaded, 16 * 3)
            lam = c_("lambda", 0, 128)
            for i in range(2):
                step(dve.tensor_tensor(S[5][:, 32 * i:32 * i + 32], lam[:, 64 * i:64 * i + 32],
                                       lam[:, 64 * i + 32:64 * i + 64], ALU.mult))
            dve.tensor_reduce(small[:, 2:4], S[5][:, 0:64].rearrange("p (i n) -> p i n", i=2), AX, ALU.add)\
                .then_inc(small_ready, 1)
            dve.tensor_scalar(small[:, 8:12], c_("g_subln", 0, 4), 1.0 - LAMBDA_INIT, None, ALU.mult)
            dve.tensor_scalar(small[:, 16:17], c_("g_fox_q"), HD ** -0.5, None, ALU.mult)
            dve.tensor_scalar(small[:, 17:18], c_("g_swa_q"), HD ** -0.5, None, ALU.mult)
            dve.tensor_scalar(small[:, 18:19], c_("g_mem_q"), P ** -0.5, None, ALU.mult)
            take(small_done, 2)
            step(dve.tensor_tensor(small[:, 7:8], small[:, 5:6], small[:, 4:5], ALU.subtract))
            dve.tensor_scalar(small[:, 6:7], small[:, 7:8], -LAMBDA_INIT, None, ALU.add)
            dve.tensor_tensor(wf_lo[:, :, :], c_("w_forget", 0, 64).rearrange("p (k h) -> p k h", k=KD),
                              wf_hi[:, :, :].bitcast(F32), ALU.subtract)

            def gain(i, g):
                a = 8 + 24 * i
                return dve.scalar_tensor_tensor(out=gs[:, i, :], in0=mod[:, a:a + 8], scalar=1.0, in1=c_(g, 0, 8),
                                                op0=ALU.add, op1=ALU.mult)

            for k in range(KD):
                add_squares(k)
            for s in range(2, ADA_FIRST):
                ada_product(s)

            def first_modulation():
                take(ada_used, ADA_FIRST)
                n = 2 * ADA_FIRST
                step(dve.tensor_tensor(mod[:, 0:n], mod[:, 0:n], c_("b_ada", 0, n), ALU.add))
                step(gain(0, "g_mix"))

            norm("first", first_modulation)
            stage_end()

            for i in range(2):
                dve.memset(pool_in[:, i, 0:8], 0.0)
                dve.memset(pool_in[:, i, 8 + T:16 + T], 0.0)
                dve.memset(conv_in[:, i, 0:1], 0.0)
                dve.memset(conv_in[:, i, 1 + T:2 + T], 0.0)
            skip(2)
            n = at_["tile"]
            skip(2)
            for i in range(2):
                dve.wait_ge(lin_free[(n + i) % 4], (n + i) // 4 + 1)
                tile(lambda b: dve.tensor_tensor(conv_in[:, i, 1:1 + T], c_gate_t[:, i, :], b[:, :], ALU.mult))
            n = at_["tile"] + 1
            dve.wait_ge(lin_free[n % 4], n // 4 + 1)
            skip(2 + 4 + 4 + 8)
            step(dve.drain())

            for i in range(2):
                w = [c_("conv", 2 * k + i) for k in range(3)]
                y = S[4 + i]
                step(dve.tensor_scalar(y, conv_in[:, i, 0:T], w[0], None, ALU.mult))
                step(dve.scalar_tensor_tensor(out=y, in0=conv_in[:, i, 1:1 + T], scalar=w[1], in1=y,
                                              op0=ALU.mult, op1=ALU.add))
                step(dve.scalar_tensor_tensor(out=y, in0=conv_in[:, i, 2:2 + T], scalar=w[2], in1=y,
                                              op0=ALU.mult, op1=ALU.add))
                dve.tensor_tensor(y, y, b_gate_t[:, i, :], ALU.mult).then_inc(whole_ready, 1)
            split(4, lambda i: Qt[:, i, :], "B", followed=False)
            split(2, lambda i: S[4 + i], "B", first=6, followed=False)
            take(table_loaded, 2 * 16)
            for g in range(2):
                u = pool_in[:, g, :]
                a, b = pool_sum[:, 0, :], pool_sum[:, 1, :]
                step(dve.tensor_tensor(a[:, 1:528], u[:, 0:527], u[:, 1:528], ALU.add))
                step(dve.tensor_tensor(b[:, 2:527], a[:, 1:526], a[:, 3:528], ALU.add))
                if g:
                    step(dve.tensor_tensor(a[:, 4:525], b[:, 2:523], b[:, 6:527], ALU.add))
                    step(dve.tensor_tensor(b[:, 8:521], a[:, 4:517], a[:, 12:525], ALU.add))
                for r, sums in ((0, a), (1, b)):
                    rows = slice(64 * r, 64 * r + 64)
                    step(dve.tensor_tensor(S[g][rows, :], sums[rows, 8:8 + T], recip_cnt[g][rows, :], ALU.mult))
                    step(dve.tensor_tensor(S[g][rows, :], S[g][rows, :], u[rows, 8:8 + T], ALU.subtract))
            dve.drain().then_inc(diff_ready, 1)
            for g in range(2):
                b, n = work()
                dve.tensor_scalar(S[2 + g], bank[4 + b][:, :], c_("pool_scale", g), None, ALU.mult)\
                    .then_inc(work_free[b], 1)
                dve.wait_ge(work_free[b], n)
                dve.drain().then_inc(whole_ready, 1)
            split(2, lambda i: S[2 + i], "B", first=4, followed=False)
            split(4, lambda i: Kt[:, i, :], "A", followed=False)
            stage_end()
            attention("diff")
            take(ada_used, N_ADA - ADA_FIRST)
            n = 2 * ADA_FIRST
            step(dve.tensor_tensor(mod[:, n:48], mod[:, n:48], c_("b_ada", n, 48 - n), ALU.add))
            gain(1, "g_ffn")
            stage_end()
            head_norm("subln")
            for i in range(4):
                dve.drain().then_inc(whole_ready, 1)
            split(4, lambda i: Ot[:, i, :], "B")
            stage_end()

            def residual(gate=None, squares=True):
                for m in range(KD + 1):
                    if squares and m:
                        add_squares(m - 1)
                    if m == KD:
                        break
                    if gate is None:
                        tile(lambda b: dve.tensor_tensor(X[:, m, :], b[:, :], X[:, m, :], ALU.add))
                    else:
                        tile(lambda b: dve.scalar_tensor_tensor(out=X[:, m, :], in0=b[:, :],
                                                                scalar=mod[:, gate + m:gate + m + 1],
                                                                in1=X[:, m, :], op0=ALU.mult, op1=ALU.add))

            residual(16)
            stage_end()
            norm("ffn")
            stage_end()
            for g in FFN_GROUPS:
                for i in range(g):
                    n = at_["tile"]
                    dve.wait_ge(lin_free[n % 4], n // 4 + 1)
                    skip(1)
                    tile(lambda b: dve.tensor_tensor(S[2 + i % 2], S[i % 2], b[:, :], ALU.mult))
                    dve.wait_ge(lin_free[(n + 1) % 4], (n + 1) // 4 + 1)
                    dve.drain().then_inc(whole_ready, 1)
                    rest(i, S[2 + i % 2], "B", 0)
                stage_end()
                residual(40, squares=g == FFN_GROUPS[-1])
                stage_end()
            norm("final")
            stage_end()
            norm("second")
            stage_end()
            for br in BRANCHES:
                skip(4)
                if br == "fox":
                    head_norm("fox_q", "fox_k")
                    skip(4 + 8)
                    x = S[3][:, 0:32]
                    for q in range(QT):
                        tile(lambda b: dve.tensor_tensor(x[:, HEADS * q:HEADS * q + HEADS], b[:, 0:HEADS],
                                                         c_("b_forget", 0, 8), ALU.add))
                    dve.wait_ge(lin_free[(at_["tile"] - 1) % 4], (at_["tile"] - 1) // 4 + 1)
                    dve.scalar_tensor_tensor(out=S[0][:, 0:32], in0=x, scalar=-1.0, in1=x,
                                             op0=ALU.mult, op1=ALU.min).then_inc(small_ready, 1)
                    take(small_done)
                    dve.scalar_tensor_tensor(out=log_f.rearrange("p q h -> p (q h)"), in0=x, scalar=0.0,
                                             in1=S[2][:, 0:32], op0=ALU.min, op1=ALU.subtract)
                    stage_end()
                    b, n = work()
                    dve.tensor_copy(cq.rearrange("p q h -> p (q h)"), bank[4 + b][:, 0:32])\
                        .then_inc(work_free[b], 1)
                elif br == "swa":
                    skip(1 + QT)
                    head_norm("swa_q", "swa_k")
                else:
                    for k in range(KD):
                        add_squares(k, MEM)
                    norm("mem")
                    stage_end()
                    skip(4 + 4)
                    head_norm("mem_q", "mem_k")
                stage_end()
                attention(br)
                stage_end()
                o = mem_o if br == "mem" else Ot
                for i in range(4):
                    dve.drain().then_inc(whole_ready, 1)
                split(4, lambda i: o[:, i, :], "B")
                stage_end()
                for i in range(KD):
                    take(gate_ready)
                    n = at_["tile"]
                    if br == "fox":
                        tile(lambda b: dve.tensor_tensor(merged[:, i, :], gate_t[i], b[:, :], ALU.mult))
                    else:
                        tile(lambda b: dve.tensor_tensor(S[2], gate_t[i], b[:, :], ALU.mult))
                        dve.wait_ge(lin_free[n % 4], n // 4 + 1)
                        step(dve.tensor_tensor(merged[:, i, :], merged[:, i, :], S[2], ALU.add))
                stage_end()
            for i in range(KD):
                dve.drain().then_inc(whole_ready, 1)
            split(8, lambda k: merged[:, k, :], "B")
            stage_end()
            residual()
            stage_end()
            norm("peer")
            dve.drain().then_inc(dve_stage, 1)
            take(act_stage, 2)

            def top16(sources, values, indices, rests, free=None):
                for s, v in zip(sources, values):
                    ins = dve.max(v[:, 0:8], s)
                step(ins)
                for s, v, i in zip(sources, values, indices):
                    dve.max_index(i[:, 0:8], v[:, 0:8], s)
                for s, v, r in zip(sources, values, rests):
                    ins = dve.match_replace(r, v[:, 0:8], s, -3.0e38)
                if free:
                    ins.then_inc(free[0], 1)
                    dve.wait_ge(*free)
                else:
                    step(ins)
                for v, r in zip(values, rests):
                    ins = dve.max(v[:, 8:16], r)
                step(ins)
                for v, i, r in zip(values, indices, rests):
                    ins = dve.max_index(i[:, 8:16], v[:, 8:16], r)

            top_iu, sum_iu = top_i.bitcast(U32), sum_i.bitcast(U32)
            for h in range(HEADS):
                skip(2)
                for q in range(QT):
                    b, n = work()
                    c = cand[:, q % 2, :]
                    top16([bank[4 + b][:, KEYS * i:KEYS * i + KEYS] for i in range(2)],
                          [top_v[:, q, h, TOPK * i:TOPK * i + TOPK] for i in range(2)],
                          [top_iu[:, q, h, TOPK * i:TOPK * i + TOPK] for i in range(2)],
                          [rest_a[:, i, :] for i in range(2)], free=(work_free[b], n))
                    v = top_v[:, q, h, :]
                    step(dve.tensor_tensor(c.rearrange("p (i j) -> p i j", i=TOPK),
                                           v[:, 0:TOPK].unsqueeze(2).to_broadcast([P, TOPK, TOPK]),
                                           v[:, TOPK:2 * TOPK].unsqueeze(1).to_broadcast([P, TOPK, TOPK]),
                                           ALU.add))
                    top16([c], [sum_v[:, q, h, :]], [sum_iu[:, q, h, :]], [cand_rest])
            d = eq[:, 0:512].rearrange("p (g s) -> p g s", s=TOPK)
            ex = eq[:, 512:1024].rearrange("p (g s) -> p g s", s=TOPK)
            sv = sum_v.rearrange("p q h s -> p (q h) s")
            dve.tensor_tensor(d, sv, sv[:, :, 0:1].to_broadcast([P, QT * HEADS, TOPK]), ALU.subtract)\
                .then_inc(small_ready, 1)
            take(small_done)
            gsum = eq[:, 1024:1024 + QT * HEADS]
            step(dve.tensor_reduce(gsum, ex, AX, ALU.add))
            step(dve.reciprocal(gsum, gsum))
            step(dve.tensor_tensor(picks[:, :, 2, :].rearrange("p q (h s) -> p q h s", h=HEADS),
                                   ex.rearrange("p (q h) s -> p q h s", q=QT),
                                   gsum.rearrange("p (q h) -> p q h", q=QT).unsqueeze(3)
                                   .to_broadcast([P, QT, HEADS, TOPK]), ALU.mult))
            iwu = iw.bitcast(U32)
            eq3 = eq.rearrange("p (s j) -> p s j", j=TOPK)
            eq4 = eq.rearrange("p (h s j) -> p h s j", h=HEADS, j=TOPK)
            for q in range(QT):
                si = sum_iu[:, q, :, :].rearrange("p h s -> p (h s)")
                dve.tensor_scalar(iwu[:, 0, :], si, 4, None, ALU.logical_shift_right)
                dve.tensor_scalar(iwu[:, 1, :], si, 15, None, ALU.bitwise_and)
                step(dve.tensor_copy(top_f, top_iu[:, q, :, :]))
                dve.tensor_copy(sel_hi, iwu[:, 0, :])
                step(dve.tensor_copy(sel_lo, iwu[:, 1, :]))
                for i, sel in enumerate((sel_hi, sel_lo)):
                    step(dve.tensor_tensor(eq3, sel.unsqueeze(2).to_broadcast([P, P, TOPK]),
                                           iota16.unsqueeze(1).to_broadcast([P, P, TOPK]), ALU.is_equal))
                    step(dve.tensor_tensor(eq4, eq4, top_f[:, :, TOPK * i:TOPK * i + TOPK].unsqueeze(2)
                                           .to_broadcast([P, HEADS, TOPK, TOPK]), ALU.mult))
                    step(dve.tensor_reduce(picks[:, q, i, :], eq3, AX, ALU.add))
            stage_end()
            stage_end()
            with dve.Fori(0, T - 3, 4) as t:
                for j in range(4):
                    dve.wait_ge(hot_used, t + (j + 1))
                    dve.tensor_scalar(hot[:, j, 0, :], iota, picks_t[:, 0, bass.ds(t + j, 1)], None, ALU.is_equal)
                    dve.tensor_scalar(hot[:, j, 1, :], iota, picks_t[:, 1, bass.ds(t + j, 1)],
                                      picks_t[:, 2, bass.ds(t + j, 1)], ALU.is_equal, ALU.mult)\
                        .then_inc(hot_ready, 1)

            def gated(s, j):
                dve.wait_ge(pair_loaded[j], s * 16 + 32)
                dve.tensor_tensor(prod[:, j, :].rearrange("p (i q t) -> p i q t", i=2, q=GB),
                                  gelu_in[:, j, :].rearrange("p (i q t) -> p i q t", i=2, q=GB),
                                  g_in[:, j, :].rearrange("p (q i t) -> p i q t", i=2, q=GB), ALU.mult)\
                    .then_inc(act_ready, 1)
                dve.wait_ge(act_hi_ready, s + (j + 1))
                dve.tensor_tensor(B_lo[:, 4 + 2 * j:6 + 2 * j, :], prod[:, j, :].rearrange("p (i t) -> p i t", i=2),
                                  B_hi[:, 4 + 2 * j:6 + 2 * j, :].bitcast(F32), ALU.subtract)\
                    .then_inc(act_lo_ready, 1)

            for j in range(2):
                gated(0, j)
            with dve.Fori(2, PAIRS - 1, 2) as s:
                for j in range(2):
                    gated(s, j)
            dve.wait_ge(slab_used, N_MID + 2 * PAIRS)
            for m in range(KD):
                dve.tensor_tensor(X[:, m, :], bank[m][:, :], X[:, m, :], ALU.add)
            dve.drain().then_inc(x_done, 1)


def _slab(w):
    import numpy as np
    k = w.shape[0] // P
    a = w.reshape(k, P, w.shape[1]).transpose(1, 0, 2).reshape(P, -1)
    out = np.zeros((P, SLAB), np.float32)
    out[:, :a.shape[1]] = a
    return out


def _stream(i):
    import numpy as np
    slabs = []

    def columns(w, first=0, last=None):
        for a in range(first, w.shape[1] if last is None else last, 256):
            slabs.append(_slab(w[:, a:a + 256]))

    ada = i["w_ada"][0].T.reshape(N_ADA, 2, P, D).transpose(0, 2, 1, 3).reshape(N_ADA, P, SLAB)
    slabs.extend(ada[:ADA_FIRST])
    w = i["w_in"][0]
    columns(w, 1536, 1792)
    columns(w, 2048, 2304)
    columns(w, 2304, 2560)
    columns(w, 1792, 2048)
    columns(w, 0, 1536)
    assert len(slabs) == ADA_FIRST + ADA_LATER_AT
    slabs.extend(ada[ADA_FIRST:])
    columns(i["w_out"][0])
    wg, wd = i["w_gate_up"][0], i["w_down"][0]
    f = 0
    for g in FFN_GROUPS:
        for j in range(f, f + g):
            slabs.append(_slab(np.concatenate([wg[:, P * j:P * j + P], wg[:, DFF + P * j:DFF + P * j + P]], 1)))
        columns(wd[P * f:P * (f + g)])
        f += g
    w = i["w_in_2"][0]
    gates_at = 2824
    pairs = [h for n in range(4) for h in (n, n + 4)]
    w_o = [i["w_fox_o_2"][0],
           i["w_swa_o_2"][0].reshape(HEADS, HD, D)[pairs].reshape(HEADS * HD, D), i["w_mem_o_2"][0]]
    for n, br in enumerate(("fox", "swa", "mem")):
        if br == "fox":
            columns(w, 0, 1536)
        elif br == "swa":
            columns(w[:, 1544:2056].reshape(D, HEADS, HD)[:, pairs].reshape(D, HEADS * HD))
            columns(w, 2056, 2312)
        else:
            columns(w, 2312, 2824)
            columns(i["w_mem_kv_2"][0])
        columns(w, gates_at + D * n, gates_at + D * (n + 1))
        for m in range(2):
            slabs.append(_slab(w_o[n][:, 512 * m:512 * m + 512]))
    columns(i["w_out_2"][0])
    u = i["peer_u_2"][0].reshape(KEYS, PAIRS, 2, KD, P)
    u = np.ascontiguousarray(u.transpose(1, 4, 2, 3, 0)).reshape(PAIRS, P, SLAB)
    v = i["peer_v_2"][0].reshape(KEYS, PAIRS, SLAB).transpose(1, 0, 2)
    for h in range(HEADS):
        slabs.append(_slab(i["w_peer_q_2"][0][:, 256 * h:256 * h + 256]))
        slabs.append(u[h])
    assert len(slabs) == N_ADA + N_MID + HEADS, len(slabs)
    return np.concatenate([np.stack(slabs), u[HEADS:], v])


def _columns(i):
    import numpy as np

    def tiles(a):
        return a.reshape(-1, P).T

    def rows(a):
        return np.broadcast_to(a.reshape(1, -1), (P, a.size))

    def twice(a):
        return np.concatenate([a.reshape(-1)] * 2).reshape(P, 1)

    parts = {
        "b_ada": tiles(i["b_ada"]), "g_mix": tiles(i["g_mix"]), "g_subln": tiles(i["g_subln"]),
        "pool_scale": tiles(i["pool_scale"]), "conv": tiles(i["conv_w"]), "g_ffn": tiles(i["g_ffn"]),
        "g_final": tiles(i["g_final"]), "g_norm1": tiles(i["norm1_g_2"]), "b_gate": tiles(i["b_gate_2"]),
        "g_fox_q": twice(i["fox_q_g_2"]), "g_fox_k": twice(i["fox_k_g_2"]), "g_swa_q": twice(i["swa_q_g_2"]),
        "g_swa_k": twice(i["swa_k_g_2"]), "g_mem": tiles(i["mem_norm_g_2"]), "g_mem_q": tiles(i["mem_q_g_2"]),
        "g_mem_k": tiles(i["mem_k_g_2"]), "g_norm2": tiles(i["norm2_g_2"]), "b_forget": rows(i["b_forget_2"]),
        "sinks": rows(i["swa_sinks_2"]),
        "lambda": rows(np.concatenate([i[n].reshape(-1) for n in ("lambda_q1", "lambda_k1", "lambda_q2", "lambda_k2")])),
        "w_forget": i["w_in_2"][0][:, 1536:1544].reshape(KD, P, HEADS).transpose(1, 0, 2).reshape(P, -1),
        "w_pool": i["w_pool"][0].reshape(2, P, 64).transpose(1, 0, 2).reshape(P, -1),
    }
    return np.ascontiguousarray(np.concatenate([parts[n] for n, _ in COLS] + [rows(i["c"])], 1))


def _tables():
    import numpy as np
    p = np.arange(P)[:, None]
    out = {"ident": np.eye(P), "mean_all": np.full((P, P), 1.0 / D), "mean_128": np.full((P, P), 1.0 / P),
           "mean_64": (p // 64 == np.arange(P)[None] // 64) / 64.0,
           "distance": np.abs(p - np.arange(896)[None] + 384),
           "causal": np.where(np.arange(P)[None] <= p, 0.0, NEG_INF), "upto": p <= np.arange(512)[None],
           "iota": np.broadcast_to(np.arange(P)[None], (P, P)), "iota16": np.broadcast_to(np.arange(16)[None], (P, 16))}
    t = np.arange(T)
    counts = []
    for w in (2, 4, 8, 16):
        counts.append(np.clip(t + w - w // 2, 0, T) - np.clip(t - w // 2, 0, T))
    r = np.stack([1.0 / c for c in counts])
    out["pool_recip"] = np.concatenate([np.repeat(r[2 * g:2 * g + 2], 64, axis=0) for g in range(2)], 1)
    d = p + P - np.arange(256)[None]
    ok = (d >= 0) & (d < P)
    out["swa_distance"] = np.where(ok, -d, 0)
    out["swa_mask"] = np.where(ok, 0.0, NEG_INF)
    return np.ascontiguousarray(np.concatenate([out[n].astype(np.float32) for n, _ in TABLES], 1))


def kernel(**inputs):
    import numpy as np
    import concourse.bacc as bacc
    from concourse.bass_utils import run_bass_kernel_spmd

    i = {k: np.asarray(v) for k, v in inputs.items()}
    keys_t = np.stack([i["peer_keys1_2"][0], i["peer_keys2_2"][0]], 1).reshape(16, KEYS, P).transpose(2, 0, 1)\
        .reshape(P, 16 * KEYS)
    arrays = {"x_t": np.ascontiguousarray(i["x"][0].T), "weights": _stream(i), "columns": _columns(i),
              "tables": _tables(), "mem_t_in": np.ascontiguousarray(i["mem_2"][0].T),
              "keys_t": np.ascontiguousarray(keys_t)}
    nc = bacc.Bacc("TRN2", target_bir_lowering=False, num_devices=1)
    args = [nc.dram_tensor(n, a.shape, F32, kind="ExternalInput").ap() for n, a in arrays.items()]
    out = nc.dram_tensor("out_t", (D, T), F32, kind="ExternalOutput").ap()
    build(nc, *args, out)
    r = run_bass_kernel_spmd(nc, [arrays], core_ids=[0])
    return np.ascontiguousarray(r.results[0]["out_t"].T)[None]
```
